# Optimizing a Trainium2 kernel written in Bass

```python
import math
import jax, jax.numpy as jnp
from jax import lax
import numpy as np

D_MODEL = 2048
BATCH = 1
SEQ = 256
DEPTH = 1

N_MIXERS = 3
D_FF = 4 * D_MODEL
D_PLE = 256
NORM_EPS = 1e-6
LN_EPS = 1e-5
NEG = -1e30

NSA_HEADS = 16
NSA_KV_HEADS = 4
NSA_HPG = NSA_HEADS // NSA_KV_HEADS
NSA_HEAD_DIM = D_MODEL // NSA_HEADS
NSA_CMP_LEN = 32
NSA_CMP_STRIDE = 16
NSA_CMP_HIDDEN = NSA_HEAD_DIM
NSA_SEL_LEN = 64
NSA_SEL_TOPK = 16
NSA_SEL_LOCAL = 2
NSA_WINDOW = 512
NSA_Q_BLOCK = 32
NSA_FORCE = 1e9
NSA_IN_WIDTH = NSA_HEADS * NSA_HEAD_DIM + 6 * NSA_KV_HEADS * NSA_HEAD_DIM + 3 * NSA_HEADS

CONV_WIDTH = 31
CONV_INNER = D_MODEL

GLA_HEADS = 4
GLA_DK = D_MODEL // 2 // GLA_HEADS
GLA_DV = D_MODEL // GLA_HEADS
GLA_GATE_RANK = 16
GLA_GATE_NORM = 16.0
GLA_CHUNK = 64
GLA_IN_WIDTH = 2 * GLA_HEADS * GLA_DK + 2 * GLA_HEADS * GLA_DV + GLA_GATE_RANK


def rms_norm(x, gain):
    xf = x.astype(jnp.float32)
    y = xf * lax.rsqrt(jnp.mean(xf * xf, axis=-1, keepdims=True) + NORM_EPS)
    return (y * gain.astype(jnp.float32)).astype(x.dtype)

def layer_norm(x, gain, bias):
    xf = x.astype(jnp.float32)
    mu = jnp.mean(xf, axis=-1, keepdims=True)
    xc = xf - mu
    y = xc * lax.rsqrt(jnp.mean(xc * xc, axis=-1, keepdims=True) + LN_EPS)
    return (y * gain.astype(jnp.float32) + bias.astype(jnp.float32)).astype(x.dtype)

def masked_softmax(s, valid):
    s = jnp.where(valid, s.astype(jnp.float32), NEG)
    return jax.nn.softmax(s, axis=-1) * valid

def nsa_mixer(h, w_in, w_out, pos_k, w1_k, w2_k, pos_v, w1_v, w2_v):
    B, S, _ = h.shape
    G, HPG, Dh = NSA_KV_HEADS, NSA_HPG, NSA_HEAD_DIM
    kvw = G * Dh
    proj = h @ w_in
    cuts = [NSA_HEADS * Dh + i * kvw for i in range(7)]
    q, kc, vc, ks, vs, kw, vw, gates = jnp.split(proj, cuts, axis=-1)
    q = q.reshape(B, S, G, HPG, Dh) * (Dh ** -0.5)
    kc, vc, ks, vs, kw, vw = (a.reshape(B, S, G, Dh) for a in (kc, vc, ks, vs, kw, vw))
    gates = jax.nn.sigmoid(gates.reshape(B, S, G, HPG, 3))

    n_cmp = (S - NSA_CMP_LEN) // NSA_CMP_STRIDE + 1
    cmp_idx = np.arange(n_cmp)[:, None] * NSA_CMP_STRIDE + np.arange(NSA_CMP_LEN)[None, :]
    cmp_end = cmp_idx[:, -1]

    def compress(kv, pos, w1, w2):
        blk = kv[:, cmp_idx] + pos[None, None, :, None, :]
        blk = blk.transpose(0, 1, 3, 2, 4).reshape(B, n_cmp, G, NSA_CMP_LEN * Dh)
        return jax.nn.silu(blk @ w1) @ w2

    k_cmp = compress(kc, pos_k, w1_k, w2_k)
    v_cmp = compress(vc, pos_v, w1_v, w2_v)

    n_sel = S // NSA_SEL_LEN
    n_top = min(NSA_SEL_TOPK, n_sel)
    cmp_start = np.arange(n_cmp) * NSA_CMP_STRIDE
    sel_start = np.arange(n_sel) * NSA_SEL_LEN
    overlap = jnp.asarray(((cmp_start[:, None] <= sel_start[None, :] + NSA_SEL_LEN - 1)
                           & (cmp_start[:, None] + NSA_CMP_LEN - 1 >= sel_start[None, :])).astype(np.float32))
    ks_blk = ks.reshape(B, n_sel, NSA_SEL_LEN, G, Dh).transpose(0, 3, 1, 2, 4)
    vs_blk = vs.reshape(B, n_sel, NSA_SEL_LEN, G, Dh).transpose(0, 3, 1, 2, 4)
    b_ix = jnp.arange(B)[:, None, None, None]
    g_ix = jnp.arange(G)[None, :, None, None]
    blk_ids = jnp.arange(n_sel)
    tok_off = jnp.arange(NSA_SEL_LEN)

    pad = ((0, 0), (NSA_WINDOW, 0), (0, 0), (0, 0))
    kw_pad = jnp.pad(kw, pad)
    vw_pad = jnp.pad(vw, pad)
    QB = NSA_Q_BLOCK

    def block(start):
        t = start + jnp.arange(QB)
        qb = lax.dynamic_slice_in_dim(q, start, QB, axis=1)
        gb = lax.dynamic_slice_in_dim(gates, start, QB, axis=1)

        valid_c = cmp_end[None, :] <= t[:, None]
        p_c = masked_softmax(jnp.einsum('bqghd,bngd->bghqn', qb, k_cmp), valid_c)
        o_c = jnp.einsum('bghqn,bngd->bqghd', p_c.astype(v_cmp.dtype), v_cmp)

        imp = jnp.einsum('bghqn,nm->bgqm', p_c, overlap)
        diff = (t // NSA_SEL_LEN)[:, None] - blk_ids[None, :]
        forced = (blk_ids[None, :] == 0) | ((diff >= 0) & (diff < NSA_SEL_LOCAL))
        imp = jnp.where(forced, NSA_FORCE, imp)
        imp = jnp.where(diff >= 0, imp, -NSA_FORCE)
        _, sel = lax.top_k(imp, n_top)
        k_sel = ks_blk[b_ix, g_ix, sel]
        v_sel = vs_blk[b_ix, g_ix, sel]
        tok = sel[..., None] * NSA_SEL_LEN + tok_off
        valid_s = (tok <= t[None, None, :, None, None]).reshape(B, G, 1, QB, n_top * NSA_SEL_LEN)
        s_s = jnp.einsum('bqghd,bgqnld->bghqnl', qb, k_sel).reshape(B, G, HPG, QB, n_top * NSA_SEL_LEN)
        p_s = masked_softmax(s_s, valid_s)
        o_s = jnp.einsum('bghqk,bgqkd->bqghd', p_s.astype(v_sel.dtype),
                         v_sel.reshape(B, G, QB, n_top * NSA_SEL_LEN, Dh))

        kwb = lax.dynamic_slice_in_dim(kw_pad, start, QB + NSA_WINDOW, axis=1)
        vwb = lax.dynamic_slice_in_dim(vw_pad, start, QB + NSA_WINDOW, axis=1)
        kpos = start - NSA_WINDOW + jnp.arange(QB + NSA_WINDOW)
        valid_w = ((kpos[None, :] <= t[:, None]) & (kpos[None, :] > t[:, None] - NSA_WINDOW)
                   & (kpos[None, :] >= 0))
        p_w = masked_softmax(jnp.einsum('bqghd,bkgd->bghqk', qb, kwb), valid_w)
        o_w = jnp.einsum('bghqk,bkgd->bqghd', p_w.astype(vwb.dtype), vwb)

        return gb[..., 0, None] * o_c + gb[..., 1, None] * o_s + gb[..., 2, None] * o_w

    out = lax.map(block, jnp.arange(S // QB) * QB)
    out = out.transpose(1, 0, 2, 3, 4, 5).reshape(B, S, NSA_HEADS * Dh)
    return out @ w_out

def conv_mixer(h, w_in, dw, db, ln_g, ln_b, w_out):
    a, g = jnp.split(h @ w_in, 2, axis=-1)
    u = a * jax.nn.sigmoid(g)
    y = lax.conv_general_dilated(
        u, dw[:, None, :], window_strides=(1,), padding=[(CONV_WIDTH - 1, 0)],
        dimension_numbers=('NWC', 'WIO', 'NWC'), feature_group_count=CONV_INNER) + db
    y = jax.nn.silu(layer_norm(y, ln_g, ln_b))
    return y @ w_out

def gla_mixer(h, w_in, w_gate_up, b_gate, norm_g, w_out):
    B, S, _ = h.shape
    H, dk, dv, C = GLA_HEADS, GLA_DK, GLA_DV, GLA_CHUNK
    nC = S // C
    cuts = [H * dk, 2 * H * dk, 2 * H * dk + H * dv, 2 * H * dk + 2 * H * dv]
    q, k, v, r, gz = jnp.split(h @ w_in, cuts, axis=-1)
    glog = jax.nn.log_sigmoid((gz @ w_gate_up + b_gate).astype(jnp.float32)) / GLA_GATE_NORM
    f32 = jnp.float32
    q = q.astype(f32).reshape(B, nC, C, H, dk) * (dk ** -0.5)
    k = k.astype(f32).reshape(B, nC, C, H, dk)
    v = v.astype(f32).reshape(B, nC, C, H, dv)
    bcum = jnp.cumsum(glog.reshape(B, nC, C, H, dk), axis=2)
    blast = bcum[:, :, -1]
    q_dec = q * jnp.exp(bcum)
    k_intra = k * jnp.exp(-bcum)
    k_state = k * jnp.exp(blast[:, :, None] - bcum)
    causal = jnp.asarray(np.tril(np.ones((C, C), dtype=bool)))
    A = jnp.where(causal, jnp.einsum('bncha,bnsha->bnhcs', q_dec, k_intra), 0.0)
    o_intra = jnp.einsum('bnhcs,bnshv->bnchv', A, v)

    def step(state, xs):
        qd, kst, vv, dl = xs
        o = jnp.einsum('bcha,bhav->bchv', qd, state)
        state = state * jnp.exp(dl)[..., None] + jnp.einsum('bcha,bchv->bhav', kst, vv)
        return state, o

    xs = tuple(jnp.moveaxis(a, 1, 0) for a in (q_dec, k_state, v, blast))
    _, o_inter = lax.scan(step, jnp.zeros((B, H, dk, dv), f32), xs)
    o = (o_intra + jnp.moveaxis(o_inter, 0, 1)).reshape(B, S, H, dv)
    o = o * lax.rsqrt(jnp.mean(o * o, axis=-1, keepdims=True) + NORM_EPS) * norm_g.astype(f32)
    o = o.reshape(B, S, H * dv).astype(h.dtype) * jax.nn.silu(r)
    return o @ w_out

def first_inputs(seed: int = 0) -> dict:
    key = jax.random.key(seed)
    keys = iter(jax.random.split(key, 64))

    def nrm(shape, scale):
        return jax.random.normal(next(keys), shape, jnp.float32) * scale

    def gain(shape):
        return 1.0 + nrm(shape, 0.02)

    n_nsa = len(range(0, DEPTH, N_MIXERS))
    n_conv = len(range(1, DEPTH, N_MIXERS))
    n_gla = len(range(2, DEPTH, N_MIXERS))
    D, Dh, L = D_MODEL, NSA_HEAD_DIM, NSA_CMP_LEN
    return {
        "x": nrm((BATCH, SEQ, D), 1.0),
        "p": nrm((DEPTH, BATCH, SEQ, D_PLE), 1.0),
        "norm_mix": gain((DEPTH, D)),
        "norm_ffn": gain((DEPTH, D)),
        "norm_ple": gain((DEPTH, D)),
        "norm_final": gain((D,)),
        "ffn_w1": nrm((DEPTH, D, D_FF), D ** -0.5),
        "ffn_w2": nrm((DEPTH, D_FF, D), D_FF ** -0.5),
        "ple_w_proj": nrm((DEPTH, D_PLE, D), D_PLE ** -0.5),
        "ple_w_gate": nrm((DEPTH, D, D), D ** -0.5),
        "nsa_w_in": nrm((n_nsa, D, NSA_IN_WIDTH), D ** -0.5),
        "nsa_w_out": nrm((n_nsa, NSA_HEADS * Dh, D), (NSA_HEADS * Dh) ** -0.5),
        "nsa_cmp_pos_k": nrm((n_nsa, L, Dh), 0.02),
        "nsa_cmp_w1_k": nrm((n_nsa, L * Dh, NSA_CMP_HIDDEN), (L * Dh) ** -0.5),
        "nsa_cmp_w2_k": nrm((n_nsa, NSA_CMP_HIDDEN, Dh), NSA_CMP_HIDDEN ** -0.5),
        "nsa_cmp_pos_v": nrm((n_nsa, L, Dh), 0.02),
        "nsa_cmp_w1_v": nrm((n_nsa, L * Dh, NSA_CMP_HIDDEN), (L * Dh) ** -0.5),
        "nsa_cmp_w2_v": nrm((n_nsa, NSA_CMP_HIDDEN, Dh), NSA_CMP_HIDDEN ** -0.5),
        "conv_w_in": nrm((n_conv, D, 2 * CONV_INNER), D ** -0.5),
        "conv_dw": nrm((n_conv, CONV_WIDTH, CONV_INNER), CONV_WIDTH ** -0.5),
        "conv_db": nrm((n_conv, CONV_INNER), 0.01),
        "conv_ln_g": gain((n_conv, CONV_INNER)),
        "conv_ln_b": nrm((n_conv, CONV_INNER), 0.01),
        "conv_w_out": nrm((n_conv, CONV_INNER, D), CONV_INNER ** -0.5),
        "gla_w_in": nrm((n_gla, D, GLA_IN_WIDTH), D ** -0.5),
        "gla_w_gate_up": nrm((n_gla, GLA_GATE_RANK, GLA_HEADS * GLA_DK), GLA_GATE_RANK ** -0.5),
        "gla_b_gate": nrm((n_gla, GLA_HEADS * GLA_DK), 0.01),
        "gla_norm_g": gain((n_gla, GLA_DV)),
        "gla_w_out": nrm((n_gla, GLA_HEADS * GLA_DV, D), (GLA_HEADS * GLA_DV) ** -0.5),
    }

def first_block(x, p, norm_mix, norm_ffn, norm_ple, norm_final, ffn_w1, ffn_w2,
              ple_w_proj, ple_w_gate, nsa_w_in, nsa_w_out, nsa_cmp_pos_k, nsa_cmp_w1_k,
              nsa_cmp_w2_k, nsa_cmp_pos_v, nsa_cmp_w1_v, nsa_cmp_w2_v, conv_w_in, conv_dw,
              conv_db, conv_ln_g, conv_ln_b, conv_w_out, gla_w_in, gla_w_gate_up,
              gla_b_gate, gla_norm_g, gla_w_out):
    h = x
    for i in range(DEPTH):
        m, j = i % N_MIXERS, i // N_MIXERS
        hn = rms_norm(h, norm_mix[i])
        if m == 0:
            y = nsa_mixer(hn, nsa_w_in[j], nsa_w_out[j], nsa_cmp_pos_k[j], nsa_cmp_w1_k[j],
                          nsa_cmp_w2_k[j], nsa_cmp_pos_v[j], nsa_cmp_w1_v[j], nsa_cmp_w2_v[j])
        elif m == 1:
            y = conv_mixer(hn, conv_w_in[j], conv_dw[j], conv_db[j], conv_ln_g[j],
                           conv_ln_b[j], conv_w_out[j])
        else:
            y = gla_mixer(hn, gla_w_in[j], gla_w_gate_up[j], gla_b_gate[j], gla_norm_g[j],
                          gla_w_out[j])
        h = h + y
        hn = rms_norm(h, norm_ffn[i])
        h = h + jnp.square(jax.nn.relu(hn @ ffn_w1[i])) @ ffn_w2[i]
        gate = jax.nn.sigmoid(rms_norm(h, norm_ple[i]) @ ple_w_gate[i])
        h = h + (p[i] @ ple_w_proj[i]) * gate
    return rms_norm(h, norm_final)


N_MIXERS_2 = 4
HEAD_DIM = 64
N_HEADS = D_MODEL // HEAD_DIM
N_KV_HEADS = N_HEADS // 4
GQA_GROUP = N_HEADS // N_KV_HEADS
WINDOW = 128
Q_BLOCK = 128
DIFF_HEADS = D_MODEL // (2 * HEAD_DIM)
DIFF_V_DIM = 2 * HEAD_DIM
HGRN_HEAD_DIM = 128
HGRN_HEADS = D_MODEL // HGRN_HEAD_DIM
HGRN_CHUNK = 64
IDX_HEADS = 16
IDX_DIM = 64
TOPK_MAX = 256
D_FF_2 = 5632
CONV_WIDTH_2 = 3
NUM_BUCKETS = 32
MAX_DISTANCE = 128
RMS_EPS = 1e-6
N_SWA = len(range(0, DEPTH, N_MIXERS_2))
N_DIFF = len(range(1, DEPTH, N_MIXERS_2))
N_HGRN = len(range(2, DEPTH, N_MIXERS_2))
N_DSA = len(range(3, DEPTH, N_MIXERS_2))
SWA_SPLITS = (N_HEADS * HEAD_DIM, N_KV_HEADS * HEAD_DIM, N_KV_HEADS * HEAD_DIM)
SWA_IN = sum(SWA_SPLITS)
DIFF_SPLITS = (DIFF_HEADS * 2 * HEAD_DIM, DIFF_HEADS * 2 * HEAD_DIM, DIFF_HEADS * DIFF_V_DIM)
DIFF_IN = sum(DIFF_SPLITS)
HGRN_IN = 4 * HGRN_HEADS * HGRN_HEAD_DIM
DSA_SPLITS = (N_HEADS * HEAD_DIM, N_KV_HEADS * HEAD_DIM, N_KV_HEADS * HEAD_DIM,
              IDX_HEADS * IDX_DIM, IDX_DIM, IDX_HEADS)
DSA_IN = sum(DSA_SPLITS)


def split_cols(z, sizes):
    return jnp.split(z, [int(c) for c in np.cumsum(sizes)[:-1]], axis=-1)

def rms_norm_2(x, g):
    xf = x.astype(jnp.float32)
    y = xf * lax.rsqrt(jnp.mean(xf * xf, axis=-1, keepdims=True) + RMS_EPS)
    return (y * g.astype(jnp.float32)).astype(x.dtype)

def rel_position_bias(dist, table):
    n = jnp.maximum(dist, 0)
    max_exact = NUM_BUCKETS // 2
    log_ratio = jnp.log(jnp.maximum(n, 1).astype(jnp.float32) / max_exact) / math.log(MAX_DISTANCE / max_exact)
    large = jnp.minimum(max_exact + (log_ratio * (NUM_BUCKETS - max_exact)).astype(jnp.int32), NUM_BUCKETS - 1)
    bucket = jnp.where(n < max_exact, n, large)
    return table.astype(jnp.float32)[bucket]

def swa_sink_attention(h, w_in, w_out, sinks, bias_table):
    B, S, _ = h.shape
    nb = S // Q_BLOCK
    q, k, v = split_cols(h @ w_in, SWA_SPLITS)
    q = q.reshape(B, nb, Q_BLOCK, N_KV_HEADS, GQA_GROUP, HEAD_DIM)
    pad = ((0, 0), (Q_BLOCK, 0), (0, 0))
    kp = jnp.pad(k, pad).reshape(B, nb + 1, Q_BLOCK, N_KV_HEADS, HEAD_DIM)
    vp = jnp.pad(v, pad).reshape(B, nb + 1, Q_BLOCK, N_KV_HEADS, HEAD_DIM)
    kb = jnp.concatenate([kp[:, :-1], kp[:, 1:]], axis=2)
    vb = jnp.concatenate([vp[:, :-1], vp[:, 1:]], axis=2)
    qi = jnp.arange(Q_BLOCK)
    kj = jnp.arange(2 * Q_BLOCK) - Q_BLOCK
    dist = qi[:, None] - kj[None, :]
    in_band = (dist >= 0) & (dist < WINDOW)
    key_exists = (jnp.arange(nb)[:, None] > 0) | (kj[None, :] >= 0)
    mask = in_band[None] & key_exists[:, None, :]
    bias = rel_position_bias(dist, bias_table).transpose(2, 0, 1).reshape(
        N_KV_HEADS, GQA_GROUP, Q_BLOCK, 2 * Q_BLOCK)
    s = jnp.einsum('bnqhgd,bnshd->bnhgqs', q, kb).astype(jnp.float32) * HEAD_DIM ** -0.5 + bias
    s = jnp.where(mask[None, :, None, None], s, -jnp.inf)
    sink = jnp.broadcast_to(sinks.astype(jnp.float32).reshape(N_KV_HEADS, GQA_GROUP, 1, 1),
                            s.shape[:-1] + (1,))
    p = jax.nn.softmax(jnp.concatenate([s, sink], axis=-1), axis=-1)[..., :-1]
    o = jnp.einsum('bnhgqs,bnshd->bnqhgd', p.astype(vb.dtype), vb)
    return o.reshape(B, S, N_HEADS * HEAD_DIM) @ w_out

def diff_attention(h, w_in, w_out, lambdas, subln_g, bias_table, layer_idx):
    B, S, _ = h.shape
    nb = S // Q_BLOCK
    q, k, v = split_cols(h @ w_in, DIFF_SPLITS)
    q = q.reshape(B, nb, Q_BLOCK, DIFF_HEADS, 2, HEAD_DIM).transpose(1, 0, 2, 3, 4, 5)
    k = k.reshape(B, S, DIFF_HEADS, 2, HEAD_DIM)
    v = v.reshape(B, S, DIFF_HEADS, DIFF_V_DIM)
    lam_init = 0.8 - 0.6 * math.exp(-0.3 * layer_idx)
    lf = lambdas.astype(jnp.float32)
    lam = jnp.exp(jnp.sum(lf[0] * lf[1])) - jnp.exp(jnp.sum(lf[2] * lf[3])) + lam_init
    kpos = jnp.arange(S)

    def block(args):
        qb, start = args
        dist = (start + jnp.arange(Q_BLOCK))[:, None] - kpos[None, :]
        bias = rel_position_bias(dist, bias_table).reshape(Q_BLOCK, S, DIFF_HEADS, 2).transpose(2, 3, 0, 1)
        s = jnp.einsum('bqhmd,bshmd->bhmqs', qb, k).astype(jnp.float32) * HEAD_DIM ** -0.5 + bias
        p = jax.nn.softmax(jnp.where(dist >= 0, s, -jnp.inf), axis=-1)
        a = p[:, :, 0] - lam * p[:, :, 1]
        return jnp.einsum('bhqs,bshe->bqhe', a.astype(v.dtype), v)

    o = lax.map(block, (q, jnp.arange(nb) * Q_BLOCK))
    o = o.transpose(1, 0, 2, 3, 4).reshape(B, S, DIFF_HEADS, DIFF_V_DIM)
    o = rms_norm_2(o, subln_g) * (1.0 - lam_init)
    return o.reshape(B, S, DIFF_HEADS * DIFF_V_DIM) @ w_out

def hgrn2_recurrence(h, w_in, w_out, lb, norm_g):
    B, S, _ = h.shape
    nc = S // HGRN_CHUNK
    f32 = jnp.float32
    q, fz, i, g = jnp.split(h @ w_in, 4, axis=-1)

    def chunks(t):
        return t.astype(f32).reshape(B, nc, HGRN_CHUNK, HGRN_HEADS, HGRN_HEAD_DIM).transpose(1, 0, 3, 2, 4)

    lbf = lb.astype(f32)
    log_f = jnp.logaddexp(jnp.log(lbf), jnp.log1p(-lbf) + jax.nn.log_sigmoid(fz.astype(f32)))
    key = -jnp.expm1(log_f)
    qs, ks, vs, gs = chunks(jax.nn.silu(q.astype(f32))), chunks(key), chunks(i), chunks(log_f)
    causal = jnp.tril(jnp.ones((HGRN_CHUNK, HGRN_CHUNK), dtype=bool))

    def step(state, inp):
        qc, kc, vc, gc = inp
        b = jnp.cumsum(gc, axis=2)
        o_inter = jnp.einsum('bhtk,bhkv->bhtv', qc * jnp.exp(b), state)
        rel = jnp.where(causal[:, :, None], b[:, :, :, None, :] - b[:, :, None, :, :], -jnp.inf)
        att = jnp.einsum('bhtsk,bhsk->bhts', qc[:, :, :, None, :] * jnp.exp(rel), kc)
        o_intra = jnp.einsum('bhts,bhsv->bhtv', att, vc)
        b_end = b[:, :, -1:, :]
        state = state * jnp.exp(b_end[:, :, 0, :, None]) + jnp.einsum(
            'bhsk,bhsv->bhkv', kc * jnp.exp(b_end - b), vc)
        return state, o_inter + o_intra

    state0 = jnp.zeros((B, HGRN_HEADS, HGRN_HEAD_DIM, HGRN_HEAD_DIM), f32)
    _, o = lax.scan(step, state0, (qs, ks, vs, gs))
    o = o.transpose(1, 0, 3, 2, 4).reshape(B, S, HGRN_HEADS, HGRN_HEAD_DIM)
    gate = jax.nn.silu(g.astype(f32)).reshape(B, S, HGRN_HEADS, HGRN_HEAD_DIM)
    o = (rms_norm_2(o, norm_g) * gate).astype(h.dtype)
    return o.reshape(B, S, HGRN_HEADS * HGRN_HEAD_DIM) @ w_out

def dsa_sparse_attention(h, w_in, w_out, bias_table):
    B, S, _ = h.shape
    nb = S // Q_BLOCK
    n_sel = min(TOPK_MAX, S // 4)
    f32 = jnp.float32
    q, k, v, qi, ki, wi = split_cols(h @ w_in, DSA_SPLITS)
    q = q.reshape(B, nb, Q_BLOCK, N_KV_HEADS, GQA_GROUP, HEAD_DIM).transpose(1, 0, 2, 3, 4, 5)
    qi = qi.reshape(B, nb, Q_BLOCK, IDX_HEADS, IDX_DIM).transpose(1, 0, 2, 3, 4)
    wi = wi.reshape(B, nb, Q_BLOCK, IDX_HEADS).transpose(1, 0, 2, 3)
    k = k.reshape(B, S, N_KV_HEADS, HEAD_DIM)
    v = v.reshape(B, S, N_KV_HEADS, HEAD_DIM)
    kpos = jnp.arange(S)
    gather = jax.vmap(lambda t, idx: t[idx])

    def block(args):
        qb, qib, wib, start = args
        qpos = start + jnp.arange(Q_BLOCK)
        logits = jnp.einsum('bqhd,bsd->bqhs', qib, ki).astype(f32) * IDX_DIM ** -0.5
        score = jnp.einsum('bqh,bqhs->bqs', wib.astype(f32) * IDX_HEADS ** -0.5, jax.nn.relu(logits))
        score = jnp.where(qpos[:, None] >= kpos[None, :], score, -jnp.inf)
        _, idx = lax.top_k(score, n_sel)
        valid = idx <= qpos[None, :, None]
        kg, vg = gather(k, idx), gather(v, idx)
        s = jnp.einsum('bqhgd,bqkhd->bhgqk', qb, kg).astype(f32) * HEAD_DIM ** -0.5
        bias = rel_position_bias(qpos[None, :, None] - idx, bias_table).transpose(0, 3, 1, 2).reshape(
            B, N_KV_HEADS, GQA_GROUP, Q_BLOCK, n_sel)
        s = jnp.where(valid[:, None, None], s + bias, -jnp.inf)
        p = jax.nn.softmax(s, axis=-1)
        return jnp.einsum('bhgqk,bqkhd->bqhgd', p.astype(vg.dtype), vg)

    o = lax.map(block, (q, qi, wi, jnp.arange(nb) * Q_BLOCK))
    return o.transpose(1, 0, 2, 3, 4, 5).reshape(B, S, N_HEADS * HEAD_DIM) @ w_out

def conv_ffn(h, w_up, conv_w, w_down):
    S = h.shape[1]
    u = h @ w_up
    up = jnp.pad(u, ((0, 0), (CONV_WIDTH_2 - 1, 0), (0, 0)))
    c = conv_w[0] * up[:, 0:S]
    for j in range(1, CONV_WIDTH_2):
        c = c + conv_w[j] * up[:, j:j + S]
    gate, val = jnp.split(c, 2, axis=-1)
    return (jax.nn.silu(gate) * val) @ w_down

def second_inputs(seed: int = 0) -> dict:
    key = jax.random.key(seed)
    ks = jax.random.split(key, 20)
    f32 = jnp.float32

    def dense(k, shape, fan_in):
        return jax.random.normal(k, shape, f32) * fan_in ** -0.5

    return {
        'x': jax.random.normal(ks[0], (BATCH, SEQ, D_MODEL), f32),
        'rel_bias_table': 0.3 * jax.random.normal(ks[1], (NUM_BUCKETS, N_HEADS), f32),
        'hgrn_lb_logits': 0.5 * jax.random.normal(ks[2], (DEPTH, HGRN_HEADS * HGRN_HEAD_DIM), f32),
        'norm_g': 1.0 + 0.02 * jax.random.normal(ks[3], (DEPTH, 4, D_MODEL), f32),
        'ffn_w_up': dense(ks[4], (DEPTH, D_MODEL, 2 * D_FF_2), D_MODEL),
        'ffn_conv': dense(ks[5], (DEPTH, CONV_WIDTH_2, 2 * D_FF_2), CONV_WIDTH_2),
        'ffn_w_down': dense(ks[6], (DEPTH, D_FF_2, D_MODEL), D_FF_2),
        'swa_w_in': dense(ks[7], (N_SWA, D_MODEL, SWA_IN), D_MODEL),
        'swa_w_out': dense(ks[8], (N_SWA, N_HEADS * HEAD_DIM, D_MODEL), N_HEADS * HEAD_DIM),
        'swa_sinks': 0.5 * jax.random.normal(ks[9], (N_SWA, N_HEADS), f32),
        'diff_w_in': dense(ks[10], (N_DIFF, D_MODEL, DIFF_IN), D_MODEL),
        'diff_w_out': dense(ks[11], (N_DIFF, DIFF_HEADS * DIFF_V_DIM, D_MODEL), DIFF_HEADS * DIFF_V_DIM),
        'diff_lambda': 0.1 * jax.random.normal(ks[12], (N_DIFF, 4, HEAD_DIM), f32),
        'diff_subln_g': 1.0 + 0.02 * jax.random.normal(ks[13], (N_DIFF, DIFF_V_DIM), f32),
        'hgrn_w_in': dense(ks[14], (N_HGRN, D_MODEL, HGRN_IN), D_MODEL),
        'hgrn_w_out': dense(ks[15], (N_HGRN, HGRN_HEADS * HGRN_HEAD_DIM, D_MODEL), HGRN_HEADS * HGRN_HEAD_DIM),
        'hgrn_norm_g': 1.0 + 0.02 * jax.random.normal(ks[16], (N_HGRN, HGRN_HEAD_DIM), f32),
        'dsa_w_in': dense(ks[17], (N_DSA, D_MODEL, DSA_IN), D_MODEL),
        'dsa_w_out': dense(ks[18], (N_DSA, N_HEADS * HEAD_DIM, D_MODEL), N_HEADS * HEAD_DIM),
    }

def second_block(x, rel_bias_table, hgrn_lb_logits, norm_g, ffn_w_up, ffn_conv, ffn_w_down,
              swa_w_in, swa_w_out, swa_sinks, diff_w_in, diff_w_out, diff_lambda, diff_subln_g,
              hgrn_w_in, hgrn_w_out, hgrn_norm_g, dsa_w_in, dsa_w_out):
    lb_soft = jax.nn.softmax(hgrn_lb_logits.astype(jnp.float32), axis=0)
    lb_all = jnp.cumsum(lb_soft, axis=0) - lb_soft[0]
    for i in range(DEPTH):
        kind, j = i % N_MIXERS_2, i // N_MIXERS_2
        h = rms_norm_2(x, norm_g[i, 0])
        if kind == 0:
            m = swa_sink_attention(h, swa_w_in[j], swa_w_out[j], swa_sinks[j], rel_bias_table)
        elif kind == 1:
            m = diff_attention(h, diff_w_in[j], diff_w_out[j], diff_lambda[j], diff_subln_g[j],
                               rel_bias_table, i)
        elif kind == 2:
            m = hgrn2_recurrence(h, hgrn_w_in[j], hgrn_w_out[j], lb_all[i], hgrn_norm_g[j])
        else:
            m = dsa_sparse_attention(h, dsa_w_in[j], dsa_w_out[j], rel_bias_table)
        x = x + rms_norm_2(m, norm_g[i, 1])
        h = rms_norm_2(x, norm_g[i, 2])
        x = x + rms_norm_2(conv_ffn(h, ffn_w_up[i], ffn_conv[i], ffn_w_down[i]), norm_g[i, 3])
    return x


def setup_inputs(seed=0):
    out = dict(first_inputs(seed))
    for name, value in second_inputs(seed + 1).items():
        if name != "x":
            out[name + "_2"] = value
    return out


def reference(
    x, p, norm_mix, norm_ffn, norm_ple, norm_final, ffn_w1, ffn_w2, ple_w_proj, ple_w_gate,
    nsa_w_in, nsa_w_out, nsa_cmp_pos_k, nsa_cmp_w1_k, nsa_cmp_w2_k, nsa_cmp_pos_v, nsa_cmp_w1_v,
    nsa_cmp_w2_v, conv_w_in, conv_dw, conv_db, conv_ln_g, conv_ln_b, conv_w_out, gla_w_in,
    gla_w_gate_up, gla_b_gate, gla_norm_g, gla_w_out, rel_bias_table_2, hgrn_lb_logits_2,
    norm_g_2, ffn_w_up_2, ffn_conv_2, ffn_w_down_2, swa_w_in_2, swa_w_out_2, swa_sinks_2,
    diff_w_in_2, diff_w_out_2, diff_lambda_2, diff_subln_g_2, hgrn_w_in_2, hgrn_w_out_2,
    hgrn_norm_g_2, dsa_w_in_2, dsa_w_out_2,
):
    x = first_block(
        x, p, norm_mix, norm_ffn, norm_ple, norm_final, ffn_w1, ffn_w2, ple_w_proj, ple_w_gate,
        nsa_w_in, nsa_w_out, nsa_cmp_pos_k, nsa_cmp_w1_k, nsa_cmp_w2_k, nsa_cmp_pos_v,
        nsa_cmp_w1_v, nsa_cmp_w2_v, conv_w_in, conv_dw, conv_db, conv_ln_g, conv_ln_b,
        conv_w_out, gla_w_in, gla_w_gate_up, gla_b_gate, gla_norm_g, gla_w_out,
    )
    return second_block(
        x, rel_bias_table_2, hgrn_lb_logits_2, norm_g_2, ffn_w_up_2, ffn_conv_2, ffn_w_down_2,
        swa_w_in_2, swa_w_out_2, swa_sinks_2, diff_w_in_2, diff_w_out_2, diff_lambda_2,
        diff_subln_g_2, hgrn_w_in_2, hgrn_w_out_2, hgrn_norm_g_2, dsa_w_in_2, dsa_w_out_2,
    )


_drawn_inputs = setup_inputs


def setup_inputs(seed=0):
    import zlib

    import numpy as np

    out = dict(_drawn_inputs(seed))
    spreads = {}
    factors = {'norm_mix': 6.166,
     'norm_ffn': 9.225,
     'norm_ple': 200.0,
     'nsa_cmp_pos_k': 22.749,
     'nsa_cmp_pos_v': 35.265,
     'swa_sinks_2': 3.333,
     'p': 8.0,
     'ple_w_proj': 8.0,
     'ple_w_gate': 8.0}
    for name, (base, spread) in spreads.items():
        noise = np.random.default_rng([zlib.crc32(name.encode()), seed]).standard_normal(out[name].shape)
        drawn = base * np.exp(spread * noise) if base else spread * noise
        out[name] = __import__('jax').numpy.asarray(drawn.astype(out[name].dtype))
    for name, factor in factors.items():
        out[name] = (out[name] * factor).astype(out[name].dtype)
    return out
```

```python
from contextlib import ExitStack

import numpy as np

P = 128
S = 256
D = 2048
DT = D // P
QT = S // P
EPS = 1e-6
NEG = -1e30

HEADS, KVG, HPG = 16, 4, 4
CL, CS = 32, 16
NCMP = (S - CL) // CS + 1
NPAD = 32
D_FF = 8192
CH = 16
FF_CHUNKS = D_FF // P // CH
D_PLE = 256
SWA_HEADS, SWA_KV, HD = 32, 8, 64
WIN = 128
PAIRS = SWA_KV // 2
D_FF2 = 5632
FF2_T = D_FF2 // P
CHUNKS2 = [16, 16, 12]
NBUCK, MAXD = 32, 128
RB = 384
SLOTS = 4
LEAD = 3
BLK = 8
PW = BLK * P

STAGES = [("kv", 16, 16), ("q", 16, 16), ("v", 4, 16), ("cmp", 2, 32), ("misc", 4, 2), ("wo", 16, 16)]
for _c in range(FF_CHUNKS):
    STAGES += [(f"ff{_c}", CH, 16), (f"fd{_c}", 16, CH)]
STAGES += [("proj", 16, 2), ("gate", 16, 16), ("k2", 4, 16), ("v2", 2, 16), ("q2", 16, 16), ("wo2", 16, 16)]
for _c, _n in enumerate(CHUNKS2):
    STAGES += [(f"up{_c}", 2 * _n, 16), (f"dn{_c}", 16, _n)]

PB, UB, ZB = {}, {}, {}
NORM_BEFORE = {"kv": 1, "wo": 0, "ff0": 1, "gate": 1, "k2": 2, "up0": 2}
NZ = {"v": 0, "v2": 0, "misc": 0}
_p = _u = _z = 0
for _name, _n, _k in STAGES:
    _u += NORM_BEFORE.get(_name, 0)
    PB[_name], UB[_name], ZB[_name] = _p, _u, _z
    _blocks = _n * _k * (2 if _name in ("v", "v2") else 1)
    if _name in ("v", "v2"):
        _blocks = _n // 2 * 4 * 16
    _p += 1 if _name == "misc" else _blocks // BLK
    _u += _n
    _z += NZ.get(_name, _n)
NPIECE = _p
UB["end"] = _u


def columns(widths):
    at, out = 0, {}
    for name, width in widths:
        out[name] = (at, at + width)
        at += width
    return out, at


CO, NCONST = columns([("ident", P), ("mask", 2 * P), ("cmask", QT * CS), ("cvalid", QT * CS)])
SO, NSETUP = columns([("onehot", RB), ("band", RB), ("table", SWA_HEADS)])
PO, NPAR = columns([("g_mix", DT), ("g_ffn", DT), ("g_ple", DT), ("g_fin", DT), ("g0", DT), ("g1", DT), ("g2", DT),
                    ("g3", DT), ("conv", 3 * 2 * FF2_T), ("pos_k", CL), ("pos_v", CL), ("sink", SWA_HEADS)])


class Steps:

    def __init__(self, eng, sem, base=0):
        self.eng, self.sem, self.n = eng, sem, base

    def __call__(self, ins):
        self.n = self.n + 1
        ins.then_inc(self.sem, 1)
        self.eng.wait_ge(self.sem, self.n)


def program(nc, xT, pT, wstream, consts, setup, params, out):
    import concourse.bass as bass
    from concourse import mybir

    F32, FR = mybir.dt.float32, mybir.dt.float32r
    ALU, ACT = mybir.AluOpType, mybir.ActivationFunctionType
    AX = mybir.AxisListType.X
    ds = bass.ds

    bias_rows = nc.dram_tensor("bias_rows", [SWA_HEADS, P * RB], F32)

    with ExitStack() as ctx:
        def sb(name, shape, dt=F32):
            return ctx.enter_context(nc.sbuf_tensor(name, shape, dt))

        def sem(name):
            return ctx.enter_context(nc.semaphore(name))

        raw = sb("raw", [P, SLOTS, PW])
        whi = sb("whi", [P, SLOTS, PW], FR)
        wlo = sb("wlo", [P, SLOTS, PW], FR)
        x = sb("x", [P, DT, S])
        A = sb("A", [P, DT, 2, S], FR)
        H = sb("H", [P, CH, 2, S], FR)
        pA = sb("pA", [P, 2, 2, S], FR)
        y = sb("y", [P, DT, S])
        kT = sb("kT", [P, 2, KVG, S])
        vN = sb("vN", [P, 2 * QT, 4 * P])
        qs = sb("qs", [P, HPG, S])
        kst = sb("kst", [P, 2, S])
        vst = sb("vst", [P, 2 * QT, P])
        Sm = sb("Sm", [P, 3 * 8 * P])
        PT = sb("PT", [P, QT, 8, P])
        bias = sb("bias", [P, 8, 2 * P])
        con = sb("con", [P, NCONST])
        par = sb("par", [P, NPAR])
        ones = sb("ones", [P, P])
        acc = sb("acc", [P, S])
        rs = sb("rs", [P, S])
        rcol = sb("rcol", [P, QT])
        gg = sb("gg", [P, DT])
        gts = sb("gts", [P, QT, 3 * HEADS])
        small = sb("small", [P, 6, 16])
        psum = [ctx.enter_context(nc.psum_tensor(f"bank{i}", [P, 512], F32)) for i in range(8)]

        z = qs
        bflat = bias[:, :, :].rearrange("p a b -> p (a b)")
        ptf = PT[:, :, :, :].rearrange("p a b c -> p (a b c)")

        def ring(flat, a, n=4, w=S):
            return flat[:, a:a + n * w].rearrange("p (n w) -> p n w", n=n)

        zr, sq = ring(bflat, 0), ring(bflat, 4 * S)
        tA, tB, tC = ring(Sm, 0), ring(Sm, 4 * S), ring(Sm, 8 * S)
        ub, c0 = ring(ptf, 0, 4, S + 4), ring(ptf, 4 * (S + 4), 2)
        sq2 = ring(ptf, 0)
        acc2, rs2, rs3 = tC[:, 0, :], tC[:, 1, :], tC[:, 2, :]
        csig, ch = tC[:, 3, 0:128], tC[:, 3, 128:256]
        pcT = bflat[:, 0:1024].rearrange("p (t r q) -> p t r q", t=QT, r=HPG)
        vczall = bflat[:, 1024:1536].rearrange("p (g d) -> p g d", g=KVG)
        vcz, kcmp = bflat[:, 1536:1664], bflat[:, 1664:1792]
        cs = bflat[:, 1792:1920].rearrange("p (a b) -> p a b", a=8)
        kvc = Sm[:, 0:2048].rearrange("p (b g t) -> p b g t", b=2, g=KVG)
        blkf = ptf[:, 0:CL * KVG * NCMP].rearrange("p (l g n) -> p l g n", l=CL, g=KVG)
        NB = KVG * NCMP
        blks = H[:, :, :, :].rearrange("p a b c -> p (a b c)")[:, 0:2 * CL * 2 * NB].rearrange(
            "p (b l h c) -> p b l h c", b=2, l=CL, h=2)
        cprob = Sm[:, 0:512].rearrange("p (t h n) -> p t h n", t=QT, h=HEADS)
        cpad = Sm[:, 1024:2048].rearrange("p (t r g n) -> p t r g n", t=QT, r=HPG, g=KVG)
        Smq = [Sm[:, 0:8 * P].rearrange("p (e k) -> p e k", e=8),
               Sm[:, 8 * P:24 * P].rearrange("p (e k) -> p e k", e=8)]
        mx, nmx, sums, esk, tot, coef = (small[:, i, :] for i in range(6))
        ident = con[:, CO["ident"][0]:CO["ident"][1]]
        mask = con[:, CO["mask"][0]:CO["mask"][1]]
        cmask = con[:, CO["cmask"][0]:CO["cmask"][1]].rearrange("p (t n) -> p t n", t=QT)
        cvalid = con[:, CO["cvalid"][0]:CO["cvalid"][1]].rearrange("p (t n) -> p t n", t=QT)

        def gain(name, t):
            return par[:, ds(PO[name][0] + t, 1)]

        def tile(buf, t):
            return buf[:, ds(t, 1), :].rearrange("p a b -> p (a b)")

        def part(buf, t, h):
            return buf[:, ds(t, 1), h, :].rearrange("p a b -> p (a b)")

        raw_landed = [sem(f"raw_landed{i}") for i in range(SLOTS)]
        hi_ready, lo_ready = sem("hi_ready"), sem("lo_ready")
        piece_used = sem("piece_used")
        z_ready = sem("z_ready")
        z_used = sem("z_used")
        in_x, in_c, in_p, in_s = sem("in_x"), sem("in_c"), sem("in_p"), sem("in_s")
        ones_set, gg_ready, pad_zero = sem("ones_set"), sem("gg_ready"), sem("pad_zero")
        table_sum, table_row, rows_out = (sem(n) for n in ("table_sum", "table_row", "rows_out"))
        x0_hi, a0_ready, x0_sq = sem("x0_hi"), sem("a0_ready"), sem("x0_sq")
        p_hi, p_ready = sem("p_hi"), sem("p_ready")
        acc_step = sem("acc_step")
        acc_zero = sem("acc_zero")
        sum_ready, sum_step, var_ready, root_ready, rs_ready = (sem(n) for n in ("sum_ready", "sum_step", "var_ready", "root_ready", "rs_ready"))
        rs_turned, rcol_ready = sem("rs_turned"), sem("rcol_ready")
        blk_step, blk_hi, blk_ready = sem("blk_step"), sem("blk_hi"), sem("blk_ready")
        csig_ready, ch_ready, ch_hi, h1_ready = (sem(n) for n in ("csig_ready", "ch_ready", "ch_hi", "h1_ready"))
        gate_sum, gates_ready, kcmp_ready, vcmp_ready = (sem(n) for n in ("gate_sum", "gates_ready", "kcmp_ready", "vcmp_ready"))
        vcz_zero, cpad_zero, c_scores, c_step, c_shift, c_exp, cp_ready, c_turned, pcT_ready = (
            sem(n) for n in ("vcz_zero", "cpad_zero", "c_scores", "c_step", "c_shift", "c_exp", "cp_ready", "c_turned", "pcT_ready"))
        att = {k: {n: sem(f"{k}_{n}") for n in (
            "q_staged", "kv_staged", "scores", "max", "step", "shift", "sinkdiff", "exp", "sinkexp", "coef", "scaled",
            "turned", "pt_act", "pt_dve", "o_done", "o_hi", "o_ready", "bias_in")} for k in ("nsa", "swa")}
        wo_hi, wo_sq, a1_ready = sem("wo_hi"), sem("wo_sq"), sem("a1_ready")
        ff_relu, ff_hi, ff_step, ff_ready = sem("ff_relu"), sem("ff_hi"), sem("ff_step"), sem("ff_ready")
        fd_hi, fd_sq, a2_ready = sem("fd_hi"), sem("fd_sq"), sem("a2_ready")
        ple_sig, ple_step, ple_x, ple_hi, ple_sq, a3_ready = (sem(n) for n in ("ple_sig", "ple_step", "ple_x", "ple_hi", "ple_sq", "a3_ready"))
        xn_ready = sem("xn_ready")
        wo2_sq = sem("wo2_sq")
        post_t, post_x, post_hi, post_sq, a4_ready = (sem(n) for n in ("post_t", "post_x", "post_hi", "post_sq", "a4_ready"))
        up_c0, up_step, up_conv, up_sig, up_gated, up_h, up_hi, up_ready = (
            sem(n) for n in ("up_c0", "up_step", "up_conv", "up_sig", "up_gated", "up_h", "up_hi", "up_ready"))
        dn_sq = sem("dn_sq")
        fin_t, fin_x, out_done = sem("fin_t"), sem("fin_x"), sem("out_done")

        NORMS = ["kv", "ff0", "gate", "k2", "post", "up0", "end"]
        ACC0 = {n: DT * i for i, n in enumerate(NORMS)}
        ACC0.update({n: ACC0[n] + DT for n in ("post", "up0", "end")})
        NACC = {n: (2 * DT if n == "k2" else DT) for n in NORMS}
        RS0 = {n: i for i, n in enumerate(NORMS)}

        def o_parts(nsa, t):
            if nsa:
                return [(slice(0, P), psum[t])]
            return [(slice(h * HD, h * HD + HD), psum[2 * t + h]) for h in range(2)]

        def ends(n, K):
            at = {}
            for j in range(n):
                at.setdefault(((j + 1) * K - 1) // BLK, []).append(j)
            return at

        block = ctx.enter_context(nc.Block())

        @block.sync
        def _(sp):
            sp.dma_start(par[:, :], params).then_inc(in_c, 16)
            sp.dma_start(con[:, :], consts).then_inc(in_c, 16)
            for i in range(4):
                sp.dma_start(x[:, 4 * i:4 * i + 4, :], xT[:, 4 * i:4 * i + 4, :]).then_inc(in_x, 16)
            for i in range(SLOTS):
                sp.dma_start(raw[:, i, :], wstream[i]).then_inc(raw_landed[i], 16)

            def load(i, s):
                sp.wait_ge(lo_ready, i - SLOTS + 1)
                sp.dma_start(raw[:, s, :], wstream[ds(i, 1)].rearrange("a p n -> p (a n)")).then_inc(raw_landed[s], 16)

            with sp.Fori(0, NPIECE // SLOTS - 1) as it:
                for j in range(SLOTS):
                    load(it * SLOTS + (SLOTS + j), j)
            for i in range(NPIECE // SLOTS * SLOTS, NPIECE):
                sp.wait_ge(lo_ready, i - SLOTS + 1)
                sp.dma_start(raw[:, i % SLOTS, :], wstream[i]).then_inc(raw_landed[i % SLOTS], 16)
            for i in range(4):
                sp.wait_ge(fin_x, 4 * i + 4)
                sp.dma_start(out[:, 4 * i:4 * i + 4, :], x[:, 4 * i:4 * i + 4, :]).then_inc(out_done, 16)
            sp.wait_ge(out_done, 64)

        @block.tensor
        def _(pe):
            pe.sem_inc(piece_used, SLOTS)

            def units(p, p0, u, u0, n, K, moving, ready=None, width=S):
                for b in range(n * K):
                    j, k = divmod(b, K)
                    s = (p0 + b // BLK) % SLOTS
                    if b % BLK == 0:
                        pe.wait_ge(lo_ready, p + (b // BLK + 1))
                    if k == 0:
                        pe.wait_ge(z_ready, u + (j + 1))
                    if ready and j == 0:
                        pe.wait_ge(*ready(k))
                    bank = psum[(u0 + j) % 4]
                    w = slice(b % BLK * P, b % BLK * P + P)
                    m = moving(j, k)

                    def lo():
                        return nc.tensor.matmul(bank[:, 0:width], wlo[:, s, w], m[:, 0, :], start=False, stop=False)
                    if k == K - 1:
                        lo()
                    last = nc.tensor.matmul(bank[:, 0:2 * width], whi[:, s, w], m, start=(k == 0), stop=(k == K - 1))
                    if k < K - 1:
                        last = lo()
                    if b % BLK == BLK - 1:
                        last.then_inc(piece_used, 1)

            def norm(name, u, src=acc[:, :]):
                pe.wait_ge(z_ready, u + 1)
                pe.wait_ge(acc_step, ACC0[name] + NACC[name])
                nc.tensor.matmul(psum[u % 4][:, 0:S], ones[:, :], src, start=True, stop=True).then_inc(sum_ready, 1)

            def turn_rs(i):
                pe.wait_ge(rs_ready, i)
                for t in range(QT):
                    last = nc.tensor.transpose(psum[4][:, t * P:t * P + P], rs[:, t * P:t * P + P], ident)
                last.then_inc(rs_turned, 1)

            def natural(p, u, src):
                for t in range(QT):
                    pe.wait_ge(z_ready, u + t + 1)
                for k in range(DT):
                    if k % 2 == 0:
                        pe.wait_ge(lo_ready, p + k // 2 + 1)
                    s, w = (p + k // 2) % SLOTS, slice(k % 2 * 512, k % 2 * 512 + 512)
                    for t in range(QT):
                        tok = slice(t * P, t * P + P)
                        bank = psum[(u + t) % 4]
                        nc.tensor.matmul(bank[:, :], src[:, k, 0, tok], whi[:, s, w], start=(k == 0), stop=False)
                        nc.tensor.matmul(bank[:, :], src[:, k, 0, tok], wlo[:, s, w], start=False, stop=False)
                        last = nc.tensor.matmul(bank[:, :], src[:, k, 1, tok], whi[:, s, w], start=False, stop=(k == DT - 1))
                    if k % 2 == 1:
                        last.then_inc(piece_used, 1)

            def attention(kind):
                sm = att[kind]
                nsa = kind == "nsa"
                with pe.Fori(0, KVG) as it:
                    pe.wait_ge(sm["q_staged"], it + 1)
                    pe.wait_ge(sm["kv_staged"], it * (3 if nsa else 2) + (3 if nsa else 2))
                    pe.wait_ge(sm["o_ready"], it * 2 + 2)
                    for t in range(QT):
                        nk = (t + 1) * P
                        for e in range(8):
                            if nsa:
                                lhs, rhs = qs[:, e % 4, t * P:t * P + P], kst[:, e // 4, 0:nk]
                            else:
                                h = slice(e // 4 * HD, e // 4 * HD + HD)
                                lhs, rhs = qs[h, e % 4, t * P:t * P + P], kst[h, 0, 0:nk]
                            bank, c = (psum[e // 4], e % 4 * P) if t == 0 else (psum[2 + e // 2], e % 2 * 2 * P)
                            nc.tensor.matmul(bank[:, c:c + nk], lhs, rhs, start=True, stop=True).then_inc(sm["scores"], 1)
                    n = 0
                    for t in range(QT):
                        for half in range(2):
                            pe.wait_ge(sm["scaled"], it * 4 + (2 * t + half + 1))
                            for kt in range(t + 1):
                                done = sm["pt_act"] if n % 2 == 0 else sm["pt_dve"]
                                pe.wait_ge(done, it * 3 + (n // 2 + 1))
                                for e in range(4):
                                    last = nc.tensor.transpose(psum[6 + n % 2][:, e * P:e * P + P],
                                                               Smq[t][:, half * 4 + e, kt * P:kt * P + P], ident)
                                last.then_inc(sm["turned"], 1)
                                n += 1
                        pe.wait_ge(sm["pt_act"], it * 3 + (n // 2 + 1))
                        pe.wait_ge(sm["pt_dve"], it * 3 + (n // 2 + 1))
                        if nsa:
                            steps = [(vst[:, b * QT + kt, :], PT[:, kt, 4 * b:4 * b + 4, :]) for b in range(2) for kt in range(t + 1)]
                            steps.append((vcz, pcT[:, t, :, :]))
                            for i, (lhs, rhs) in enumerate(steps):
                                last = nc.tensor.matmul(psum[t][:, :], lhs, rhs, start=(i == 0), stop=(i == len(steps) - 1))
                        else:
                            for half in range(2):
                                for kt in range(t + 1):
                                    last = nc.tensor.matmul(psum[2 * t + half][:, :], vst[:, kt, :], PT[:, kt, 4 * half:4 * half + 4, :],
                                                            start=(kt == 0), stop=(kt == t))
                        last.then_inc(sm["o_done"], 1)

            pe.wait_ge(in_s, 16)
            nc.tensor.matmul(psum[7][0:SWA_HEADS, 0:RB], bflat[0:NBUCK, SO["table"][0]:SO["table"][1]],
                             bflat[0:NBUCK, SO["onehot"][0]:SO["onehot"][1]], start=True, stop=True).then_inc(table_sum, 1)
            pe.wait_ge(ones_set, 1)
            norm("kv", 0)
            pe.wait_ge(in_c, 32)
            turn_rs(1)

            for st in ("kv", "q"):
                with pe.Fori(0, 4) as it:
                    units(it * 8 + PB[st], PB[st], it * 4 + UB[st], UB[st], 4, DT, lambda j, k: A[:, k, :, :],
                          (lambda k: (a0_ready, k + 1)) if st == "kv" else None)
            for b in range(2):
                natural(PB["v"] + 8 * b, UB["v"] + 2 * b, A)
            pe.wait_ge(blk_ready, 2)
            units(PB["cmp"], PB["cmp"], UB["cmp"], UB["cmp"], 2, CL, lambda b, l: blks[:, b, l, :, :], width=NB)
            p, u = PB["misc"], UB["misc"]
            s = p % SLOTS
            pe.wait_ge(lo_ready, p + 1)
            for t in range(QT):
                pe.wait_ge(z_ready, u + t + 1)
                tok = slice(t * P, t * P + P)
                bank = psum[(u + t) % 4][:, 0:48]
                for k in range(DT):
                    w = slice(k * 48, k * 48 + 48)
                    nc.tensor.matmul(bank, A[:, k, 0, tok], whi[:, s, w], start=(k == 0), stop=False)
                    nc.tensor.matmul(bank, A[:, k, 0, tok], wlo[:, s, w], start=False, stop=False)
                    last = nc.tensor.matmul(bank, A[:, k, 1, tok], whi[:, s, w], start=False, stop=(k == DT - 1))
                last.then_inc(gate_sum, 1)
            wk, wv = slice(16 * 48, 16 * 48 + P), slice(16 * 48 + P, 16 * 48 + 2 * P)
            pe.wait_ge(h1_ready, 2)
            pe.wait_ge(z_ready, u + 3)
            bank = psum[(u + 2) % 4][:, 0:P]
            nc.tensor.matmul(bank, whi[:, s, wk], pA[:, 0, 0, 0:P], start=True, stop=False)
            nc.tensor.matmul(bank, wlo[:, s, wk], pA[:, 0, 0, 0:P], start=False, stop=False)
            nc.tensor.matmul(bank, whi[:, s, wk], pA[:, 0, 1, 0:P], start=False, stop=True).then_inc(gate_sum, 1)
            pe.wait_ge(z_ready, u + 4)
            bank = psum[(u + 3) % 4][:, 0:P]
            nc.tensor.matmul(bank, pA[:, 1, 0, 0:P], whi[:, s, wv], start=True, stop=False)
            nc.tensor.matmul(bank, pA[:, 1, 0, 0:P], wlo[:, s, wv], start=False, stop=False)
            nc.tensor.matmul(bank, pA[:, 1, 1, 0:P], whi[:, s, wv], start=False, stop=True).then_inc(gate_sum, 1)
            pe.sem_inc(piece_used, 1)
            pe.wait_ge(kcmp_ready, 1)
            pe.wait_ge(z_used, 4 + ZB["q"] + 16)
            pe.wait_ge(rcol_ready, 1)
            for t in range(QT):
                for h in range(HEADS):
                    g = h // HPG
                    last = nc.tensor.matmul(psum[4 + t][:, h * CS:h * CS + CS], y[:, h, t * P:t * P + P],
                                            kcmp[:, g * NPAD:g * NPAD + CS], start=True, stop=True)
                last.then_inc(c_scores, 1)
            for t in range(QT):
                pe.wait_ge(cp_ready, t + 1)
                for r in range(HPG):
                    last = nc.tensor.transpose(psum[6 + t][:, r * P:r * P + P],
                                               cpad[:, t, r, :, :].rearrange("p g n -> p (g n)"), ident)
                last.then_inc(c_turned, 1)
            pe.wait_ge(z_ready, 4 + UB["wo"])
            pe.wait_ge(pcT_ready, QT)
            attention("nsa")
            with pe.Fori(0, 4) as it:
                units(it * 8 + PB["wo"], PB["wo"], it * 4 + UB["wo"], UB["wo"], 4, DT, lambda j, k: H[:, k, :, :],
                      lambda k: (att["nsa"]["o_ready"], 2 + k // 4 * 2 + 2))

            norm("ff0", UB["ff0"] - 1)

            def chunk(c):
                with pe.Fori(0, 4) as it:
                    units(c * 64 + it * 8 + PB["ff0"], PB["ff0"], c * 32 + it * 4 + UB["ff0"], UB["ff0"], 4, DT,
                          lambda j, k: A[:, k, :, :], lambda k: (a1_ready, k + 1))
                with pe.Fori(0, 4) as it:
                    units(c * 64 + it * 8 + PB["fd0"], PB["fd0"], c * 32 + it * 4 + UB["fd0"], UB["fd0"], 4, CH,
                          lambda j, k: H[:, k, :, :], lambda k: (ff_ready, c * CH + (k + 1)))
            with pe.Fori(0, FF_CHUNKS - 1) as c:
                chunk(c)
            chunk(FF_CHUNKS - 1)

            pe.wait_ge(p_ready, 2)
            units(PB["proj"], PB["proj"], UB["proj"], UB["proj"], DT, 2, lambda j, k: pA[:, k, :, :])
            norm("gate", UB["gate"] - 1)
            with pe.Fori(0, 4) as it:
                units(it * 8 + PB["gate"], PB["gate"], it * 4 + UB["gate"], UB["gate"], 4, DT, lambda j, k: A[:, k, :, :],
                      lambda k: (a2_ready, k + 1))

            norm("k2", UB["k2"] - 2)
            norm("k2", UB["k2"] - 1, acc2)
            turn_rs(5)
            units(PB["k2"], PB["k2"], UB["k2"], UB["k2"], 4, DT, lambda j, k: H[:, k, :, :], lambda k: (a3_ready, k + 1))
            natural(PB["v2"], UB["v2"], H)
            with pe.Fori(0, 4) as it:
                units(it * 8 + PB["q2"], PB["q2"], it * 4 + UB["q2"], UB["q2"], 4, DT, lambda j, k: H[:, k, :, :])
            pe.wait_ge(z_ready, 4 + UB["wo2"])
            attention("swa")
            with pe.Fori(0, 4) as it:
                units(it * 8 + PB["wo2"], PB["wo2"], it * 4 + UB["wo2"], UB["wo2"], 4, DT, lambda j, k: H[:, k, :, :],
                      lambda k: (att["swa"]["o_ready"], 2 + k // 4 * 2 + 2))
            norm("post", UB["up0"] - 2)
            norm("up0", UB["up0"] - 1)

            t0 = 0
            for c, n in enumerate(CHUNKS2):
                up, dn = f"up{c}", f"dn{c}"
                with pe.Fori(0, n // 2) as it:
                    units(it * 8 + PB[up], PB[up], it * 4 + UB[up], UB[up], 4, DT, lambda j, k: A[:, k, :, :],
                          lambda k: (a4_ready, k + 1))
                if n == CH:
                    with pe.Fori(0, 4) as it:
                        units(it * 8 + PB[dn], PB[dn], it * 4 + UB[dn], UB[dn], 4, n, lambda j, k: H[:, k, :, :],
                              lambda k: (up_ready, t0 + k + 1))
                else:
                    for it in range(2):
                        units(it * n + PB[dn], PB[dn], it * 8 + UB[dn], UB[dn], 8, n, lambda j, k: H[:, k, :, :],
                              lambda k: (up_ready, t0 + k + 1))
                t0 += n
            norm("end", UB["end"])

        @block.vector
        def _(dve):
            V = nc.vector
            dve.sem_inc(z_ready, 4)

            def split_lo(i, s):
                dve.wait_ge(hi_ready, i + 1)
                V.tensor_tensor(wlo[:, s, :], raw[:, s, :], whi[:, s, :].bitcast(F32), ALU.subtract).then_inc(lo_ready, 1)

            def body(p, p0, u, u0, zu, z0, n, K, late=None, width=S, last=False):
                at = ends(n, K)
                waiting = []
                for i in range(n * K // BLK):
                    if not last or i + LEAD < n * K // BLK:
                        split_lo(p + (i + LEAD), (p0 + i + LEAD) % SLOTS)
                    while waiting:
                        late(waiting.pop(0))
                    for j in at.get(i, []):
                        dve.wait_ge(piece_used, p + (SLOTS + i + 1))
                        dve.wait_ge(z_used, zu + (j + 1))
                        V.tensor_reduce(z[:, (z0 + j) % 4, 0:width],
                                        psum[(u0 + j) % 4][:, 0:2 * width].rearrange("p (h c) -> p c h", h=2),
                                        AX, ALU.add).then_inc(z_ready, 1)
                        if late:
                            waiting.append(j)
                while waiting:
                    late(waiting.pop(0))

            steps = Steps(dve, sum_step)

            def rsqrt(dst, var, n):
                dve.wait_ge(root_ready, n)
                steps(V.reciprocal(dst, dst))
                steps(V.tensor_tensor(var, var, dst, ALU.mult))
                steps(V.tensor_tensor(var, var, dst, ALU.mult))
                steps(V.tensor_scalar(var, var, -0.5, 1.5, ALU.mult, ALU.add))
                return V.tensor_tensor(dst, dst, var, ALU.mult)

            def norm(u, dst, n):
                dve.wait_ge(sum_ready, n)
                V.tensor_scalar(acc[:, :], psum[u % 4][:, 0:S], 1.0 / D, EPS, ALU.mult, ALU.add).then_inc(var_ready, 1)
                dve.wait_ge(var_ready, n)
                dve.sem_inc(z_ready, 1)
                return rsqrt(dst, acc[:, :], n)

            def columns_of_rs(n):
                dve.wait_ge(rs_turned, n)
                V.tensor_copy(rcol[:, :], psum[4][:, 0:QT * P].rearrange("p (t c) -> p t c", t=QT)[:, :, 0]).then_inc(rcol_ready, 1)
                dve.wait_ge(rcol_ready, n)

            def values(p, u, v0):
                for i in range(8):
                    split_lo(p + i + LEAD, (p + i + LEAD) % SLOTS)
                dve.wait_ge(piece_used, SLOTS + p + 8)
                for t in range(QT):
                    V.tensor_scalar(vN[:, v0 + t, :], psum[(u + t) % 4][:, :], rcol[:, t:t + 1], None, ALU.mult).then_inc(z_ready, 1)

            def norm_lo(dst, name, hi_sem, ready):
                def late(t, i):
                    dve.wait_ge(hi_sem, i + 1)
                    V.scalar_tensor_tensor(part(dst, t, 1), tile(x, t), gain(name, t) if name else gg[:, ds(t, 1)],
                                           part(dst, t, 0).bitcast(F32), ALU.mult, ALU.subtract).then_inc(ready, 1)
                return late

            def attention(kind):
                sm = att[kind]
                nsa = kind == "nsa"
                dve.sem_inc(sm["o_ready"], 2)
                dve.sem_inc(sm["pt_dve"], 1)
                per = 2
                with dve.Fori(0, KVG) as it:
                    st = Steps(dve, sm["step"], it * (2 * per))
                    for t in range(QT):
                        nk = (t + 1) * P
                        c = slice(8 * t, 8 * t + 8)
                        if not nsa and t == 0:
                            dve.wait_ge(sm["bias_in"], it * 16 + 16)
                        for e in range(8):
                            bank, o = (psum[e // 4], e % 4 * P) if t == 0 else (psum[2 + e // 2], e % 2 * 2 * P)
                            add = mask[:, 2 * P - nk:] if nsa else bias[:, e, 2 * P - nk:]
                            in_bank = 4 if t == 0 else 2
                            if e % in_bank == 0:
                                dve.wait_ge(sm["scores"], it * 16 + (8 * t + e + in_bank))
                                V.memset(tot[:, 8 * t + e:8 * t + e + 1], 0.0)
                            V.tensor_tensor_reduce(Smq[t][:, e, :], bank[:, o:o + nk], add, 1.0, -3e38, ALU.add, ALU.max,
                                                   mx[:, 8 * t + e:8 * t + e + 1]).then_inc(sm["max"], 1)
                        dve.wait_ge(sm["max"], it * 16 + (8 * t + 8))
                        if nsa:
                            V.tensor_scalar(nmx[:, c], mx[:, c], -1.0, None, ALU.mult).then_inc(sm["shift"], 1)
                        else:
                            sink = par[:, ds(it * 8 + PO["sink"][0], 8)]
                            st(V.tensor_tensor(mx[:, c], mx[:, c], sink, ALU.max))
                            V.tensor_scalar(nmx[:, c], mx[:, c], -1.0, None, ALU.mult).then_inc(sm["shift"], 1)
                            V.tensor_tensor(esk[:, c], sink, mx[:, c], ALU.subtract).then_inc(sm["sinkdiff"], 1)
                    for t in range(QT):
                        c = slice(8 * t, 8 * t + 8)
                        dve.wait_ge(sm["exp"], it * 16 + (8 * t + 8))
                        if nsa:
                            st(V.reciprocal(tot[:, c], sums[:, c]))
                            st(V.tensor_copy(coef[:, c], gts[:, t, ds(it * 12 + 4, 8)]))
                            V.tensor_tensor(coef[:, c], coef[:, c], tot[:, c], ALU.mult).then_inc(sm["coef"], 1)
                        else:
                            dve.wait_ge(sm["sinkexp"], it * 2 + (t + 1))
                            st(V.tensor_tensor(tot[:, c], sums[:, c], esk[:, c], ALU.add))
                            V.reciprocal(coef[:, c], tot[:, c]).then_inc(sm["coef"], 1)
                    for n, (t, half, kt) in enumerate([(0, 0, 0), (0, 1, 0), (1, 0, 0), (1, 0, 1), (1, 1, 0), (1, 1, 1)]):
                        if n % 2 == 1:
                            dve.wait_ge(sm["turned"], it * 6 + (n + 1))
                            V.tensor_copy(PT[:, kt, 4 * half:4 * half + 4, :],
                                          psum[6 + n % 2][:, :].rearrange("p (e q) -> p e q", e=4)).then_inc(sm["pt_dve"], 1)
                        if n in (1, 5):
                            tok = slice(t * P, t * P + P)
                            dve.wait_ge(sm["o_hi"], it * 2 + (t + 1))
                            for rows, bank in o_parts(nsa, t):
                                last = V.tensor_tensor(H[rows, ds(it * 4, 4), 1, tok], bank[rows, :].rearrange("p (r q) -> p r q", r=4),
                                                       H[rows, ds(it * 4, 4), 0, tok].bitcast(F32), ALU.subtract)
                            last.then_inc(sm["o_ready"], 1)

            dve.wait_ge(table_sum, 1)
            V.tensor_tensor(bflat[0:NBUCK, 1024:1024 + RB], psum[7][0:SWA_HEADS, 0:RB],
                            bflat[0:NBUCK, SO["band"][0]:SO["band"][1]], ALU.add).then_inc(table_row, 1)
            dve.wait_ge(in_c, 32)
            V.tensor_tensor(gg[:, :], par[:, PO["g_fin"][0]:PO["g_fin"][1]], par[:, PO["g0"][0]:PO["g0"][1]],
                            ALU.mult).then_inc(gg_ready, 1)
            for t in range(DT):
                dve.wait_ge(x0_hi, t + 1)
                V.scalar_tensor_tensor(A[:, t, 1, :], x[:, t, :], gain("g_mix", t), A[:, t, 0, :].bitcast(F32), ALU.mult,
                                       ALU.subtract).then_inc(a0_ready, 1)
                if t % 4 == 3 and t // 4 < LEAD:
                    split_lo(t // 4, t // 4)
            norm(0, rs[:, :], 1).then_inc(rs_ready, 1)
            dve.wait_ge(rs_ready, 1)
            V.tensor_scalar(rs2, rs[:, :], float(P) ** -0.5, None, ALU.mult).then_inc(rs_ready, 1)
            columns_of_rs(1)
            for st in ("kv", "q"):
                with dve.Fori(0, 4) as it:
                    body(it * 8 + PB[st], PB[st], it * 4 + UB[st], UB[st], it * 4 + ZB[st], ZB[st], 4, DT)
            dve.wait_ge(z_used, 4 + ZB["kv"] + 8)
            for b, pos in enumerate(("pos_k", "pos_v")):
                src = kvc[:, b, :, :].rearrange("p g (m s) -> p s g m", s=CS)
                for half in range(2):
                    emb = par[:, PO[pos][0] + CS * half:PO[pos][0] + CS * half + CS].unsqueeze(2).to_broadcast([P, CS, NCMP])
                    for g in range(KVG):
                        V.tensor_tensor(blkf[:, CS * half:CS * half + CS, g, :], src[:, :, g, half:half + NCMP], emb,
                                        ALU.add).then_inc(blk_step, 1)
                dve.wait_ge(blk_hi, b + 1)
                dve.wait_ge(blk_step, 8 * b + 8)
                V.tensor_tensor(blks[:, b, :, 1, :], blkf[:, :, :, :].rearrange("p l g n -> p l (g n)"),
                                blks[:, b, :, 0, :].bitcast(F32), ALU.subtract).then_inc(blk_ready, 1)
                dve.wait_ge(blk_ready, b + 1)
            for b in range(2):
                values(PB["v"] + 8 * b, UB["v"] + 2 * b, 2 * b)
            body(PB["cmp"], PB["cmp"], UB["cmp"], UB["cmp"], ZB["cmp"], ZB["cmp"], 2, CL, width=NB)
            split_lo(PB["misc"] + LEAD, (PB["misc"] + LEAD) % SLOTS)
            u = UB["misc"]
            for b in range(2):
                dve.wait_ge(ch_hi, b + 1)
                V.tensor_tensor(pA[:, b, 1, 0:P].rearrange("p (g n) -> p g n", g=KVG)[:, :, 0:NCMP],
                                ch[:, b * 64:b * 64 + NB].rearrange("p (g n) -> p g n", g=KVG),
                                pA[:, b, 0, 0:P].rearrange("p (g n) -> p g n", g=KVG)[:, :, 0:NCMP].bitcast(F32),
                                ALU.subtract).then_inc(h1_ready, 1)
            for t in range(QT):
                dve.wait_ge(gate_sum, t + 1)
                V.tensor_scalar(gts[:, t, :], psum[(u + t) % 4][:, 0:48], rcol[:, t:t + 1], None, ALU.mult).then_inc(z_ready, 1)
            dve.wait_ge(gate_sum, 3)
            V.tensor_copy(kcmp, psum[(u + 2) % 4][:, 0:P]).then_inc(kcmp_ready, 1)
            dve.wait_ge(kcmp_ready, 1)
            dve.sem_inc(z_ready, 1)
            dve.wait_ge(gate_sum, 4)
            dve.wait_ge(vcz_zero, 1)
            for g in range(KVG):
                rows = slice(g * NPAD, g * NPAD + NPAD)
                V.tensor_copy(vczall[rows, g, :], psum[(u + 3) % 4][rows, 0:P]).then_inc(vcmp_ready, 1)
            dve.wait_ge(vcmp_ready, KVG)
            dve.sem_inc(z_ready, 1)
            st = Steps(dve, c_step)
            dve.wait_ge(cpad_zero, 1)
            for t in range(QT):
                c = cprob[:, t, :, :]
                dve.wait_ge(c_scores, t + 1)
                st(V.tensor_tensor(c, psum[4 + t][:, 0:HEADS * CS].rearrange("p (h n) -> p h n", h=HEADS),
                                   cmask[:, t, :].unsqueeze(1).to_broadcast([P, HEADS, CS]), ALU.add))
                st(V.tensor_reduce(cs[:, t, :], c, AX, ALU.max))
                V.tensor_tensor(c, c, cs[:, t, :].unsqueeze(2).to_broadcast([P, HEADS, CS]), ALU.subtract).then_inc(c_shift, 1)
            dve.wait_ge(gates_ready, QT)
            for t in range(QT):
                c = cprob[:, t, :, :]
                dve.wait_ge(c_exp, t + 1)
                st(V.tensor_reduce(cs[:, 2 + t, :], c, AX, ALU.add))
                st(V.reciprocal(cs[:, 4 + t, :], cs[:, 2 + t, :]))
                st(V.tensor_tensor(cs[:, 6 + t, :].rearrange("p (g r) -> p g r", g=KVG),
                                   cs[:, 4 + t, :].rearrange("p (g r) -> p g r", g=KVG),
                                   gts[:, t, :].rearrange("p (g b r) -> p g b r", g=KVG, b=3)[:, :, 0, :], ALU.mult))
                st(V.tensor_tensor(c, c, cs[:, 6 + t, :].unsqueeze(2).to_broadcast([P, HEADS, CS]), ALU.mult))
                for g in range(KVG):
                    last = V.tensor_tensor(cpad[:, t, :, g, 0:CS], c[:, HPG * g:HPG * g + HPG, :],
                                           cvalid[:, t, :].unsqueeze(1).to_broadcast([P, HPG, CS]), ALU.mult)
                last.then_inc(cp_ready, 1)
            for t in range(QT):
                dve.wait_ge(c_turned, t + 1)
                V.tensor_copy(pcT[:, t, :, :], psum[6 + t][:, :].rearrange("p (r q) -> p r q", r=HPG)).then_inc(pcT_ready, 1)
            attention("nsa")

            lo1 = norm_lo(A, "g_ffn", wo_hi, a1_ready)
            with dve.Fori(0, 4) as it:
                body(it * 8 + PB["wo"], PB["wo"], it * 4 + UB["wo"], UB["wo"], it * 4 + ZB["wo"], ZB["wo"], 4, DT,
                     lambda j: lo1(it * 4 + j, it * 4 + j))
            norm(UB["ff0"] - 1, rs[:, :], 2).then_inc(rs_ready, 1)
            for k in range(2):
                dve.wait_ge(p_hi, k + 1)
                V.tensor_tensor(pA[:, k, 1, :], tC[:, k, :], pA[:, k, 0, :].bitcast(F32), ALU.subtract).then_inc(p_ready, 1)

            def chunk(c, late):
                for st, K in (("ff0", DT), ("fd0", CH)):
                    with dve.Fori(0, 4) as it:
                        body(c * 64 + it * 8 + PB[st], PB[st], c * 32 + it * 4 + UB[st], UB[st],
                             c * 32 + it * 4 + ZB[st], ZB[st], 4, K,
                             (lambda j: late(it * 4 + j, it * 4 + j)) if late and st == "fd0" else None)
            with dve.Fori(0, FF_CHUNKS - 1) as c:
                chunk(c, None)
            chunk(FF_CHUNKS - 1, norm_lo(A, "g_ple", fd_hi, a2_ready))
            body(PB["proj"], PB["proj"], UB["proj"], UB["proj"], ZB["proj"], ZB["proj"], DT, 2)
            norm(UB["gate"] - 1, rs[:, :], 3).then_inc(rs_ready, 1)
            lo3 = norm_lo(H, None, ple_hi, a3_ready)
            with dve.Fori(0, 4) as it:
                body(it * 8 + PB["gate"], PB["gate"], it * 4 + UB["gate"], UB["gate"], it * 4 + ZB["gate"], ZB["gate"], 4, DT,
                     lambda j: lo3(it * 4 + j, it * 4 + j))
            steps(norm(UB["k2"] - 2, rs3, 4))
            dve.wait_ge(sum_ready, 5)
            steps(V.scalar_tensor_tensor(acc2, psum[(UB["k2"] - 1) % 4][:, 0:S], 1.0 / D, rs3, ALU.mult, ALU.mult))
            dve.sem_inc(z_ready, 1)
            steps(V.tensor_tensor(acc2, acc2, rs3, ALU.mult))
            V.tensor_scalar(acc2, acc2, EPS, None, ALU.add).then_inc(var_ready, 1)
            steps(rsqrt(rs[:, :], acc2, 5))
            V.tensor_tensor(rs[:, :], rs[:, :], rs3, ALU.mult).then_inc(rs_ready, 1)
            dve.wait_ge(rs_ready, 5)
            V.tensor_scalar(rs2, rs[:, :], float(HD) ** -0.5, None, ALU.mult).then_inc(rs_ready, 1)
            columns_of_rs(2)
            body(PB["k2"], PB["k2"], UB["k2"], UB["k2"], ZB["k2"], ZB["k2"], 4, DT)
            values(PB["v2"], UB["v2"], 0)

            def normed(t):
                V.scalar_tensor_tensor(tile(x, t), tile(x, t), gain("g_fin", t), rs3, ALU.mult, ALU.mult).then_inc(xn_ready, 1)
            with dve.Fori(0, 4) as it:
                body(it * 8 + PB["q2"], PB["q2"], it * 4 + UB["q2"], UB["q2"], it * 4 + ZB["q2"], ZB["q2"], 4, DT,
                     lambda j: normed(it * 4 + j))
            attention("swa")
            with dve.Fori(0, 4) as it:
                body(it * 8 + PB["wo2"], PB["wo2"], it * 4 + UB["wo2"], UB["wo2"], it * 4 + ZB["wo2"], ZB["wo2"], 4, DT)
            norm(UB["up0"] - 2, rs[:, :], 6).then_inc(rs_ready, 1)
            dve.wait_ge(rs_ready, 7)
            dve.wait_ge(xn_ready, DT)
            lo4 = norm_lo(A, "g2", post_hi, a4_ready)
            with dve.Fori(0, 4) as it:
                for j in range(4):
                    V.scalar_tensor_tensor(tA[:, j, :], tile(y, it * 4 + j), gain("g1", it * 4 + j), rs[:, :], ALU.mult,
                                           ALU.mult).then_inc(post_t, 1)
                for j in range(4):
                    lo4(it * 4 + j, it * 4 + j)
            norm(UB["up0"] - 1, rs[:, :], 7).then_inc(rs_ready, 1)

            def conv(i, slot):
                dve.wait_ge(up_c0, i + 1)
                w = [par[:, ds(i * 3 + (PO["conv"][0] + k), 1)] for k in range(3)]
                V.scalar_tensor_tensor(tA[:, slot, :], ub[:, slot, 1:S + 1], w[1], c0[:, slot % 2, :], ALU.mult,
                                       ALU.add).then_inc(up_step, 1)
                dve.wait_ge(up_step, i + 1)
                V.scalar_tensor_tensor(tB[:, slot, :], ub[:, slot, 2:S + 2], w[2], tA[:, slot, :], ALU.mult,
                                       ALU.add).then_inc(up_conv, 1)

            t0 = 0
            for c, n in enumerate(CHUNKS2):
                up, dn = f"up{c}", f"dn{c}"
                with dve.Fori(0, n // 2) as it:
                    body(it * 8 + PB[up], PB[up], it * 4 + UB[up], UB[up], it * 4 + ZB[up], ZB[up], 4, DT,
                         lambda j: conv(it * 4 + (2 * t0 + j), j))
                if n == CH:
                    with dve.Fori(0, 4) as it:
                        body(it * 8 + PB[dn], PB[dn], it * 4 + UB[dn], UB[dn], it * 4 + ZB[dn], ZB[dn], 4, n)
                else:
                    for it in range(2):
                        body(it * n + PB[dn], PB[dn], it * 8 + UB[dn], UB[dn], it * 8 + ZB[dn], ZB[dn], 8, n, last=(it == 1))
                t0 += n
            norm(UB["end"], rs[:, :], 8).then_inc(rs_ready, 1)
            dve.wait_ge(rs_ready, 9)
            with dve.Fori(0, 4) as it:
                for j in range(4):
                    V.scalar_tensor_tensor(tile(y, it * 4 + j), tile(y, it * 4 + j), gain("g3", it * 4 + j), rs[:, :],
                                           ALU.mult, ALU.mult).then_inc(fin_t, 1)

        @block.scalar
        def _(act):
            C = nc.scalar

            def split_hi(i, s, lap):
                act.wait_ge(raw_landed[s], lap)
                act.wait_ge(piece_used, i + 1)
                C.copy(whi[:, s, :], raw[:, s, :]).then_inc(hi_ready, 1)

            def split(p, p0, i, per, it):
                q = p0 + i
                split_hi(p + i, q % SLOTS, (it * (per // SLOTS) + (q // SLOTS + 1)) * 16)

            def body(p, p0, it, n, K, each=None, late=None, last=False):
                at = ends(n, K)
                per = n * K // BLK
                waiting = []
                for i in range(per):
                    if not last or i + LEAD < per:
                        split(p, p0, i + LEAD, per, it)
                    while waiting:
                        late(waiting.pop(0))
                    for j in at.get(i, []):
                        if each:
                            each(j)
                        if late:
                            waiting.append(j)
                while waiting:
                    late(waiting.pop(0))

            def norm_hi(name, src_sem, src0, hi_sem, sq_sem):
                def each(t, i, j):
                    act.wait_ge(src_sem, i + src0 + 1)
                    C.activation(part(A, t, 0), tile(x, t), ACT.Copy, scale=gain(name, t)).then_inc(hi_sem, 1)
                    C.activation(sq[:, j, :], tile(x, t), ACT.Square).then_inc(sq_sem, 1)
                return each

            def attention(kind):
                sm = att[kind]
                nsa = kind == "nsa"
                act.sem_inc(sm["pt_act"], 1)
                with act.Fori(0, KVG) as it:
                    if not nsa:
                        rows = bias_rows.ap()[ds(it * 8, 8), P - 1:P - 1 + P * (RB - 1)]
                        act.dma_start(bias[:, :, :], rows.rearrange("e (q i) -> q e i", q=P)[:, :, 0:2 * P]).then_inc(sm["bias_in"], 16)
                    C.copy(qs[:, :, :], y[:, ds(it * 4, 4), :]).then_inc(sm["q_staged"], 1)
                    for t in range(QT):
                        c = slice(8 * t, 8 * t + 8)
                        act.wait_ge(sm["shift"], it * 2 + (t + 1))
                        for e in range(8):
                            i = 8 * t + e
                            C.activation(Smq[t][:, e, :], Smq[t][:, e, :], ACT.Exp, bias=nmx[:, i:i + 1],
                                         accum_out=sums[:, i:i + 1]).then_inc(sm["exp"], 1)
                        if not nsa:
                            act.wait_ge(sm["sinkdiff"], it * 2 + (t + 1))
                            C.activation(esk[:, c], esk[:, c], ACT.Exp).then_inc(sm["sinkexp"], 1)
                    for n, (t, half, kt) in enumerate([(0, 0, 0), (0, 1, 0), (1, 0, 0), (1, 0, 1), (1, 1, 0), (1, 1, 1)]):
                        if n % 2 == 0:
                            act.wait_ge(sm["turned"], it * 6 + (n + 1))
                            C.copy(PT[:, kt, 4 * half:4 * half + 4, :],
                                   psum[6 + n % 2][:, :].rearrange("p (e q) -> p e q", e=4)).then_inc(sm["pt_act"], 1)
                        if n in (1, 5):
                            tok = slice(t * P, t * P + P)
                            act.wait_ge(sm["o_done"], it * 2 + (t + 1))
                            for rows, bank in o_parts(nsa, t):
                                last = C.copy(H[rows, ds(it * 4, 4), 0, tok], bank[rows, :].rearrange("p (r q) -> p r q", r=4))
                            last.then_inc(sm["o_hi"], 1)

            def root(n, dst, var=acc[:, :]):
                act.wait_ge(var_ready, n)
                C.activation(dst, var, ACT.Sqrt).then_inc(root_ready, 1)

            act.dma_start(bflat[0:NBUCK, 0:NSETUP], setup).then_inc(in_s, 16)
            act.wait_ge(in_c, 32)
            for t in range(DT):
                if t % 4 == 0:
                    act.wait_ge(in_x, 64)
                C.activation(A[:, t, 0, :], x[:, t, :], ACT.Copy, scale=gain("g_mix", t)).then_inc(x0_hi, 1)
                C.activation(tile(y, t), x[:, t, :], ACT.Square).then_inc(x0_sq, 1)
                if t % 4 == 3 and t // 4 < LEAD:
                    split_hi(t // 4, t // 4, 16)
            act.wait_ge(table_row, 1)
            act.dma_start(bias_rows.ap().rearrange("h (q i) -> h q i", q=P),
                          bflat[0:NBUCK, 1024:1024 + RB].unsqueeze(1).to_broadcast([SWA_HEADS, P, RB])).then_inc(rows_out, 16)
            root(1, rs[:, :])
            for st in ("kv", "q"):
                with act.Fori(0, 4) as it:
                    body(it * 8 + PB[st], PB[st], it, 4, DT)
            for b in range(2):
                act.wait_ge(blk_step, 8 * b + 8)
                C.copy(blks[:, b, :, 0, :], blkf[:, :, :, :].rearrange("p l g n -> p l (g n)")).then_inc(blk_hi, 1)
            for i in range(16):
                split(PB["v"], PB["v"], i + LEAD, 0, 0)

            def csilu(b):
                act.wait_ge(z_used, 4 + ZB["cmp"] + b + 1)
                C.activation(csig[:, b * 64:b * 64 + NB], zr[:, b, 0:NB], ACT.Sigmoid).then_inc(csig_ready, 1)
                act.wait_ge(ch_ready, b + 1)
                act.wait_ge(pad_zero, 1)
                C.copy(pA[:, b, 0, 0:P].rearrange("p (g n) -> p g n", g=KVG)[:, :, 0:NCMP],
                       ch[:, b * 64:b * 64 + NB].rearrange("p (g n) -> p g n", g=KVG)).then_inc(ch_hi, 1)
            body(PB["cmp"], PB["cmp"], 0, 2, CL, csilu)
            split(PB["misc"], PB["misc"], LEAD, 0, 0)
            for t in range(QT):
                act.wait_ge(z_ready, 4 + UB["misc"] + t + 1)
                C.activation(gts[:, t, :], gts[:, t, :], ACT.Sigmoid).then_inc(gates_ready, 1)
            for t in range(QT):
                act.wait_ge(c_shift, t + 1)
                C.activation(cprob[:, t, :, :], cprob[:, t, :, :], ACT.Exp).then_inc(c_exp, 1)
            act.wait_ge(z_used, 4 + ZB["wo"])
            attention("nsa")
            act.dma_start(tC[:, 0:2, :], pT).then_inc(in_p, 16)

            h1 = norm_hi("g_ffn", z_used, 4 + ZB["wo"], wo_hi, wo_sq)
            with act.Fori(0, 4) as it:
                body(it * 8 + PB["wo"], PB["wo"], it, 4, DT, lambda j: h1(it * 4 + j, it * 4 + j, j))

            root(2, rs[:, :])
            act.wait_ge(in_p, 16)
            for k in range(2):
                C.copy(pA[:, k, 0, :], tC[:, k, :]).then_inc(p_hi, 1)

            def chunk(c, prep):
                def hidden(it, j):
                    i = c * 16 + it * 4 + j
                    act.wait_ge(z_used, c * 32 + it * 4 + (4 + ZB["ff0"] + j + 1))
                    C.activation(tA[:, j, :], zr[:, j, :], ACT.Relu).then_inc(ff_relu, 1)
                    act.wait_ge(ff_relu, i + 1)
                    C.activation(part(H, it * 4 + j, 0), tA[:, j, :], ACT.Square).then_inc(ff_hi, 1)
                with act.Fori(0, 4) as it:
                    body(c * 64 + it * 8 + PB["ff0"], PB["ff0"], c * 8 + it, 4, DT, lambda j: hidden(it, j))
                with act.Fori(0, 4) as it:
                    body(c * 64 + it * 8 + PB["fd0"], PB["fd0"], c * 8 + it, 4, CH,
                         (lambda j: prep(it * 4 + j, it * 4 + j, j)) if prep else None)
            with act.Fori(0, FF_CHUNKS - 1) as c:
                chunk(c, None)
            last = f"fd{FF_CHUNKS - 1}"
            chunk(FF_CHUNKS - 1, norm_hi("g_ple", z_used, 4 + ZB[last], fd_hi, fd_sq))
            body(PB["proj"], PB["proj"], 0, DT, 2)

            def gated(t, i, j):
                act.wait_ge(z_used, i + (4 + ZB["gate"] + 1))
                C.activation(tA[:, j, :], zr[:, j, :], ACT.Sigmoid).then_inc(ple_sig, 1)
                act.wait_ge(ple_x, i + 1)
                C.activation(part(H, t, 0), tile(x, t), ACT.Copy, scale=gg[:, ds(t, 1)]).then_inc(ple_hi, 1)
                C.activation(sq[:, j, :], tile(x, t), ACT.Square).then_inc(ple_sq, 1)
                C.activation(sq2[:, j, :], tile(x, t), ACT.Square, scale=gain("g_fin", t)).then_inc(ple_sq, 1)
            root(3, rs[:, :])
            act.wait_ge(gg_ready, 1)
            with act.Fori(0, 4) as it:
                body(it * 8 + PB["gate"], PB["gate"], it, 4, DT, lambda j: gated(it * 4 + j, it * 4 + j, j))
            root(4, rs3)
            root(5, rs[:, :], acc2)
            body(PB["k2"], PB["k2"], 0, 4, DT)
            for i in range(8):
                split(PB["v2"], PB["v2"], i + LEAD, 0, 0)
            with act.Fori(0, 4) as it:
                body(it * 8 + PB["q2"], PB["q2"], it, 4, DT)
            act.wait_ge(z_used, 4 + ZB["wo2"])
            act.wait_ge(rows_out, 16)
            attention("swa")

            def squares(src_sem, n0, sq_sem):
                def each(t, i, j):
                    act.wait_ge(src_sem, i + (n0 + 1))
                    C.activation(sq[:, j, :], tile(y, t), ACT.Square).then_inc(sq_sem, 1)
                return each
            s2 = squares(z_used, 4 + ZB["wo2"], wo2_sq)
            with act.Fori(0, 4) as it:
                body(it * 8 + PB["wo2"], PB["wo2"], it, 4, DT, lambda j: s2(it * 4 + j, it * 4 + j, j))
            root(6, rs[:, :])
            h4 = norm_hi("g2", post_x, 0, post_hi, post_sq)
            with act.Fori(0, 4) as it:
                for j in range(4):
                    h4(it * 4 + j, it * 4 + j, j)
            root(7, rs[:, :])

            t0 = 0
            for c, n in enumerate(CHUNKS2):
                up, dn = f"up{c}", f"dn{c}"

                def tap(i, iz, j):
                    act.wait_ge(z_used, iz + 1)
                    C.activation(c0[:, j % 2, :], ub[:, j, 0:S], ACT.Copy,
                                 scale=par[:, ds(i * 3 + PO["conv"][0], 1)]).then_inc(up_c0, 1)

                def tail(it, j):
                    if j % 2 == 0:
                        act.wait_ge(up_conv, it * 4 + (2 * t0 + j + 1))
                        C.activation(tC[:, j, :], tB[:, j, :], ACT.Sigmoid).then_inc(up_sig, 1)
                    else:
                        act.wait_ge(up_h, it * 2 + (t0 + j // 2 + 1))
                        C.copy(part(H, it * 2 + j // 2, 0), zr[:, j, :]).then_inc(up_hi, 1)
                with act.Fori(0, n // 2) as it:
                    body(it * 8 + PB[up], PB[up], it, 4, DT,
                         lambda j: tap(it * 4 + (2 * t0 + j), it * 4 + (4 + ZB[up] + j), j), lambda j: tail(it, j))
                if n == CH:
                    with act.Fori(0, 4) as it:
                        body(it * 8 + PB[dn], PB[dn], it, 4, n)
                else:
                    s3 = squares(z_used, 4 + ZB[dn], dn_sq)
                    for it in range(2):
                        body(it * n + PB[dn], PB[dn], it, 8, n, lambda j: s3(it * 8 + j, it * 8 + j, j % 4), last=(it == 1))
                t0 += n
            root(8, rs[:, :])

        @block.gpsimd
        def _(pool):
            G = nc.gpsimd
            pool.sem_inc(z_used, 4)
            G.memset(ones[:, :], 1.0).then_inc(ones_set, 1)

            def add_acc(dst, src, n):
                pool.wait_ge(acc_step, n)
                G.tensor_tensor(dst, dst, src, ALU.add).then_inc(acc_step, 1)

            def take(u, z0, j, fn):
                pool.wait_ge(z_ready, u + (4 + j + 1))
                fn(z[:, (z0 + j) % 4, :]).then_inc(z_used, 1)

            def mul(dst, by):
                return lambda zz: G.tensor_tensor(dst, zz, by, ALU.mult)

            pool.sem_inc(acc_step, 1)
            pool.wait_ge(x0_sq, 2)
            G.tensor_tensor(acc[:, :], y[:, 0, :], y[:, 1, :], ALU.add).then_inc(acc_step, 1)
            for t in range(2, DT):
                pool.wait_ge(x0_sq, t + 1)
                add_acc(acc[:, :], y[:, t, :], t)
            pool.wait_ge(rs_ready, 2)
            for b in range(2):
                with pool.Fori(0, 2) as it:
                    for j in range(4):
                        dst = kvc if b == 0 else kT
                        take(it * 4 + (UB["kv"] + 8 * b), ZB["kv"], j,
                             mul(dst[:, ds(it, 1), j, :].rearrange("p a t -> p (a t)"), rs[:, :]))
            with pool.Fori(0, 4) as it:
                for j in range(4):
                    take(it * 4 + UB["q"], ZB["q"], j, mul(tile(y, it * 4 + j), rs2))
            pool.wait_ge(rows_out, 16)
            G.memset(pA[:, :, :, :].rearrange("p a b c -> p (a b c)").bitcast(F32), 0.0).then_inc(pad_zero, 1)
            for b in range(2):
                take(UB["cmp"], ZB["cmp"], b, lambda zz: G.tensor_copy(zr[:, b, 0:NB], zz[:, 0:NB]))
                pool.wait_ge(csig_ready, b + 1)
                G.tensor_tensor(ch[:, b * 64:b * 64 + NB], zr[:, b, 0:NB], csig[:, b * 64:b * 64 + NB], ALU.mult).then_inc(ch_ready, 1)
            G.memset(vczall[:, :, :], 0.0).then_inc(vcz_zero, 1)
            G.memset(cpad[:, :, :, :, :].rearrange("p t r g n -> p (t r g n)"), 0.0).then_inc(cpad_zero, 1)

            def attention(kind):
                sm = att[kind]
                nsa = kind == "nsa"
                with pool.Fori(0, KVG) as it:
                    pool.wait_ge(sm["o_ready"], it * 2 + 2)
                    if nsa:
                        G.tensor_copy(kst[:, :, :], kT[:, :, ds(it, 1), :].rearrange("p b a t -> p b (a t)")).then_inc(sm["kv_staged"], 1)
                        G.tensor_copy(vst[:, :, :], vN[:, :, ds(it * P, P)]).then_inc(sm["kv_staged"], 1)
                        G.tensor_copy(vcz, tile(vczall, it)).then_inc(sm["kv_staged"], 1)
                    else:
                        G.tensor_copy(kst[:, 0, :], kT[:, 0, ds(it, 1), :].rearrange("p a t -> p (a t)")).then_inc(sm["kv_staged"], 1)
                        G.tensor_copy(vst[:, 0:QT, :], vN[:, 0:QT, ds(it * P, P)]).then_inc(sm["kv_staged"], 1)
                    for t in range(QT):
                        pool.wait_ge(sm["coef"], it * 2 + (t + 1))
                        for half in range(2):
                            e = slice(4 * half, 4 * half + 4)
                            c = coef[:, 8 * t + 4 * half:8 * t + 4 * half + 4].unsqueeze(2).to_broadcast([P, 4, (t + 1) * P])
                            G.tensor_tensor(Smq[t][:, e, :], Smq[t][:, e, :], c, ALU.mult).then_inc(sm["scaled"], 1)

            pool.wait_ge(vcmp_ready, KVG)
            attention("nsa")

            def residual(st, c, it, j):
                take(c * 32 + it * 4 + UB[st], ZB[st], j,
                     lambda zz: G.tensor_tensor(tile(x, it * 4 + j), tile(x, it * 4 + j), zz, ALU.add))

            G.memset(acc[:, :], 0.0).then_inc(acc_zero, 1)
            pool.wait_ge(acc_zero, 1)
            with pool.Fori(0, 4) as it:
                for j in range(4):
                    residual("wo", 0, it, j)
                    pool.wait_ge(wo_sq, it * 4 + (j + 1))
                    add_acc(acc[:, :], sq[:, j, :], it * 4 + (ACC0["ff0"] + j))
            pool.wait_ge(rs_ready, 3)

            def chunk(c, prep):
                with pool.Fori(0, 4) as it:
                    for j in range(4):
                        i = c * 16 + it * 4 + j
                        take(c * 32 + it * 4 + UB["ff0"], ZB["ff0"], j, mul(zr[:, j, :], rs[:, :]))
                        pool.wait_ge(ff_relu, i + 1)
                        G.tensor_tensor(tB[:, j, :], tA[:, j, :], tA[:, j, :], ALU.mult).then_inc(ff_step, 1)
                        pool.wait_ge(ff_step, i + 1)
                        pool.wait_ge(ff_hi, i + 1)
                        G.tensor_tensor(part(H, it * 4 + j, 1), tB[:, j, :], part(H, it * 4 + j, 0).bitcast(F32),
                                        ALU.subtract).then_inc(ff_ready, 1)
                with pool.Fori(0, 4) as it:
                    for j in range(4):
                        residual("fd0", c, it, j)
                        if prep:
                            pool.wait_ge(fd_sq, it * 4 + (j + 1))
                            add_acc(acc[:, :], sq[:, j, :], it * 4 + (ACC0["gate"] + j))
            with pool.Fori(0, FF_CHUNKS - 1) as c:
                chunk(c, False)
            G.memset(acc[:, :], 0.0).then_inc(acc_zero, 1)
            pool.wait_ge(acc_zero, 2)
            chunk(FF_CHUNKS - 1, True)
            for j in range(DT):
                take(UB["proj"], ZB["proj"], j, lambda zz: G.tensor_copy(y[:, j, :], zz))
            pool.wait_ge(rs_ready, 4)
            G.memset(acc[:, :], 0.0).then_inc(acc_zero, 1)
            G.memset(acc2, 0.0).then_inc(acc_zero, 1)
            pool.wait_ge(acc_zero, 4)
            with pool.Fori(0, 4) as it:
                for j in range(4):
                    t = it * 4 + j
                    take(it * 4 + UB["gate"], ZB["gate"], j, mul(zr[:, j, :], rs[:, :]))
                    pool.wait_ge(ple_sig, t + 1)
                    G.tensor_tensor(tB[:, j, :], tA[:, j, :], tile(y, t), ALU.mult).then_inc(ple_step, 1)
                    pool.wait_ge(ple_step, t + 1)
                    G.tensor_tensor(tile(x, t), tile(x, t), tB[:, j, :], ALU.add).then_inc(ple_x, 1)
                    pool.wait_ge(ple_sq, it * 8 + (2 * j + 2))
                    add_acc(acc[:, :], sq[:, j, :], it * 8 + (ACC0["k2"] + 2 * j))
                    add_acc(acc2, sq2[:, j, :], it * 8 + (ACC0["k2"] + 2 * j + 1))
            pool.wait_ge(rs_ready, 6)
            for j in range(4):
                take(UB["k2"], ZB["k2"], j, mul(kT[:, 0, j, :], rs[:, :]))
            with pool.Fori(0, 4) as it:
                for j in range(4):
                    take(it * 4 + UB["q2"], ZB["q2"], j, mul(tile(y, it * 4 + j), rs2))
            attention("swa")
            G.memset(acc[:, :], 0.0).then_inc(acc_zero, 1)
            pool.wait_ge(acc_zero, 5)
            with pool.Fori(0, 4) as it:
                for j in range(4):
                    take(it * 4 + UB["wo2"], ZB["wo2"], j, lambda zz: G.tensor_copy(tile(y, it * 4 + j), zz))
                    pool.wait_ge(wo2_sq, it * 4 + (j + 1))
                    add_acc(acc[:, :], sq[:, j, :], it * 4 + (ACC0["post"] + j))
            pool.wait_ge(rs_ready, 7)
            G.memset(acc[:, :], 0.0).then_inc(acc_zero, 1)
            pool.wait_ge(acc_zero, 6)
            with pool.Fori(0, 4) as it:
                for j in range(4):
                    t = it * 4 + j
                    pool.wait_ge(post_t, t + 1)
                    G.tensor_tensor(tile(x, t), tile(x, t), tA[:, j, :], ALU.add).then_inc(post_x, 1)
                    pool.wait_ge(post_sq, t + 1)
                    add_acc(acc[:, :], sq[:, j, :], it * 4 + (ACC0["up0"] + j))
            G.memset(ub[:, :, 0:2], 0.0).then_inc(acc_zero, 1)
            pool.wait_ge(rs_ready, 8)
            G.memset(acc[:, :], 0.0).then_inc(acc_zero, 1)
            pool.wait_ge(acc_zero, 8)
            t0 = 0
            for c, n in enumerate(CHUNKS2):
                up, dn = f"up{c}", f"dn{c}"
                with pool.Fori(0, n // 2) as it:
                    for j in range(4):
                        take(it * 4 + UB[up], ZB[up], j, mul(ub[:, j, 2:S + 2], rs[:, :]))
                        i = it * 2 + (t0 + j // 2)
                        if j % 2 == 0:
                            pool.wait_ge(up_sig, i + 1)
                            G.tensor_tensor(tC[:, j, :], tC[:, j, :], tB[:, j, :], ALU.mult).then_inc(up_gated, 1)
                        else:
                            pool.wait_ge(up_conv, i * 2 + 2)
                            pool.wait_ge(up_gated, i + 1)
                            G.tensor_tensor(zr[:, j, :], tC[:, j - 1, :], tB[:, j, :], ALU.mult).then_inc(up_h, 1)
                            pool.wait_ge(up_h, i + 1)
                            pool.wait_ge(up_hi, i + 1)
                            G.tensor_tensor(part(H, it * 2 + j // 2, 1), zr[:, j, :], part(H, it * 2 + j // 2, 0).bitcast(F32),
                                            ALU.subtract).then_inc(up_ready, 1)
                if n == CH:
                    with pool.Fori(0, 4) as it:
                        for j in range(4):
                            t = it * 4 + j
                            take(it * 4 + UB[dn], ZB[dn], j,
                                 (lambda zz: G.tensor_copy(tile(y, t), zz)) if c == 0 else
                                 (lambda zz: G.tensor_tensor(tile(y, t), tile(y, t), zz, ALU.add)))
                else:
                    for j in range(DT):
                        take(UB[dn], ZB[dn], j, lambda zz: G.tensor_tensor(y[:, j, :], y[:, j, :], zz, ALU.add))
                        pool.wait_ge(dn_sq, j + 1)
                        add_acc(acc[:, :], sq[:, j % 4, :], ACC0["end"] + j)
                t0 += n
            with pool.Fori(0, 4) as it:
                for j in range(4):
                    t = it * 4 + j
                    pool.wait_ge(fin_t, t + 1)
                    G.tensor_tensor(tile(x, t), tile(x, t), tile(y, t), ALU.add).then_inc(fin_x, 1)


def tiled(w):
    k, n = w.shape
    return w.reshape(k // P, P, n // P, P).transpose(2, 0, 1, 3).reshape(-1, P, P)


def kernel(**inp):
    import concourse.bacc as bacc
    from concourse import mybir
    from concourse.bass_utils import run_bass_kernel_spmd

    f = np.float32
    a = {k: np.asarray(v) for k, v in inp.items()}

    w_in = a["nsa_w_in"][0]
    kvw = KVG * P
    cut = [D + i * kvw for i in range(7)]
    kc, vc, ks, vs, kw, vw = (w_in[:, cut[i]:cut[i + 1]] for i in range(6))

    def rows(w):
        k, n = w.shape
        return w.reshape(k // P, P, n // P, P).transpose(0, 2, 1, 3).reshape(-1, P, P)

    gates = w_in[:, cut[6]:].reshape(DT, P, KVG, HPG, 3).transpose(1, 0, 2, 4, 3).reshape(P, DT * 48)
    misc = np.concatenate([gates, a["nsa_cmp_w2_k"][0], a["nsa_cmp_w2_v"][0]], axis=1)
    stream = [tiled(kc), tiled(vc), tiled(ks), tiled(kw), tiled(w_in[:, :D]), rows(vs), rows(vw),
              tiled(a["nsa_cmp_w1_k"][0]), tiled(a["nsa_cmp_w1_v"][0]),
              misc.reshape(P, BLK, P).transpose(1, 0, 2), tiled(a["nsa_w_out"][0])]
    for c in range(FF_CHUNKS):
        h = slice(c * CH * P, (c + 1) * CH * P)
        stream += [tiled(a["ffn_w1"][0][:, h]), tiled(a["ffn_w2"][0][h])]
    stream += [tiled(a["ple_w_proj"][0]), tiled(a["ple_w_gate"][0])]
    swa = a["swa_w_in_2"][0]
    kv2 = SWA_KV * HD
    order = np.arange(SWA_HEADS * HD).reshape(PAIRS, 2, HPG, HD).transpose(0, 2, 1, 3).reshape(-1)
    stream += [tiled(swa[:, D:D + kv2]), rows(swa[:, D + kv2:]), tiled(swa[:, :D][:, order]), tiled(a["swa_w_out_2"][0][order])]
    up, down = a["ffn_w_up_2"][0], a["ffn_w_down_2"][0]
    both = tiled(up).reshape(2, FF2_T, DT, P, P).transpose(1, 0, 2, 3, 4)
    t0 = 0
    for n in CHUNKS2:
        stream += [both[t0:t0 + n].reshape(-1, P, P), tiled(down[t0 * P:(t0 + n) * P])]
        t0 += n
    wstream = np.ascontiguousarray(np.concatenate(stream).reshape(NPIECE, BLK, P, P).transpose(0, 2, 1, 3)).reshape(NPIECE, P, PW)

    q = np.arange(P)
    causal = np.where(q[None, :] <= q[:, None], 0, NEG)
    tok = np.arange(S).reshape(QT, P, 1)
    n = np.arange(CS)
    valid = (n * CS + CL - 1 <= tok) & (n < NCMP)
    consts = np.concatenate([np.eye(P), np.zeros((P, P)), causal, np.where(valid, 0, NEG).transpose(1, 0, 2).reshape(P, -1),
                             valid.transpose(1, 0, 2).reshape(P, -1)], axis=1).astype(f)
    dist = 2 * P - 1 - np.arange(RB)
    near = np.clip(dist, 1, None)
    exact = NBUCK // 2
    far = np.minimum(exact + (np.log(near / exact) / np.log(MAXD / exact) * (NBUCK - exact)).astype(int), NBUCK - 1)
    bucket = np.where(dist < exact, np.maximum(dist, 0), far)
    onehot = (bucket[None, :] == np.arange(NBUCK)[:, None]).astype(f)
    band = np.broadcast_to(np.where((dist >= 0) & (dist < WIN), 0, NEG), (SWA_HEADS, RB)).astype(f)
    setup = np.concatenate([onehot, band, a["rel_bias_table_2"]], axis=1)

    def col(g):
        return g.reshape(-1, P).T

    conv = a["ffn_conv_2"][0].reshape(3, 2, FF2_T, P).transpose(3, 2, 1, 0).reshape(P, -1)
    g2 = a["norm_g_2"][0]
    params = np.concatenate([col(a["norm_mix"][0]), col(a["norm_ffn"][0]), col(a["norm_ple"][0]), col(a["norm_final"]),
                             col(g2[0]), col(g2[1]), col(g2[2]), col(g2[3]), conv, a["nsa_cmp_pos_k"][0].T,
                             a["nsa_cmp_pos_v"][0].T, np.broadcast_to(a["swa_sinks_2"][0], (P, SWA_HEADS))], axis=1)
    arrays = {
        "xT": a["x"][0].T.reshape(DT, P, S).transpose(1, 0, 2),
        "pT": a["p"][0, 0].T.reshape(2, P, S).transpose(1, 0, 2),
        "wstream": wstream, "consts": consts, "setup": setup, "params": params,
    }
    arrays = {k: np.ascontiguousarray(v) for k, v in arrays.items()}

    nc = bacc.Bacc("TRN2", target_bir_lowering=False, num_devices=1)
    F32 = mybir.dt.float32
    aps = [nc.dram_tensor(k, v.shape, F32, kind="ExternalInput").ap() for k, v in arrays.items()]
    out = nc.dram_tensor("out", (P, DT, S), F32, kind="ExternalOutput").ap()
    program(nc, *aps, out)
    r = run_bass_kernel_spmd(nc, [arrays], core_ids=[0])
    return np.ascontiguousarray(r.results[0]["out"].transpose(2, 1, 0)).reshape(1, S, D)
```

```python
from contextlib import ExitStack

import numpy as np

P = 128
S = 256
D = 2048
DT = D // P
QT = S // P
EPS = 1e-6
NEG = -1e30

HEADS, KVG, HPG = 16, 4, 4
CL, CS = 32, 16
NCMP = (S - CL) // CS + 1
NPAD = 32
D_FF = 8192
CH = 16
FF_CHUNKS = D_FF // P // CH
D_PLE = 256
SWA_HEADS, SWA_KV, HD = 32, 8, 64
WIN = 128
PAIRS = SWA_KV // 2
D_FF2 = 5632
FF2_T = D_FF2 // P
CHUNKS2 = [16, 16, 12]
NBUCK, MAXD = 32, 128
RB = 384
FIRST_SPLITS = [1, 4, 7, 10]
POST_SPLITS = [7, 10, 13, 16]
SLOTS = 4
LEAD = 3
AHEAD = LEAD + 2
BLK = 8
PW = BLK * P

STAGES = [("kv", 16, 16), ("q", 16, 16), ("v", 4, 16), ("cmp", 2, 32), ("misc", 4, 2), ("wo", 16, 16)]
for _c in range(FF_CHUNKS):
    STAGES += [(f"ff{_c}", CH, 16), (f"fd{_c}", 16, CH)]
STAGES += [("proj", 16, 2), ("gate", 16, 16), ("k2", 4, 16), ("v2", 2, 16), ("q2", 16, 16), ("wo2", 16, 16)]
for _c, _n in enumerate(CHUNKS2):
    STAGES += [(f"up{_c}", 2 * _n, 16), (f"dn{_c}", 16, _n)]

PB, UB, ZB = {}, {}, {}
NZ = {"v": 0, "v2": 0, "misc": 0}
_p = _u = _z = 0
for _name, _n, _k in STAGES:
    PB[_name], UB[_name], ZB[_name] = _p, _u, _z
    _blocks = _n * _k * (2 if _name in ("v", "v2") else 1)
    if _name in ("v", "v2"):
        _blocks = _n // 2 * 4 * 16
    _p += 1 if _name == "misc" else _blocks // BLK
    _u += _n
    _z += NZ.get(_name, _n)
NPIECE = _p
UB["end"] = _u


def columns(widths):
    at, out = 0, {}
    for name, width in widths:
        out[name] = (at, at + width)
        at += width
    return out, at


CO, NCONST = columns([("ident", P), ("mask", 2 * P), ("cmask", QT * CS), ("cvalid", QT * CS)])
SO, NSETUP = columns([("onehot", RB), ("band", RB), ("table", SWA_HEADS)])
PO, NPAR = columns([("g_mix", DT), ("g_ffn", DT), ("g_ple", DT), ("g_fin", DT), ("g0", DT), ("g1", DT), ("g2", DT),
                    ("g3", DT), ("conv", 3 * 2 * FF2_T), ("pos_k", CL), ("pos_v", CL), ("sink", SWA_HEADS)])


def order(n, K):
    if not 8 < K <= 16:
        return [(j, k) for j in range(n) for k in range(K)]
    return [(j, k) for g in range(0, n, 4) for a, b in ((0, 4), (4, 8), (8, K)) for j in range(g, g + 4) for k in range(a, b)]


def ends(n, K):
    at = {}
    for b, (j, k) in enumerate(order(n, K)):
        if k == K - 1:
            at.setdefault(b // BLK, []).append(j)
    return at


class Steps:

    def __init__(self, eng, sem, base=0):
        self.eng, self.sem, self.n = eng, sem, base

    def __call__(self, ins):
        self.n = self.n + 1
        ins.then_inc(self.sem, 1)
        self.eng.wait_ge(self.sem, self.n)


def program(nc, xT, pT, wstream, consts, setup, params, out):
    import concourse.bass as bass
    from concourse import mybir

    F32, FR = mybir.dt.float32, mybir.dt.float32r
    ALU, ACT = mybir.AluOpType, mybir.ActivationFunctionType
    AX = mybir.AxisListType.X
    ds = bass.ds

    bias_rows = nc.dram_tensor("bias_rows", [SWA_HEADS, P * RB], F32)

    with ExitStack() as ctx:
        def sb(name, shape, dt=F32):
            return ctx.enter_context(nc.sbuf_tensor(name, shape, dt))

        def sem(name):
            return ctx.enter_context(nc.semaphore(name))

        raw = sb("raw", [P, SLOTS, PW])
        whi = sb("whi", [P, SLOTS, PW], FR)
        wlo = sb("wlo", [P, SLOTS, PW], FR)
        x = sb("x", [P, DT, S])
        A = sb("A", [P, DT, 2, S], FR)
        H = sb("H", [P, CH, 2, S], FR)
        pA = sb("pA", [P, 2, 2, S], FR)
        y = sb("y", [P, DT, S])
        kT = sb("kT", [P, 2, KVG, S])
        vN = sb("vN", [P, 2 * QT, 4 * P])
        qs = sb("qs", [P, HPG, S])
        kst = sb("kst", [P, 2, S])
        vst = sb("vst", [P, 2 * QT, P])
        Sm = sb("Sm", [P, 3 * 8 * P])
        PT = sb("PT", [P, QT, 8, P])
        bias = sb("bias", [P, 8, 2 * P])
        con = sb("con", [P, NCONST])
        par = sb("par", [P, NPAR])
        ones = sb("ones", [P, P])
        acc = sb("acc", [P, S])
        rs = sb("rs", [P, S])
        rcol = sb("rcol", [P, QT])
        gg = sb("gg", [P, DT])
        gts = sb("gts", [P, QT, 3 * HEADS])
        small = sb("small", [P, 6, 16])
        psum = [ctx.enter_context(nc.psum_tensor(f"bank{i}", [P, 512], F32)) for i in range(8)]

        z = qs
        bflat = bias[:, :, :].rearrange("p a b -> p (a b)")
        ptf = PT[:, :, :, :].rearrange("p a b c -> p (a b c)")

        def ring(flat, a, n=4, w=S):
            return flat[:, a:a + n * w].rearrange("p (n w) -> p n w", n=n)

        zr, sq = ring(bflat, 0), ring(bflat, 4 * S)
        tA, tB, tC = ring(Sm, 0), ring(Sm, 4 * S), ring(Sm, 8 * S)
        ub, c0 = ring(ptf, 0, 4, S + 4), ring(ptf, 4 * (S + 4), 2)
        sq2 = ring(ptf, 0)
        acc2, rs2, rs3 = tC[:, 0, :], tC[:, 1, :], tC[:, 2, :]
        csig, ch = tC[:, 3, 0:128], tC[:, 3, 128:256]
        pcT = bflat[:, 0:1024].rearrange("p (t r q) -> p t r q", t=QT, r=HPG)
        vczall = bflat[:, 1024:1536].rearrange("p (g d) -> p g d", g=KVG)
        vcz, kcmp = bflat[:, 1536:1664], bflat[:, 1664:1792]
        cs = bflat[:, 1792:1920].rearrange("p (a b) -> p a b", a=8)
        kvc = Sm[:, 0:2048].rearrange("p (b g t) -> p b g t", b=2, g=KVG)
        blkf = ptf[:, 0:CL * KVG * NCMP].rearrange("p (l g n) -> p l g n", l=CL, g=KVG)
        NB = KVG * NCMP
        blks = H[:, :, :, :].rearrange("p a b c -> p (a b c)")[:, 0:2 * CL * 2 * NB].rearrange(
            "p (b l h c) -> p b l h c", b=2, l=CL, h=2)
        cprob = Sm[:, 0:512].rearrange("p (t h n) -> p t h n", t=QT, h=HEADS)
        cpad = Sm[:, 1024:2048].rearrange("p (t r g n) -> p t r g n", t=QT, r=HPG, g=KVG)
        Smq = [Sm[:, 0:8 * P].rearrange("p (e k) -> p e k", e=8),
               Sm[:, 8 * P:24 * P].rearrange("p (e k) -> p e k", e=8)]
        mx, nmx, sums, esk, tot, coef = (small[:, i, :] for i in range(6))
        ident = con[:, CO["ident"][0]:CO["ident"][1]]
        mask = con[:, CO["mask"][0]:CO["mask"][1]]
        cmask = con[:, CO["cmask"][0]:CO["cmask"][1]].rearrange("p (t n) -> p t n", t=QT)
        cvalid = con[:, CO["cvalid"][0]:CO["cvalid"][1]].rearrange("p (t n) -> p t n", t=QT)

        def gain(name, t):
            return par[:, ds(PO[name][0] + t, 1)]

        def tile(buf, t):
            return buf[:, ds(t, 1), :].rearrange("p a b -> p (a b)")

        def part(buf, t, h):
            return buf[:, ds(t, 1), h, :].rearrange("p a b -> p (a b)")

        raw_landed = [sem(f"raw_landed{i}") for i in range(SLOTS)]
        hi_ready, lo_ready = sem("hi_ready"), sem("lo_ready")
        piece_used = sem("piece_used")
        z_ready = sem("z_ready")
        z_used = sem("z_used")
        in_x = [sem(f"in_x{i}") for i in range(4)]
        in_c, in_k, in_p, in_s = sem("in_c"), sem("in_k"), sem("in_p"), sem("in_s")
        ones_set, gg_ready, pad_zero = sem("ones_set"), sem("gg_ready"), sem("pad_zero")
        table_sum, table_row, rows_out = (sem(n) for n in ("table_sum", "table_row", "rows_out"))
        x0_hi, a0_ready, x0_sq = sem("x0_hi"), sem("a0_ready"), sem("x0_sq")
        p_hi, p_ready = sem("p_hi"), sem("p_ready")
        acc_step = sem("acc_step")
        acc_zero = sem("acc_zero")
        sum_ready, sum_step, var_ready, root_ready, rs_ready = (sem(n) for n in ("sum_ready", "sum_step", "var_ready", "root_ready", "rs_ready"))
        rs_turned, rcol_ready = sem("rs_turned"), sem("rcol_ready")
        blk_step, blk_hi, blk_ready = sem("blk_step"), sem("blk_hi"), sem("blk_ready")
        csig_ready, ch_ready, ch_hi, h1_ready = (sem(n) for n in ("csig_ready", "ch_ready", "ch_hi", "h1_ready"))
        gate_sum, gates_ready, kcmp_ready, vcmp_ready = (sem(n) for n in ("gate_sum", "gates_ready", "kcmp_ready", "vcmp_ready"))
        vcz_zero, cpad_zero, c_scores, c_step, c_shift, c_exp, cp_ready, c_turned, pcT_ready = (
            sem(n) for n in ("vcz_zero", "cpad_zero", "c_scores", "c_step", "c_shift", "c_exp", "cp_ready", "c_turned", "pcT_ready"))
        att = {k: {n: sem(f"{k}_{n}") for n in (
            "q_staged", "kv_staged", "scores", "max", "step", "shift", "sinkdiff", "exp", "sinkexp", "coef", "scaled",
            "turned", "pt_act", "pt_dve", "o_done", "o_hi", "o_ready", "bias_in")} for k in ("nsa", "swa")}
        wo_hi, wo_sq, a1_ready = sem("wo_hi"), sem("wo_sq"), sem("a1_ready")
        ff_relu, ff_hi, ff_step, ff_ready = sem("ff_relu"), sem("ff_hi"), sem("ff_step"), sem("ff_ready")
        fd_hi, fd_sq, a2_ready = sem("fd_hi"), sem("fd_sq"), sem("a2_ready")
        ple_sig, ple_step, ple_x, ple_hi, ple_sq, a3_ready = (sem(n) for n in ("ple_sig", "ple_step", "ple_x", "ple_hi", "ple_sq", "a3_ready"))
        xn_ready = sem("xn_ready")
        wo2_sq = sem("wo2_sq")
        post_t, post_x, post_hi, post_sq, a4_ready = (sem(n) for n in ("post_t", "post_x", "post_hi", "post_sq", "a4_ready"))
        up_c0, up_step, up_conv, up_sig, up_gated, up_h, up_hi, up_ready = (
            sem(n) for n in ("up_c0", "up_step", "up_conv", "up_sig", "up_gated", "up_h", "up_hi", "up_ready"))
        dn_sq = sem("dn_sq")
        fin_t, fin_x, out_done = sem("fin_t"), sem("fin_x"), sem("out_done")

        NORMS = ["kv", "ff0", "gate", "k2", "post", "up0", "end"]
        ACC0 = {n: DT * i for i, n in enumerate(NORMS)}
        ACC0.update({n: ACC0[n] + DT for n in ("post", "up0", "end")})
        NACC = {n: (2 * DT if n == "k2" else DT) for n in NORMS}
        NORM_AT = {"kv": 6, "ff0": 1, "gate": 1, "k2": 1, "up0": 4}

        def o_parts(nsa, t):
            if nsa:
                return [(slice(0, P), psum[t])]
            return [(slice(h * HD, h * HD + HD), psum[2 * t + h]) for h in range(2)]

        block = ctx.enter_context(nc.Block())

        @block.sync
        def _(sp):
            sp.dma_start(par[:, :], params).then_inc(in_c, 16)
            for i in range(4):
                sp.dma_start(x[:, 4 * i:4 * i + 4, :], xT[:, 4 * i:4 * i + 4, :]).then_inc(in_x[i], 16)
                sp.dma_start(raw[:, i, :], wstream[i]).then_inc(raw_landed[i], 16)
            sp.dma_start(con[:, :], consts).then_inc(in_k, 16)

            def load(i, s):
                sp.wait_ge(lo_ready, i - SLOTS + 1)
                sp.dma_start(raw[:, s, :], wstream[ds(i, 1)].rearrange("a p n -> p (a n)")).then_inc(raw_landed[s], 16)

            with sp.Fori(0, NPIECE // SLOTS - 1) as it:
                for j in range(SLOTS):
                    load(it * SLOTS + (SLOTS + j), j)
            for i in range(NPIECE // SLOTS * SLOTS, NPIECE):
                sp.wait_ge(lo_ready, i - SLOTS + 1)
                sp.dma_start(raw[:, i % SLOTS, :], wstream[i]).then_inc(raw_landed[i % SLOTS], 16)
            for i in range(4):
                sp.wait_ge(fin_x, 4 * i + 4)
                sp.dma_start(out[:, 4 * i:4 * i + 4, :], x[:, 4 * i:4 * i + 4, :]).then_inc(out_done, 16)
            sp.wait_ge(out_done, 64)

        @block.tensor
        def _(pe):
            pe.sem_inc(piece_used, SLOTS)

            def units(p, p0, u, u0, n, K, moving, ready=None, width=S, norm_at=None, then=None):
                for b, (j, k) in enumerate(order(n, K)):
                    s = (p0 + b // BLK) % SLOTS
                    if b % BLK == 0:
                        pe.wait_ge(lo_ready, p + (b // BLK + 1))
                    if k == 0:
                        pe.wait_ge(z_ready, u + (j + 1))
                    if ready and j == 0:
                        pe.wait_ge(*ready(k))
                    bank = psum[(u0 + j) % 4]
                    w = slice(b % BLK * P, b % BLK * P + P)
                    m = moving(j, k)

                    def lo():
                        return nc.tensor.matmul(bank[:, 0:width], wlo[:, s, w], m[:, 0, :], start=False, stop=False)
                    if k == K - 1:
                        lo()
                    last = nc.tensor.matmul(bank[:, 0:2 * width], whi[:, s, w], m, start=(k == 0), stop=(k == K - 1))
                    if k < K - 1:
                        last = lo()
                    if b % BLK == BLK - 1:
                        last.then_inc(piece_used, 1)
                        if b // BLK == norm_at:
                            then()

            def norm(name, bank=4, src=acc[:, :]):
                pe.wait_ge(acc_step, ACC0[name] + NACC[name])
                nc.tensor.matmul(psum[bank][:, 0:S], ones[:, :], src, start=True, stop=True).then_inc(sum_ready, 1)

            def turn_rs(i):
                pe.wait_ge(rs_ready, i)
                for t in range(QT):
                    last = nc.tensor.transpose(psum[6][:, t * P:t * P + P], rs[:, t * P:t * P + P], ident)
                last.then_inc(rs_turned, 1)

            def natural(p, u, src):
                for t in range(QT):
                    pe.wait_ge(z_ready, u + t + 1)
                for k in range(DT):
                    if k % 2 == 0:
                        pe.wait_ge(lo_ready, p + k // 2 + 1)
                    s, w = (p + k // 2) % SLOTS, slice(k % 2 * 512, k % 2 * 512 + 512)
                    for t in range(QT):
                        tok = slice(t * P, t * P + P)
                        bank = psum[(u + t) % 4]
                        nc.tensor.matmul(bank[:, :], src[:, k, 0, tok], whi[:, s, w], start=(k == 0), stop=False)
                        nc.tensor.matmul(bank[:, :], src[:, k, 0, tok], wlo[:, s, w], start=False, stop=False)
                        last = nc.tensor.matmul(bank[:, :], src[:, k, 1, tok], whi[:, s, w], start=False, stop=(k == DT - 1))
                    if k % 2 == 1:
                        last.then_inc(piece_used, 1)

            def attention(kind):
                sm = att[kind]
                nsa = kind == "nsa"
                with pe.Fori(0, KVG) as it:
                    pe.wait_ge(sm["q_staged"], it + 1)
                    pe.wait_ge(sm["kv_staged"], it * (3 if nsa else 2) + (3 if nsa else 2))
                    pe.wait_ge(sm["o_ready"], it * 2 + 2)
                    for t in range(QT):
                        nk = (t + 1) * P
                        for e in range(8):
                            if nsa:
                                lhs, rhs = qs[:, e % 4, t * P:t * P + P], kst[:, e // 4, 0:nk]
                            else:
                                h = slice(e // 4 * HD, e // 4 * HD + HD)
                                lhs, rhs = qs[h, e % 4, t * P:t * P + P], kst[h, 0, 0:nk]
                            bank, c = (psum[e // 4], e % 4 * P) if t == 0 else (psum[2 + e // 2], e % 2 * 2 * P)
                            nc.tensor.matmul(bank[:, c:c + nk], lhs, rhs, start=True, stop=True).then_inc(sm["scores"], 1)
                    n = 0
                    for t in range(QT):
                        for half in range(2):
                            pe.wait_ge(sm["scaled"], it * 4 + (2 * t + half + 1))
                            for kt in range(t + 1):
                                done = sm["pt_act"] if n % 2 == 0 else sm["pt_dve"]
                                pe.wait_ge(done, it * 3 + (n // 2 + 1))
                                for e in range(4):
                                    last = nc.tensor.transpose(psum[6 + n % 2][:, e * P:e * P + P],
                                                               Smq[t][:, half * 4 + e, kt * P:kt * P + P], ident)
                                last.then_inc(sm["turned"], 1)
                                n += 1
                        pe.wait_ge(sm["pt_act"], it * 3 + (n // 2 + 1))
                        pe.wait_ge(sm["pt_dve"], it * 3 + (n // 2 + 1))
                        if nsa:
                            steps = [(vst[:, b * QT + kt, :], PT[:, kt, 4 * b:4 * b + 4, :]) for b in range(2) for kt in range(t + 1)]
                            steps.append((vcz, pcT[:, t, :, :]))
                            for i, (lhs, rhs) in enumerate(steps):
                                last = nc.tensor.matmul(psum[t][:, :], lhs, rhs, start=(i == 0), stop=(i == len(steps) - 1))
                        else:
                            for half in range(2):
                                for kt in range(t + 1):
                                    last = nc.tensor.matmul(psum[2 * t + half][:, :], vst[:, kt, :], PT[:, kt, 4 * half:4 * half + 4, :],
                                                            start=(kt == 0), stop=(kt == t))
                        last.then_inc(sm["o_done"], 1)

            pe.wait_ge(ones_set, 1)

            def project(st, it, **more):
                units(it * 8 + PB[st], PB[st], it * 4 + UB[st], UB[st], 4, DT, lambda j, k: A[:, k, :, :],
                      (lambda k: (a0_ready, k + 1)) if st == "kv" else None, **more)
            project("kv", 0, norm_at=NORM_AT["kv"], then=lambda: norm("kv"))
            with pe.Fori(1, 4) as it:
                project("kv", it)
            pe.wait_ge(in_s, 16)
            nc.tensor.matmul(psum[7][0:SWA_HEADS, 0:RB], bflat[0:NBUCK, SO["table"][0]:SO["table"][1]],
                             bflat[0:NBUCK, SO["onehot"][0]:SO["onehot"][1]], start=True, stop=True).then_inc(table_sum, 1)
            pe.wait_ge(in_k, 16)
            turn_rs(1)
            with pe.Fori(0, 4) as it:
                project("q", it)
            for b in range(2):
                natural(PB["v"] + 8 * b, UB["v"] + 2 * b, A)
            pe.wait_ge(blk_ready, 2)
            units(PB["cmp"], PB["cmp"], UB["cmp"], UB["cmp"], 2, CL, lambda b, l: blks[:, b, l, :, :], width=NB)
            p, u = PB["misc"], UB["misc"]
            s = p % SLOTS
            pe.wait_ge(lo_ready, p + 1)
            for t in range(QT):
                pe.wait_ge(z_ready, u + t + 1)
                tok = slice(t * P, t * P + P)
                bank = psum[(u + t) % 4][:, 0:48]
                for k in range(DT):
                    w = slice(k * 48, k * 48 + 48)
                    nc.tensor.matmul(bank, A[:, k, 0, tok], whi[:, s, w], start=(k == 0), stop=False)
                    nc.tensor.matmul(bank, A[:, k, 0, tok], wlo[:, s, w], start=False, stop=False)
                    last = nc.tensor.matmul(bank, A[:, k, 1, tok], whi[:, s, w], start=False, stop=(k == DT - 1))
                last.then_inc(gate_sum, 1)
            wk, wv = slice(16 * 48, 16 * 48 + P), slice(16 * 48 + P, 16 * 48 + 2 * P)
            pe.wait_ge(h1_ready, 2)
            pe.wait_ge(z_ready, u + 3)
            bank = psum[(u + 2) % 4][:, 0:P]
            nc.tensor.matmul(bank, whi[:, s, wk], pA[:, 0, 0, 0:P], start=True, stop=False)
            nc.tensor.matmul(bank, wlo[:, s, wk], pA[:, 0, 0, 0:P], start=False, stop=False)
            nc.tensor.matmul(bank, whi[:, s, wk], pA[:, 0, 1, 0:P], start=False, stop=True).then_inc(gate_sum, 1)
            pe.wait_ge(z_ready, u + 4)
            bank = psum[(u + 3) % 4][:, 0:P]
            nc.tensor.matmul(bank, pA[:, 1, 0, 0:P], whi[:, s, wv], start=True, stop=False)
            nc.tensor.matmul(bank, pA[:, 1, 0, 0:P], wlo[:, s, wv], start=False, stop=False)
            nc.tensor.matmul(bank, pA[:, 1, 1, 0:P], whi[:, s, wv], start=False, stop=True).then_inc(gate_sum, 1)
            pe.sem_inc(piece_used, 1)
            pe.wait_ge(kcmp_ready, 1)
            pe.wait_ge(z_used, 4 + ZB["q"] + 16)
            pe.wait_ge(rcol_ready, 1)
            for t in range(QT):
                for h in range(HEADS):
                    g = h // HPG
                    last = nc.tensor.matmul(psum[4 + t][:, h * CS:h * CS + CS], y[:, h, t * P:t * P + P],
                                            kcmp[:, g * NPAD:g * NPAD + CS], start=True, stop=True)
                last.then_inc(c_scores, 1)
            for t in range(QT):
                pe.wait_ge(cp_ready, t + 1)
                for r in range(HPG):
                    last = nc.tensor.transpose(psum[6 + t][:, r * P:r * P + P],
                                               cpad[:, t, r, :, :].rearrange("p g n -> p (g n)"), ident)
                last.then_inc(c_turned, 1)
            pe.wait_ge(z_ready, 4 + UB["wo"])
            pe.wait_ge(pcT_ready, QT)
            attention("nsa")
            with pe.Fori(0, 4) as it:
                units(it * 8 + PB["wo"], PB["wo"], it * 4 + UB["wo"], UB["wo"], 4, DT, lambda j, k: H[:, k, :, :],
                      lambda k: (att["nsa"]["o_ready"], 2 + 2 * KVG))

            def hidden(c, it, **more):
                units(c * 64 + it * 8 + PB["ff0"], PB["ff0"], c * 32 + it * 4 + UB["ff0"], UB["ff0"], 4, DT,
                      lambda j, k: A[:, k, :, :], lambda k: (a1_ready, k + 1), **more)

            def chunk(c, first=0):
                with pe.Fori(first, 4) as it:
                    hidden(c, it)
                with pe.Fori(0, 4) as it:
                    units(c * 64 + it * 8 + PB["fd0"], PB["fd0"], c * 32 + it * 4 + UB["fd0"], UB["fd0"], 4, CH,
                          lambda j, k: H[:, k, :, :], lambda k: (ff_ready, c * CH + (k + 1)))
            hidden(0, 0, norm_at=NORM_AT["ff0"], then=lambda: norm("ff0"))
            chunk(0, 1)
            with pe.Fori(1, FF_CHUNKS) as c:
                chunk(c)

            pe.wait_ge(p_ready, 2)
            units(PB["proj"], PB["proj"], UB["proj"], UB["proj"], DT, 2, lambda j, k: pA[:, k, :, :])

            def gate(it, **more):
                units(it * 8 + PB["gate"], PB["gate"], it * 4 + UB["gate"], UB["gate"], 4, DT, lambda j, k: A[:, k, :, :],
                      lambda k: (a2_ready, k + 1), **more)
            gate(0, norm_at=NORM_AT["gate"], then=lambda: norm("gate"))
            with pe.Fori(1, 4) as it:
                gate(it)

            def norms_k2():
                norm("k2")
                norm("k2", 5, acc2)
            units(PB["k2"], PB["k2"], UB["k2"], UB["k2"], 4, DT, lambda j, k: H[:, k, :, :], lambda k: (a3_ready, k + 1),
                  norm_at=NORM_AT["k2"], then=norms_k2)
            turn_rs(5)
            natural(PB["v2"], UB["v2"], H)
            with pe.Fori(0, 4) as it:
                units(it * 8 + PB["q2"], PB["q2"], it * 4 + UB["q2"], UB["q2"], 4, DT, lambda j, k: H[:, k, :, :])
            pe.wait_ge(z_ready, 4 + UB["wo2"])
            attention("swa")
            with pe.Fori(0, 4) as it:
                units(it * 8 + PB["wo2"], PB["wo2"], it * 4 + UB["wo2"], UB["wo2"], 4, DT, lambda j, k: H[:, k, :, :],
                      lambda k: (att["swa"]["o_ready"], 2 + 2 * KVG))
            norm("post")

            t0 = 0
            for c, n in enumerate(CHUNKS2):
                up, dn = f"up{c}", f"dn{c}"

                def hidden2(it, **more):
                    units(it * 8 + PB[up], PB[up], it * 4 + UB[up], UB[up], 4, DT, lambda j, k: A[:, k, :, :],
                          lambda k: (a4_ready, k + 1), **more)
                if c == 0:
                    hidden2(0, norm_at=NORM_AT["up0"], then=lambda: norm("up0"))
                with pe.Fori(1 if c == 0 else 0, n // 2) as it:
                    hidden2(it)
                if n == CH:
                    with pe.Fori(0, 4) as it:
                        units(it * 8 + PB[dn], PB[dn], it * 4 + UB[dn], UB[dn], 4, n, lambda j, k: H[:, k, :, :],
                              lambda k: (up_ready, t0 + k + 1))
                else:
                    for it in range(2):
                        units(it * n + PB[dn], PB[dn], it * 8 + UB[dn], UB[dn], 8, n, lambda j, k: H[:, k, :, :],
                              lambda k: (up_ready, t0 + k + 1))
                t0 += n
            norm("end")

        @block.vector
        def _(dve):
            V = nc.vector
            dve.sem_inc(z_ready, 4)

            def split_lo(i, s):
                dve.wait_ge(hi_ready, i + 1)
                V.tensor_tensor(wlo[:, s, :], raw[:, s, :], whi[:, s, :].bitcast(F32), ALU.subtract).then_inc(lo_ready, 1)

            def body(p, p0, u, u0, zu, z0, n, K, late=None, lag=1, width=S, skip=0, short=0, norm_at=None, then=None):
                at = ends(n, K)
                count = n * K // BLK
                for q in range(LEAD, count + AHEAD):
                    if AHEAD + skip <= q < count + AHEAD - short:
                        split_lo(p + q, (p0 + q) % SLOTS)
                    if norm_at is not None and q == norm_at + LEAD + 1:
                        then()
                    if late:
                        for j in at.get(q - LEAD - lag, []):
                            late(j)
                    for j in at.get(q - LEAD, []):
                        dve.wait_ge(piece_used, p + (SLOTS + q - LEAD + 1))
                        dve.wait_ge(z_used, zu + (j + 1))
                        V.tensor_reduce(z[:, (z0 + j) % 4, 0:width],
                                        psum[(u0 + j) % 4][:, 0:2 * width].rearrange("p (h c) -> p c h", h=2),
                                        AX, ALU.add).then_inc(z_ready, 1)

            steps = Steps(dve, sum_step)

            def rsqrt(dst, var, n):
                dve.wait_ge(root_ready, n)
                steps(V.reciprocal(dst, dst))
                steps(V.tensor_tensor(var, var, dst, ALU.mult))
                steps(V.tensor_tensor(var, var, dst, ALU.mult))
                steps(V.tensor_scalar(var, var, -0.5, 1.5, ALU.mult, ALU.add))
                return V.tensor_tensor(dst, dst, var, ALU.mult)

            def norm(dst, n):
                dve.wait_ge(sum_ready, n)
                V.tensor_scalar(acc[:, :], psum[4][:, 0:S], 1.0 / D, EPS, ALU.mult, ALU.add).then_inc(var_ready, 1)
                dve.wait_ge(var_ready, n)
                return rsqrt(dst, acc[:, :], n)

            def columns_of_rs(n):
                dve.wait_ge(rs_turned, n)
                V.tensor_copy(rcol[:, :], psum[6][:, 0:QT * P].rearrange("p (t c) -> p t c", t=QT)[:, :, 0]).then_inc(rcol_ready, 1)
                dve.wait_ge(rcol_ready, n)

            def values(p, u, v0):
                for q in range(AHEAD, 8 + AHEAD):
                    split_lo(p + q, (p + q) % SLOTS)
                    if q == 7 + LEAD:
                        dve.wait_ge(piece_used, SLOTS + p + 8)
                        for t in range(QT):
                            V.tensor_scalar(vN[:, v0 + t, :], psum[(u + t) % 4][:, :], rcol[:, t:t + 1], None,
                                            ALU.mult).then_inc(z_ready, 1)

            def norm_lo(dst, name, hi_sem, ready):
                def late(t, i):
                    dve.wait_ge(hi_sem, i + 1)
                    V.scalar_tensor_tensor(part(dst, t, 1), tile(x, t), gain(name, t) if name else gg[:, ds(t, 1)],
                                           part(dst, t, 0).bitcast(F32), ALU.mult, ALU.subtract).then_inc(ready, 1)
                return late

            def attention(kind):
                sm = att[kind]
                nsa = kind == "nsa"
                dve.sem_inc(sm["o_ready"], 2)
                dve.sem_inc(sm["pt_dve"], 1)
                per = 2
                with dve.Fori(0, KVG) as it:
                    st = Steps(dve, sm["step"], it * (2 * per))
                    for t in range(QT):
                        nk = (t + 1) * P
                        c = slice(8 * t, 8 * t + 8)
                        if not nsa and t == 0:
                            dve.wait_ge(sm["bias_in"], it * 16 + 16)
                        for e in range(8):
                            bank, o = (psum[e // 4], e % 4 * P) if t == 0 else (psum[2 + e // 2], e % 2 * 2 * P)
                            add = mask[:, 2 * P - nk:] if nsa else bias[:, e, 2 * P - nk:]
                            in_bank = 4 if t == 0 else 2
                            if e % in_bank == 0:
                                dve.wait_ge(sm["scores"], it * 16 + (8 * t + e + in_bank))
                                V.memset(tot[:, 8 * t + e:8 * t + e + 1], 0.0)
                            V.tensor_tensor_reduce(Smq[t][:, e, :], bank[:, o:o + nk], add, 1.0, -3e38, ALU.add, ALU.max,
                                                   mx[:, 8 * t + e:8 * t + e + 1]).then_inc(sm["max"], 1)
                        dve.wait_ge(sm["max"], it * 16 + (8 * t + 8))
                        if nsa:
                            V.tensor_scalar(nmx[:, c], mx[:, c], -1.0, None, ALU.mult).then_inc(sm["shift"], 1)
                        else:
                            sink = par[:, ds(it * 8 + PO["sink"][0], 8)]
                            st(V.tensor_tensor(mx[:, c], mx[:, c], sink, ALU.max))
                            V.tensor_scalar(nmx[:, c], mx[:, c], -1.0, None, ALU.mult).then_inc(sm["shift"], 1)
                            V.tensor_tensor(esk[:, c], sink, mx[:, c], ALU.subtract).then_inc(sm["sinkdiff"], 1)
                    for t in range(QT):
                        c = slice(8 * t, 8 * t + 8)
                        dve.wait_ge(sm["exp"], it * 16 + (8 * t + 8))
                        if nsa:
                            st(V.reciprocal(tot[:, c], sums[:, c]))
                            st(V.tensor_copy(coef[:, c], gts[:, t, ds(it * 12 + 4, 8)]))
                            V.tensor_tensor(coef[:, c], coef[:, c], tot[:, c], ALU.mult).then_inc(sm["coef"], 1)
                        else:
                            dve.wait_ge(sm["sinkexp"], it * 2 + (t + 1))
                            st(V.tensor_tensor(tot[:, c], sums[:, c], esk[:, c], ALU.add))
                            V.reciprocal(coef[:, c], tot[:, c]).then_inc(sm["coef"], 1)
                    for n, (t, half, kt) in enumerate([(0, 0, 0), (0, 1, 0), (1, 0, 0), (1, 0, 1), (1, 1, 0), (1, 1, 1)]):
                        if n % 2 == 1:
                            dve.wait_ge(sm["turned"], it * 6 + (n + 1))
                            V.tensor_copy(PT[:, kt, 4 * half:4 * half + 4, :],
                                          psum[6 + n % 2][:, :].rearrange("p (e q) -> p e q", e=4)).then_inc(sm["pt_dve"], 1)
                        if n in (1, 5):
                            tok = slice(t * P, t * P + P)
                            dve.wait_ge(sm["o_hi"], it * 2 + (t + 1))
                            for rows, bank in o_parts(nsa, t):
                                last = V.tensor_tensor(H[rows, ds(it * 4, 4), 1, tok], bank[rows, :].rearrange("p (r q) -> p r q", r=4),
                                                       H[rows, ds(it * 4, 4), 0, tok].bitcast(F32), ALU.subtract)
                            last.then_inc(sm["o_ready"], 1)

            dve.wait_ge(in_c, 16)
            V.tensor_tensor(gg[:, :], par[:, PO["g_fin"][0]:PO["g_fin"][1]], par[:, PO["g0"][0]:PO["g0"][1]],
                            ALU.mult).then_inc(gg_ready, 1)
            for t in range(DT):
                dve.wait_ge(x0_hi, t + 1)
                V.scalar_tensor_tensor(A[:, t, 1, :], x[:, t, :], gain("g_mix", t), A[:, t, 0, :].bitcast(F32), ALU.mult,
                                       ALU.subtract).then_inc(a0_ready, 1)
                if t in FIRST_SPLITS:
                    split_lo(FIRST_SPLITS.index(t), FIRST_SPLITS.index(t))

            def first_norm():
                norm(rs[:, :], 1).then_inc(rs_ready, 1)
                dve.wait_ge(rs_ready, 1)
                V.tensor_scalar(rs2, rs[:, :], float(P) ** -0.5, None, ALU.mult).then_inc(rs_ready, 1)

            def project(st, it, **more):
                body(it * 8 + PB[st], PB[st], it * 4 + UB[st], UB[st], it * 4 + ZB[st], ZB[st], 4, DT, **more)
            project("kv", 0, skip=len(FIRST_SPLITS) - AHEAD, norm_at=NORM_AT["kv"], then=first_norm)
            with dve.Fori(1, 4) as it:
                project("kv", it)
            dve.wait_ge(table_sum, 1)
            V.tensor_tensor(bflat[0:NBUCK, 1024:1024 + RB], psum[7][0:SWA_HEADS, 0:RB],
                            bflat[0:NBUCK, SO["band"][0]:SO["band"][1]], ALU.add).then_inc(table_row, 1)
            columns_of_rs(1)
            with dve.Fori(0, 4) as it:
                project("q", it)
            dve.wait_ge(z_used, 4 + ZB["kv"] + 8)
            for b, pos in enumerate(("pos_k", "pos_v")):
                src = kvc[:, b, :, :].rearrange("p g (m s) -> p s g m", s=CS)
                for half in range(2):
                    emb = par[:, PO[pos][0] + CS * half:PO[pos][0] + CS * half + CS].unsqueeze(2).to_broadcast([P, CS, NCMP])
                    for g in range(KVG):
                        V.tensor_tensor(blkf[:, CS * half:CS * half + CS, g, :], src[:, :, g, half:half + NCMP], emb,
                                        ALU.add).then_inc(blk_step, 1)
                dve.wait_ge(blk_hi, b + 1)
                dve.wait_ge(blk_step, 8 * b + 8)
                V.tensor_tensor(blks[:, b, :, 1, :], blkf[:, :, :, :].rearrange("p l g n -> p l (g n)"),
                                blks[:, b, :, 0, :].bitcast(F32), ALU.subtract).then_inc(blk_ready, 1)
                dve.wait_ge(blk_ready, b + 1)
                values(PB["v"] + 8 * b, UB["v"] + 2 * b, 2 * b)
            body(PB["cmp"], PB["cmp"], UB["cmp"], UB["cmp"], ZB["cmp"], ZB["cmp"], 2, CL, width=NB, short=1)
            u = UB["misc"]
            for b in range(2):
                dve.wait_ge(ch_hi, b + 1)
                V.tensor_tensor(pA[:, b, 1, 0:P].rearrange("p (g n) -> p g n", g=KVG)[:, :, 0:NCMP],
                                ch[:, b * 64:b * 64 + NB].rearrange("p (g n) -> p g n", g=KVG),
                                pA[:, b, 0, 0:P].rearrange("p (g n) -> p g n", g=KVG)[:, :, 0:NCMP].bitcast(F32),
                                ALU.subtract).then_inc(h1_ready, 1)
            for t in range(QT):
                dve.wait_ge(gate_sum, t + 1)
                V.tensor_scalar(gts[:, t, :], psum[(u + t) % 4][:, 0:48], rcol[:, t:t + 1], None, ALU.mult).then_inc(z_ready, 1)
            dve.wait_ge(gate_sum, 3)
            V.tensor_copy(kcmp, psum[(u + 2) % 4][:, 0:P]).then_inc(kcmp_ready, 1)
            dve.wait_ge(kcmp_ready, 1)
            dve.sem_inc(z_ready, 1)
            dve.wait_ge(gate_sum, 4)
            dve.wait_ge(vcz_zero, 1)
            for g in range(KVG):
                rows = slice(g * NPAD, g * NPAD + NPAD)
                V.tensor_copy(vczall[rows, g, :], psum[(u + 3) % 4][rows, 0:P]).then_inc(vcmp_ready, 1)
            dve.wait_ge(vcmp_ready, KVG)
            dve.sem_inc(z_ready, 1)
            split_lo(PB["wo"] + 3, (PB["wo"] + 3) % SLOTS)
            st = Steps(dve, c_step)
            dve.wait_ge(cpad_zero, 1)
            for t in range(QT):
                c = cprob[:, t, :, :]
                dve.wait_ge(c_scores, t + 1)
                st(V.tensor_tensor(c, psum[4 + t][:, 0:HEADS * CS].rearrange("p (h n) -> p h n", h=HEADS),
                                   cmask[:, t, :].unsqueeze(1).to_broadcast([P, HEADS, CS]), ALU.add))
                st(V.tensor_reduce(cs[:, t, :], c, AX, ALU.max))
                V.tensor_tensor(c, c, cs[:, t, :].unsqueeze(2).to_broadcast([P, HEADS, CS]), ALU.subtract).then_inc(c_shift, 1)
            dve.wait_ge(gates_ready, QT)
            for t in range(QT):
                c = cprob[:, t, :, :]
                dve.wait_ge(c_exp, t + 1)
                st(V.tensor_reduce(cs[:, 2 + t, :], c, AX, ALU.add))
                st(V.reciprocal(cs[:, 4 + t, :], cs[:, 2 + t, :]))
                st(V.tensor_tensor(cs[:, 6 + t, :].rearrange("p (g r) -> p g r", g=KVG),
                                   cs[:, 4 + t, :].rearrange("p (g r) -> p g r", g=KVG),
                                   gts[:, t, :].rearrange("p (g b r) -> p g b r", g=KVG, b=3)[:, :, 0, :], ALU.mult))
                st(V.tensor_tensor(c, c, cs[:, 6 + t, :].unsqueeze(2).to_broadcast([P, HEADS, CS]), ALU.mult))
                for g in range(KVG):
                    last = V.tensor_tensor(cpad[:, t, :, g, 0:CS], c[:, HPG * g:HPG * g + HPG, :],
                                           cvalid[:, t, :].unsqueeze(1).to_broadcast([P, HPG, CS]), ALU.mult)
                last.then_inc(cp_ready, 1)
            for t in range(QT):
                dve.wait_ge(c_turned, t + 1)
                V.tensor_copy(pcT[:, t, :, :], psum[6 + t][:, :].rearrange("p (r q) -> p r q", r=HPG)).then_inc(pcT_ready, 1)
            attention("nsa")

            lo1 = norm_lo(A, "g_ffn", wo_hi, a1_ready)
            split_lo(PB["wo"] + 4, (PB["wo"] + 4) % SLOTS)
            with dve.Fori(0, 4) as it:
                body(it * 8 + PB["wo"], PB["wo"], it * 4 + UB["wo"], UB["wo"], it * 4 + ZB["wo"], ZB["wo"], 4, DT,
                     lambda j: lo1(it * 4 + j, it * 4 + j))

            def hidden(c, it, **more):
                body(c * 64 + it * 8 + PB["ff0"], PB["ff0"], c * 32 + it * 4 + UB["ff0"], UB["ff0"],
                     c * 32 + it * 4 + ZB["ff0"], ZB["ff0"], 4, DT, **more)

            def chunk(c, first=0, late=None):
                with dve.Fori(first, 4) as it:
                    hidden(c, it)
                with dve.Fori(0, 4) as it:
                    body(c * 64 + it * 8 + PB["fd0"], PB["fd0"], c * 32 + it * 4 + UB["fd0"], UB["fd0"],
                         c * 32 + it * 4 + ZB["fd0"], ZB["fd0"], 4, CH, (lambda j: late(it * 4 + j, it * 4 + j)) if late else None)
            hidden(0, 0, norm_at=NORM_AT["ff0"], then=lambda: norm(rs[:, :], 2).then_inc(rs_ready, 1))
            for k in range(2):
                dve.wait_ge(p_hi, k + 1)
                V.tensor_tensor(pA[:, k, 1, :], tC[:, k, :], pA[:, k, 0, :].bitcast(F32), ALU.subtract).then_inc(p_ready, 1)
            chunk(0, 1)
            with dve.Fori(1, FF_CHUNKS - 1) as c:
                chunk(c)
            chunk(FF_CHUNKS - 1, 0, norm_lo(A, "g_ple", fd_hi, a2_ready))
            body(PB["proj"], PB["proj"], UB["proj"], UB["proj"], ZB["proj"], ZB["proj"], DT, 2)
            lo3 = norm_lo(H, None, ple_hi, a3_ready)

            def gate(it, **more):
                body(it * 8 + PB["gate"], PB["gate"], it * 4 + UB["gate"], UB["gate"], it * 4 + ZB["gate"], ZB["gate"], 4, DT,
                     lambda j: lo3(it * 4 + j, it * 4 + j), lag=2, **more)
            gate(0, norm_at=NORM_AT["gate"], then=lambda: norm(rs[:, :], 3).then_inc(rs_ready, 1))
            with dve.Fori(1, 4) as it:
                gate(it)

            def norms_k2():
                steps(norm(rs3, 4))
                dve.wait_ge(sum_ready, 5)
                steps(V.scalar_tensor_tensor(acc2, psum[5][:, 0:S], 1.0 / D, rs3, ALU.mult, ALU.mult))
                steps(V.tensor_tensor(acc2, acc2, rs3, ALU.mult))
                V.tensor_scalar(acc2, acc2, EPS, None, ALU.add).then_inc(var_ready, 1)
                steps(rsqrt(rs[:, :], acc2, 5))
                V.tensor_tensor(rs[:, :], rs[:, :], rs3, ALU.mult).then_inc(rs_ready, 1)
                dve.wait_ge(rs_ready, 5)
                V.tensor_scalar(rs2, rs[:, :], float(HD) ** -0.5, None, ALU.mult).then_inc(rs_ready, 1)
            body(PB["k2"], PB["k2"], UB["k2"], UB["k2"], ZB["k2"], ZB["k2"], 4, DT, norm_at=NORM_AT["k2"], then=norms_k2)
            columns_of_rs(2)
            values(PB["v2"], UB["v2"], 0)

            def normed(t):
                V.scalar_tensor_tensor(tile(x, t), tile(x, t), gain("g_fin", t), rs3, ALU.mult, ALU.mult).then_inc(xn_ready, 1)

            def queries2(it, **more):
                body(it * 8 + PB["q2"], PB["q2"], it * 4 + UB["q2"], UB["q2"], it * 4 + ZB["q2"], ZB["q2"], 4, DT,
                     lambda j: normed(it * 4 + j), **more)
            with dve.Fori(0, 3) as it:
                queries2(it)
            queries2(3, short=1)
            attention("swa")
            split_lo(PB["wo2"] + 4, (PB["wo2"] + 4) % SLOTS)

            def out2(it, **more):
                body(it * 8 + PB["wo2"], PB["wo2"], it * 4 + UB["wo2"], UB["wo2"], it * 4 + ZB["wo2"], ZB["wo2"], 4, DT, **more)
            with dve.Fori(0, 3) as it:
                out2(it)
            out2(3, short=1)
            norm(rs[:, :], 6).then_inc(rs_ready, 1)
            dve.wait_ge(rs_ready, 7)
            dve.wait_ge(xn_ready, DT)
            lo4 = norm_lo(A, "g2", post_hi, a4_ready)
            for t in range(DT + 3):
                if t < DT:
                    V.scalar_tensor_tensor(tA[:, t % 4, :], y[:, t, :], gain("g1", t), rs[:, :], ALU.mult,
                                           ALU.mult).then_inc(post_t, 1)
                if t >= 3:
                    lo4(t - 3, t - 3)
                if t in POST_SPLITS:
                    i = 4 + POST_SPLITS.index(t)
                    split_lo(PB["up0"] + i, (PB["up0"] + i) % SLOTS)

            def conv(i, slot):
                dve.wait_ge(up_c0, i + 1)
                w = [par[:, ds(i * 3 + (PO["conv"][0] + k), 1)] for k in range(3)]
                V.scalar_tensor_tensor(tA[:, slot, :], ub[:, slot, 1:S + 1], w[1], c0[:, slot % 2, :], ALU.mult,
                                       ALU.add).then_inc(up_step, 1)
                dve.wait_ge(up_step, i + 1)
                V.scalar_tensor_tensor(tB[:, slot, :], ub[:, slot, 2:S + 2], w[2], tA[:, slot, :], ALU.mult,
                                       ALU.add).then_inc(up_conv, 1)

            t0 = 0
            for c, n in enumerate(CHUNKS2):
                up, dn = f"up{c}", f"dn{c}"

                def hidden2(it, **more):
                    body(it * 8 + PB[up], PB[up], it * 4 + UB[up], UB[up], it * 4 + ZB[up], ZB[up], 4, DT,
                         lambda j: conv(it * 4 + (2 * t0 + j), j), **more)
                if c == 0:
                    hidden2(0, skip=len(POST_SPLITS) + 4 - AHEAD, norm_at=NORM_AT["up0"],
                            then=lambda: norm(rs[:, :], 7).then_inc(rs_ready, 1))
                with dve.Fori(1 if c == 0 else 0, n // 2) as it:
                    hidden2(it)
                if n == CH:
                    with dve.Fori(0, 4) as it:
                        body(it * 8 + PB[dn], PB[dn], it * 4 + UB[dn], UB[dn], it * 4 + ZB[dn], ZB[dn], 4, n)
                else:
                    for it in range(2):
                        body(it * n + PB[dn], PB[dn], it * 8 + UB[dn], UB[dn], it * 8 + ZB[dn], ZB[dn], 8, n, short=AHEAD * it)
                t0 += n
            norm(rs[:, :], 8).then_inc(rs_ready, 1)
            dve.wait_ge(rs_ready, 9)
            with dve.Fori(0, 4) as it:
                for j in range(4):
                    V.scalar_tensor_tensor(tile(y, it * 4 + j), tile(y, it * 4 + j), gain("g3", it * 4 + j), rs[:, :],
                                           ALU.mult, ALU.mult).then_inc(fin_t, 1)

        @block.scalar
        def _(act):
            C = nc.scalar

            def split_hi(i, s, lap):
                act.wait_ge(raw_landed[s], lap)
                act.wait_ge(piece_used, i + 1)
                C.copy(whi[:, s, :], raw[:, s, :]).then_inc(hi_ready, 1)

            def split(p, p0, i, per, it):
                q = p0 + i
                split_hi(p + i, q % SLOTS, (it * (per // SLOTS) + (q // SLOTS + 1)) * 16)

            def body(p, p0, it, n, K, each=None, late=None, skip=0, short=0, norm_at=None, then=None):
                at = ends(n, K)
                count = n * K // BLK
                for q in range(LEAD, count + AHEAD):
                    if AHEAD + skip <= q < count + AHEAD - short:
                        split(p, p0, q, count, it)
                    if norm_at is not None and q == norm_at + LEAD + 1:
                        then()
                    if late:
                        for j in at.get(q - LEAD - 2, []):
                            late(j)
                    if each:
                        for j in at.get(q - LEAD - 1, []):
                            each(j)

            def norm_hi(name, src_sem, src0, hi_sem, sq_sem):
                def each(t, i, j):
                    act.wait_ge(src_sem, i + src0 + 1)
                    C.activation(part(A, t, 0), tile(x, t), ACT.Copy, scale=gain(name, t)).then_inc(hi_sem, 1)
                    C.activation(sq[:, j, :], tile(x, t), ACT.Square).then_inc(sq_sem, 1)
                return each

            def attention(kind):
                sm = att[kind]
                nsa = kind == "nsa"
                act.sem_inc(sm["pt_act"], 1)
                with act.Fori(0, KVG) as it:
                    if not nsa:
                        rows = bias_rows.ap()[ds(it * 8, 8), P - 1:P - 1 + P * (RB - 1)]
                        act.dma_start(bias[:, :, :], rows.rearrange("e (q i) -> q e i", q=P)[:, :, 0:2 * P]).then_inc(sm["bias_in"], 16)
                    C.copy(qs[:, :, :], y[:, ds(it * 4, 4), :]).then_inc(sm["q_staged"], 1)
                    for t in range(QT):
                        c = slice(8 * t, 8 * t + 8)
                        act.wait_ge(sm["shift"], it * 2 + (t + 1))
                        for e in range(8):
                            i = 8 * t + e
                            C.activation(Smq[t][:, e, :], Smq[t][:, e, :], ACT.Exp, bias=nmx[:, i:i + 1],
                                         accum_out=sums[:, i:i + 1]).then_inc(sm["exp"], 1)
                        if not nsa:
                            act.wait_ge(sm["sinkdiff"], it * 2 + (t + 1))
                            C.activation(esk[:, c], esk[:, c], ACT.Exp).then_inc(sm["sinkexp"], 1)
                    for n, (t, half, kt) in enumerate([(0, 0, 0), (0, 1, 0), (1, 0, 0), (1, 0, 1), (1, 1, 0), (1, 1, 1)]):
                        if n % 2 == 0:
                            act.wait_ge(sm["turned"], it * 6 + (n + 1))
                            C.copy(PT[:, kt, 4 * half:4 * half + 4, :],
                                   psum[6 + n % 2][:, :].rearrange("p (e q) -> p e q", e=4)).then_inc(sm["pt_act"], 1)
                        if n in (1, 5):
                            tok = slice(t * P, t * P + P)
                            act.wait_ge(sm["o_done"], it * 2 + (t + 1))
                            for rows, bank in o_parts(nsa, t):
                                last = C.copy(H[rows, ds(it * 4, 4), 0, tok], bank[rows, :].rearrange("p (r q) -> p r q", r=4))
                            last.then_inc(sm["o_hi"], 1)

            def root(n, dst, var=acc[:, :]):
                act.wait_ge(var_ready, n)
                C.activation(dst, var, ACT.Sqrt).then_inc(root_ready, 1)

            act.dma_start(bflat[0:NBUCK, 0:NSETUP], setup).then_inc(in_s, 16)
            act.wait_ge(in_c, 16)
            for t in range(DT):
                if t % 4 == 0:
                    act.wait_ge(in_x[t // 4], 16)
                C.activation(A[:, t, 0, :], x[:, t, :], ACT.Copy, scale=gain("g_mix", t)).then_inc(x0_hi, 1)
                C.activation(tile(y, t), x[:, t, :], ACT.Square).then_inc(x0_sq, 1)
                if t in FIRST_SPLITS:
                    i = FIRST_SPLITS.index(t)
                    split_hi(i, i, 16)

            def project(st, it, **more):
                body(it * 8 + PB[st], PB[st], it, 4, DT, **more)
            project("kv", 0, skip=len(FIRST_SPLITS) - AHEAD, norm_at=NORM_AT["kv"], then=lambda: root(1, rs[:, :]))
            with act.Fori(1, 4) as it:
                project("kv", it)
            act.wait_ge(table_row, 1)
            act.dma_start(bias_rows.ap().rearrange("h (q i) -> h q i", q=P),
                          bflat[0:NBUCK, 1024:1024 + RB].unsqueeze(1).to_broadcast([SWA_HEADS, P, RB])).then_inc(rows_out, 16)
            with act.Fori(0, 4) as it:
                project("q", it)
            for b in range(2):
                act.wait_ge(blk_step, 8 * b + 8)
                C.copy(blks[:, b, :, 0, :], blkf[:, :, :, :].rearrange("p l g n -> p l (g n)")).then_inc(blk_hi, 1)
                for i in range(8):
                    split(PB["v"], PB["v"], 8 * b + i + AHEAD, 0, 0)

            def csilu(b):
                act.wait_ge(z_used, 4 + ZB["cmp"] + b + 1)
                C.activation(csig[:, b * 64:b * 64 + NB], zr[:, b, 0:NB], ACT.Sigmoid).then_inc(csig_ready, 1)
                act.wait_ge(ch_ready, b + 1)
                act.wait_ge(pad_zero, 1)
                C.copy(pA[:, b, 0, 0:P].rearrange("p (g n) -> p g n", g=KVG)[:, :, 0:NCMP],
                       ch[:, b * 64:b * 64 + NB].rearrange("p (g n) -> p g n", g=KVG)).then_inc(ch_hi, 1)
            body(PB["cmp"], PB["cmp"], 0, 2, CL, csilu, short=1)
            for t in range(QT):
                act.wait_ge(z_ready, 4 + UB["misc"] + t + 1)
                C.activation(gts[:, t, :], gts[:, t, :], ACT.Sigmoid).then_inc(gates_ready, 1)
            act.wait_ge(z_ready, 4 + UB["wo"])
            split(PB["wo"], PB["wo"], 3, 0, 0)
            for t in range(QT):
                act.wait_ge(c_shift, t + 1)
                C.activation(cprob[:, t, :, :], cprob[:, t, :, :], ACT.Exp).then_inc(c_exp, 1)
            act.wait_ge(z_used, 4 + ZB["wo"])
            attention("nsa")
            act.dma_start(tC[:, 0:2, :], pT).then_inc(in_p, 16)

            h1 = norm_hi("g_ffn", z_used, 4 + ZB["wo"], wo_hi, wo_sq)
            split(PB["wo"], PB["wo"], 4, 0, 0)
            with act.Fori(0, 4) as it:
                body(it * 8 + PB["wo"], PB["wo"], it, 4, DT, lambda j: h1(it * 4 + j, it * 4 + j, j))

            def hidden(c, it, **more):
                def relu_squared(j):
                    i = c * 16 + it * 4 + j
                    act.wait_ge(z_used, c * 32 + it * 4 + (4 + ZB["ff0"] + j + 1))
                    C.activation(tA[:, j, :], zr[:, j, :], ACT.Relu).then_inc(ff_relu, 1)
                    act.wait_ge(ff_relu, i + 1)
                    C.activation(part(H, it * 4 + j, 0), tA[:, j, :], ACT.Square).then_inc(ff_hi, 1)
                body(c * 64 + it * 8 + PB["ff0"], PB["ff0"], c * 8 + it, 4, DT, relu_squared, **more)

            def chunk(c, first=0, prep=None):
                with act.Fori(first, 4) as it:
                    hidden(c, it)
                with act.Fori(0, 4) as it:
                    body(c * 64 + it * 8 + PB["fd0"], PB["fd0"], c * 8 + it, 4, CH,
                         (lambda j: prep(it * 4 + j, it * 4 + j, j)) if prep else None)
            hidden(0, 0, norm_at=NORM_AT["ff0"], then=lambda: root(2, rs[:, :]))
            act.wait_ge(in_p, 16)
            for k in range(2):
                C.copy(pA[:, k, 0, :], tC[:, k, :]).then_inc(p_hi, 1)
            chunk(0, 1)
            with act.Fori(1, FF_CHUNKS - 1) as c:
                chunk(c)
            last = f"fd{FF_CHUNKS - 1}"
            chunk(FF_CHUNKS - 1, 0, norm_hi("g_ple", z_used, 4 + ZB[last], fd_hi, fd_sq))
            body(PB["proj"], PB["proj"], 0, DT, 2)

            def gate(it, **more):
                def sigmoid(j):
                    act.wait_ge(z_used, it * 4 + (4 + ZB["gate"] + j + 1))
                    C.activation(tA[:, j, :], zr[:, j, :], ACT.Sigmoid).then_inc(ple_sig, 1)

                def next_input(j):
                    t = it * 4 + j
                    act.wait_ge(ple_x, t + 1)
                    C.activation(part(H, t, 0), tile(x, t), ACT.Copy, scale=gg[:, ds(t, 1)]).then_inc(ple_hi, 1)
                    C.activation(sq[:, j, :], tile(x, t), ACT.Square).then_inc(ple_sq, 1)
                    C.activation(sq2[:, j, :], tile(x, t), ACT.Square, scale=gain("g_fin", t)).then_inc(ple_sq, 1)
                body(it * 8 + PB["gate"], PB["gate"], it, 4, DT, sigmoid, next_input, **more)
            act.wait_ge(gg_ready, 1)
            gate(0, norm_at=NORM_AT["gate"], then=lambda: root(3, rs[:, :]))
            with act.Fori(1, 4) as it:
                gate(it)

            def roots_k2():
                root(4, rs3)
                root(5, rs[:, :], acc2)
            body(PB["k2"], PB["k2"], 0, 4, DT, norm_at=NORM_AT["k2"], then=roots_k2)
            for i in range(8):
                split(PB["v2"], PB["v2"], i + AHEAD, 0, 0)
            with act.Fori(0, 3) as it:
                body(it * 8 + PB["q2"], PB["q2"], it, 4, DT)
            body(3 * 8 + PB["q2"], PB["q2"], 3, 4, DT, short=1)
            act.wait_ge(z_used, 4 + ZB["wo2"])
            act.wait_ge(rows_out, 16)
            attention("swa")
            split(PB["wo2"], PB["wo2"], 4, 0, 0)

            def squares(src_sem, n0, sq_sem):
                def each(t, i, j):
                    act.wait_ge(src_sem, i + (n0 + 1))
                    C.activation(sq[:, j, :], tile(y, t), ACT.Square).then_inc(sq_sem, 1)
                return each
            s2 = squares(z_used, 4 + ZB["wo2"], wo2_sq)

            def out2(it, **more):
                body(it * 8 + PB["wo2"], PB["wo2"], it, 4, DT, lambda j: s2(it * 4 + j, it * 4 + j, j), **more)
            with act.Fori(0, 3) as it:
                out2(it)
            out2(3, short=1)
            root(6, rs[:, :])
            h4 = norm_hi("g2", post_x, 0, post_hi, post_sq)
            for t in range(DT + 3):
                if t < DT:
                    h4(t, t, t % 4)
                if t in POST_SPLITS:
                    split(PB["up0"], PB["up0"], 4 + POST_SPLITS.index(t), 0, 0)

            t0 = 0
            for c, n in enumerate(CHUNKS2):
                up, dn = f"up{c}", f"dn{c}"

                def hidden2(it, **more):
                    def tap(j):
                        act.wait_ge(z_used, it * 4 + (4 + ZB[up] + j + 1))
                        C.activation(c0[:, j % 2, :], ub[:, j, 0:S], ACT.Copy,
                                     scale=par[:, ds(it * 12 + (PO["conv"][0] + 3 * (2 * t0 + j)), 1)]).then_inc(up_c0, 1)

                    def tail(j):
                        if j % 2 == 0:
                            act.wait_ge(up_conv, it * 4 + (2 * t0 + j + 1))
                            C.activation(tC[:, j, :], tB[:, j, :], ACT.Sigmoid).then_inc(up_sig, 1)
                        else:
                            act.wait_ge(up_h, it * 2 + (t0 + j // 2 + 1))
                            C.copy(part(H, it * 2 + j // 2, 0), zr[:, j, :]).then_inc(up_hi, 1)
                    body(it * 8 + PB[up], PB[up], it, 4, DT, tap, tail, **more)
                if c == 0:
                    hidden2(0, skip=len(POST_SPLITS) + 4 - AHEAD, norm_at=NORM_AT["up0"], then=lambda: root(7, rs[:, :]))
                with act.Fori(1 if c == 0 else 0, n // 2) as it:
                    hidden2(it)
                if n == CH:
                    with act.Fori(0, 4) as it:
                        body(it * 8 + PB[dn], PB[dn], it, 4, n)
                else:
                    s3 = squares(z_used, 4 + ZB[dn], dn_sq)
                    for it in range(2):
                        body(it * n + PB[dn], PB[dn], it, 8, n, lambda j: s3(it * 8 + j, it * 8 + j, j % 4), short=AHEAD * it)
                t0 += n
            root(8, rs[:, :])

        @block.gpsimd
        def _(pool):
            G = nc.gpsimd
            pool.sem_inc(z_used, 4)
            G.memset(ones[:, :], 1.0).then_inc(ones_set, 1)

            def add_acc(dst, src, n):
                pool.wait_ge(acc_step, n)
                G.tensor_tensor(dst, dst, src, ALU.add).then_inc(acc_step, 1)

            def take(u, z0, j, fn):
                pool.wait_ge(z_ready, u + (4 + j + 1))
                fn(z[:, (z0 + j) % 4, :]).then_inc(z_used, 1)

            def mul(dst, by):
                return lambda zz: G.tensor_tensor(dst, zz, by, ALU.mult)

            pool.sem_inc(acc_step, 1)
            pool.wait_ge(x0_sq, 2)
            G.tensor_tensor(acc[:, :], y[:, 0, :], y[:, 1, :], ALU.add).then_inc(acc_step, 1)
            for t in range(2, DT):
                pool.wait_ge(x0_sq, t + 1)
                add_acc(acc[:, :], y[:, t, :], t)
            pool.wait_ge(rs_ready, 2)
            for b in range(2):
                with pool.Fori(0, 2) as it:
                    for j in range(4):
                        dst = kvc if b == 0 else kT
                        take(it * 4 + (UB["kv"] + 8 * b), ZB["kv"], j,
                             mul(dst[:, ds(it, 1), j, :].rearrange("p a t -> p (a t)"), rs[:, :]))
            with pool.Fori(0, 4) as it:
                for j in range(4):
                    take(it * 4 + UB["q"], ZB["q"], j, mul(tile(y, it * 4 + j), rs2))
            pool.wait_ge(rows_out, 16)
            G.memset(pA[:, :, :, :].rearrange("p a b c -> p (a b c)").bitcast(F32), 0.0).then_inc(pad_zero, 1)
            for b in range(2):
                take(UB["cmp"], ZB["cmp"], b, lambda zz: G.tensor_copy(zr[:, b, 0:NB], zz[:, 0:NB]))
                pool.wait_ge(csig_ready, b + 1)
                G.tensor_tensor(ch[:, b * 64:b * 64 + NB], zr[:, b, 0:NB], csig[:, b * 64:b * 64 + NB], ALU.mult).then_inc(ch_ready, 1)
            G.memset(vczall[:, :, :], 0.0).then_inc(vcz_zero, 1)
            G.memset(cpad[:, :, :, :, :].rearrange("p t r g n -> p (t r g n)"), 0.0).then_inc(cpad_zero, 1)

            def attention(kind):
                sm = att[kind]
                nsa = kind == "nsa"
                with pool.Fori(0, KVG) as it:
                    pool.wait_ge(sm["o_ready"], it * 2 + 2)
                    if nsa:
                        G.tensor_copy(kst[:, :, :], kT[:, :, ds(it, 1), :].rearrange("p b a t -> p b (a t)")).then_inc(sm["kv_staged"], 1)
                        G.tensor_copy(vst[:, :, :], vN[:, :, ds(it * P, P)]).then_inc(sm["kv_staged"], 1)
                        G.tensor_copy(vcz, tile(vczall, it)).then_inc(sm["kv_staged"], 1)
                    else:
                        G.tensor_copy(kst[:, 0, :], kT[:, 0, ds(it, 1), :].rearrange("p a t -> p (a t)")).then_inc(sm["kv_staged"], 1)
                        G.tensor_copy(vst[:, 0:QT, :], vN[:, 0:QT, ds(it * P, P)]).then_inc(sm["kv_staged"], 1)
                    for t in range(QT):
                        pool.wait_ge(sm["coef"], it * 2 + (t + 1))
                        for half in range(2):
                            e = slice(4 * half, 4 * half + 4)
                            c = coef[:, 8 * t + 4 * half:8 * t + 4 * half + 4].unsqueeze(2).to_broadcast([P, 4, (t + 1) * P])
                            G.tensor_tensor(Smq[t][:, e, :], Smq[t][:, e, :], c, ALU.mult).then_inc(sm["scaled"], 1)

            pool.wait_ge(vcmp_ready, KVG)
            attention("nsa")

            def residual(st, c, it, j):
                take(c * 32 + it * 4 + UB[st], ZB[st], j,
                     lambda zz: G.tensor_tensor(tile(x, it * 4 + j), tile(x, it * 4 + j), zz, ALU.add))

            G.memset(acc[:, :], 0.0).then_inc(acc_zero, 1)
            pool.wait_ge(acc_zero, 1)
            with pool.Fori(0, 4) as it:
                for j in range(4):
                    residual("wo", 0, it, j)
                    pool.wait_ge(wo_sq, it * 4 + (j + 1))
                    add_acc(acc[:, :], sq[:, j, :], it * 4 + (ACC0["ff0"] + j))
            pool.wait_ge(rs_ready, 3)

            def chunk(c, prep):
                with pool.Fori(0, 4) as it:
                    for j in range(4):
                        i = c * 16 + it * 4 + j
                        take(c * 32 + it * 4 + UB["ff0"], ZB["ff0"], j, mul(zr[:, j, :], rs[:, :]))
                        pool.wait_ge(ff_relu, i + 1)
                        G.tensor_tensor(tB[:, j, :], tA[:, j, :], tA[:, j, :], ALU.mult).then_inc(ff_step, 1)
                        pool.wait_ge(ff_step, i + 1)
                        pool.wait_ge(ff_hi, i + 1)
                        G.tensor_tensor(part(H, it * 4 + j, 1), tB[:, j, :], part(H, it * 4 + j, 0).bitcast(F32),
                                        ALU.subtract).then_inc(ff_ready, 1)
                with pool.Fori(0, 4) as it:
                    for j in range(4):
                        residual("fd0", c, it, j)
                        if prep:
                            pool.wait_ge(fd_sq, it * 4 + (j + 1))
                            add_acc(acc[:, :], sq[:, j, :], it * 4 + (ACC0["gate"] + j))
            with pool.Fori(0, FF_CHUNKS - 1) as c:
                chunk(c, False)
            G.memset(acc[:, :], 0.0).then_inc(acc_zero, 1)
            pool.wait_ge(acc_zero, 2)
            chunk(FF_CHUNKS - 1, True)
            for j in range(DT):
                take(UB["proj"], ZB["proj"], j, lambda zz: G.tensor_copy(y[:, j, :], zz))
            pool.wait_ge(rs_ready, 4)
            G.memset(acc[:, :], 0.0).then_inc(acc_zero, 1)
            G.memset(acc2, 0.0).then_inc(acc_zero, 1)
            pool.wait_ge(acc_zero, 4)
            with pool.Fori(0, 4) as it:
                for j in range(4):
                    t = it * 4 + j
                    take(it * 4 + UB["gate"], ZB["gate"], j, mul(zr[:, j, :], rs[:, :]))
                    pool.wait_ge(ple_sig, t + 1)
                    G.tensor_tensor(tB[:, j, :], tA[:, j, :], tile(y, t), ALU.mult).then_inc(ple_step, 1)
                    pool.wait_ge(ple_step, t + 1)
                    G.tensor_tensor(tile(x, t), tile(x, t), tB[:, j, :], ALU.add).then_inc(ple_x, 1)
                    for i in ([j - 1] if 0 < j < 3 else [j - 1, j] if j == 3 else []):
                        pool.wait_ge(ple_sq, it * 8 + (2 * i + 2))
                        add_acc(acc[:, :], sq[:, i, :], it * 8 + (ACC0["k2"] + 2 * i))
                        add_acc(acc2, sq2[:, i, :], it * 8 + (ACC0["k2"] + 2 * i + 1))
            pool.wait_ge(rs_ready, 6)
            for j in range(4):
                take(UB["k2"], ZB["k2"], j, mul(kT[:, 0, j, :], rs[:, :]))
            with pool.Fori(0, 4) as it:
                for j in range(4):
                    take(it * 4 + UB["q2"], ZB["q2"], j, mul(tile(y, it * 4 + j), rs2))
            attention("swa")
            G.memset(acc[:, :], 0.0).then_inc(acc_zero, 1)
            pool.wait_ge(acc_zero, 5)
            with pool.Fori(0, 4) as it:
                for j in range(4):
                    take(it * 4 + UB["wo2"], ZB["wo2"], j, lambda zz: G.tensor_copy(tile(y, it * 4 + j), zz))
                    pool.wait_ge(wo2_sq, it * 4 + (j + 1))
                    add_acc(acc[:, :], sq[:, j, :], it * 4 + (ACC0["post"] + j))
            pool.wait_ge(rs_ready, 7)
            G.memset(acc[:, :], 0.0).then_inc(acc_zero, 1)
            pool.wait_ge(acc_zero, 6)
            with pool.Fori(0, 4) as it:
                for j in range(4):
                    t = it * 4 + j
                    pool.wait_ge(post_t, t + 1)
                    G.tensor_tensor(tile(x, t), tile(x, t), tA[:, j, :], ALU.add).then_inc(post_x, 1)
                    pool.wait_ge(post_sq, t + 1)
                    add_acc(acc[:, :], sq[:, j, :], it * 4 + (ACC0["up0"] + j))
            G.memset(ub[:, :, 0:2], 0.0).then_inc(acc_zero, 1)
            pool.wait_ge(rs_ready, 8)
            G.memset(acc[:, :], 0.0).then_inc(acc_zero, 1)
            pool.wait_ge(acc_zero, 8)
            t0 = 0
            for c, n in enumerate(CHUNKS2):
                up, dn = f"up{c}", f"dn{c}"
                with pool.Fori(0, n // 2) as it:
                    def preact(j):
                        take(it * 4 + UB[up], ZB[up], j, mul(ub[:, j, 2:S + 2], rs[:, :]))

                    def gated(j):
                        pool.wait_ge(up_sig, it * 2 + (t0 + j // 2 + 1))
                        G.tensor_tensor(tC[:, j, :], tC[:, j, :], tB[:, j, :], ALU.mult).then_inc(up_gated, 1)

                    def product(j):
                        i = it * 2 + (t0 + j // 2)
                        pool.wait_ge(up_conv, i * 2 + 2)
                        pool.wait_ge(up_gated, i + 1)
                        G.tensor_tensor(zr[:, j, :], tC[:, j - 1, :], tB[:, j, :], ALU.mult).then_inc(up_h, 1)

                    def product_lo(j):
                        i = it * 2 + (t0 + j // 2)
                        pool.wait_ge(up_h, i + 1)
                        pool.wait_ge(up_hi, i + 1)
                        G.tensor_tensor(part(H, it * 2 + j // 2, 1), zr[:, j, :], part(H, it * 2 + j // 2, 0).bitcast(F32),
                                        ALU.subtract).then_inc(up_ready, 1)
                    preact(0)
                    preact(1)
                    gated(0)
                    preact(2)
                    product(1)
                    preact(3)
                    product_lo(1)
                    gated(2)
                    product(3)
                    product_lo(3)
                if n == CH:
                    with pool.Fori(0, 4) as it:
                        for j in range(4):
                            t = it * 4 + j
                            take(it * 4 + UB[dn], ZB[dn], j,
                                 (lambda zz: G.tensor_copy(tile(y, t), zz)) if c == 0 else
                                 (lambda zz: G.tensor_tensor(tile(y, t), tile(y, t), zz, ALU.add)))
                else:
                    for j in range(DT):
                        take(UB[dn], ZB[dn], j, lambda zz: G.tensor_tensor(y[:, j, :], y[:, j, :], zz, ALU.add))
                        pool.wait_ge(dn_sq, j + 1)
                        add_acc(acc[:, :], sq[:, j % 4, :], ACC0["end"] + j)
                t0 += n
            with pool.Fori(0, 4) as it:
                for j in range(4):
                    t = it * 4 + j
                    pool.wait_ge(fin_t, t + 1)
                    G.tensor_tensor(tile(x, t), tile(x, t), tile(y, t), ALU.add).then_inc(fin_x, 1)


def tiled(w):
    k, n = w.shape
    tiles = w.reshape(k // P, P, n // P, P).transpose(2, 0, 1, 3)
    return ordered(tiles)


def ordered(tiles):
    unit, kt = zip(*order(*tiles.shape[:2]))
    return tiles[list(unit), list(kt)]


def kernel(**inp):
    import concourse.bacc as bacc
    from concourse import mybir
    from concourse.bass_utils import run_bass_kernel_spmd

    f = np.float32
    a = {k: np.asarray(v) for k, v in inp.items()}

    w_in = a["nsa_w_in"][0]
    kvw = KVG * P
    cut = [D + i * kvw for i in range(7)]
    kc, vc, ks, vs, kw, vw = (w_in[:, cut[i]:cut[i + 1]] for i in range(6))

    def rows(w):
        k, n = w.shape
        return w.reshape(k // P, P, n // P, P).transpose(0, 2, 1, 3).reshape(-1, P, P)

    gates = w_in[:, cut[6]:].reshape(DT, P, KVG, HPG, 3).transpose(1, 0, 2, 4, 3).reshape(P, DT * 48)
    misc = np.concatenate([gates, a["nsa_cmp_w2_k"][0], a["nsa_cmp_w2_v"][0]], axis=1)
    stream = [tiled(kc), tiled(vc), tiled(ks), tiled(kw), tiled(w_in[:, :D]), rows(vs), rows(vw),
              tiled(a["nsa_cmp_w1_k"][0]), tiled(a["nsa_cmp_w1_v"][0]),
              misc.reshape(P, BLK, P).transpose(1, 0, 2), tiled(a["nsa_w_out"][0])]
    for c in range(FF_CHUNKS):
        h = slice(c * CH * P, (c + 1) * CH * P)
        stream += [tiled(a["ffn_w1"][0][:, h]), tiled(a["ffn_w2"][0][h])]
    stream += [tiled(a["ple_w_proj"][0]), tiled(a["ple_w_gate"][0])]
    swa = a["swa_w_in_2"][0]
    kv2 = SWA_KV * HD
    order = np.arange(SWA_HEADS * HD).reshape(PAIRS, 2, HPG, HD).transpose(0, 2, 1, 3).reshape(-1)
    stream += [tiled(swa[:, D:D + kv2]), rows(swa[:, D + kv2:]), tiled(swa[:, :D][:, order]), tiled(a["swa_w_out_2"][0][order])]
    up, down = a["ffn_w_up_2"][0], a["ffn_w_down_2"][0]
    both = up.reshape(DT, P, 2, FF2_T, P).transpose(3, 2, 0, 1, 4)
    t0 = 0
    for n in CHUNKS2:
        stream += [ordered(both[t0:t0 + n].reshape(2 * n, DT, P, P)), tiled(down[t0 * P:(t0 + n) * P])]
        t0 += n
    wstream = np.ascontiguousarray(np.concatenate(stream).reshape(NPIECE, BLK, P, P).transpose(0, 2, 1, 3)).reshape(NPIECE, P, PW)

    q = np.arange(P)
    causal = np.where(q[None, :] <= q[:, None], 0, NEG)
    tok = np.arange(S).reshape(QT, P, 1)
    n = np.arange(CS)
    valid = (n * CS + CL - 1 <= tok) & (n < NCMP)
    consts = np.concatenate([np.eye(P), np.zeros((P, P)), causal, np.where(valid, 0, NEG).transpose(1, 0, 2).reshape(P, -1),
                             valid.transpose(1, 0, 2).reshape(P, -1)], axis=1).astype(f)
    dist = 2 * P - 1 - np.arange(RB)
    near = np.clip(dist, 1, None)
    exact = NBUCK // 2
    far = np.minimum(exact + (np.log(near / exact) / np.log(MAXD / exact) * (NBUCK - exact)).astype(int), NBUCK - 1)
    bucket = np.where(dist < exact, np.maximum(dist, 0), far)
    onehot = (bucket[None, :] == np.arange(NBUCK)[:, None]).astype(f)
    band = np.broadcast_to(np.where((dist >= 0) & (dist < WIN), 0, NEG), (SWA_HEADS, RB)).astype(f)
    setup = np.concatenate([onehot, band, a["rel_bias_table_2"]], axis=1)

    def col(g):
        return g.reshape(-1, P).T

    conv = a["ffn_conv_2"][0].reshape(3, 2, FF2_T, P).transpose(3, 2, 1, 0).reshape(P, -1)
    g2 = a["norm_g_2"][0]
    params = np.concatenate([col(a["norm_mix"][0]), col(a["norm_ffn"][0]), col(a["norm_ple"][0]), col(a["norm_final"]),
                             col(g2[0]), col(g2[1]), col(g2[2]), col(g2[3]), conv, a["nsa_cmp_pos_k"][0].T,
                             a["nsa_cmp_pos_v"][0].T, np.broadcast_to(a["swa_sinks_2"][0], (P, SWA_HEADS))], axis=1)
    arrays = {
        "xT": a["x"][0].T.reshape(DT, P, S).transpose(1, 0, 2),
        "pT": a["p"][0, 0].T.reshape(2, P, S).transpose(1, 0, 2),
        "wstream": wstream, "consts": consts, "setup": setup, "params": params,
    }
    arrays = {k: np.ascontiguousarray(v) for k, v in arrays.items()}

    nc = bacc.Bacc("TRN2", target_bir_lowering=False, num_devices=1)
    F32 = mybir.dt.float32
    aps = [nc.dram_tensor(k, v.shape, F32, kind="ExternalInput").ap() for k, v in arrays.items()]
    out = nc.dram_tensor("out", (P, DT, S), F32, kind="ExternalOutput").ap()
    program(nc, *aps, out)
    r = run_bass_kernel_spmd(nc, [arrays], core_ids=[0])
    return np.ascontiguousarray(r.results[0]["out"].transpose(2, 1, 0)).reshape(1, S, D)
```

```python
from contextlib import ExitStack

import numpy as np

P = 128
S = 256
D = 2048
DT = D // P
QT = S // P
EPS = 1e-6
NEG = -1e30

HEADS, KVG, HPG = 16, 4, 4
CL, CS = 32, 16
NCMP = (S - CL) // CS + 1
NPAD = 32
NB = KVG * NCMP
D_FF = 8192
CH = 16
FF_CHUNKS = D_FF // P // CH
D_PLE = 256
SWA_HEADS, SWA_KV, HD = 32, 8, 64
WIN = 128
PAIRS = SWA_KV // 2
D_FF2 = 5632
FF2_T = D_FF2 // P
CHUNKS2 = [16, 16, 12]
NBUCK, MAXD = 32, 128
RB = 384
FIRST_SPLITS = [1, 3, 6, 9, 13, 17]
FIRST_LAG = 6
POST_SPLITS = [8, 11, 14, 17]
FIN_CHUNKS = [(0, 4), (4, 8), (8, 12), (12, 14), (14, 16)]
FIN_DVE = [3, 6, 9, 12, 15]
SLOTS = 4
LEAD = 3
AHEAD = LEAD + 2
BLK = 8
PW = BLK * P

STAGES = [("kv", 16, 16), ("q", 16, 16), ("cv", 4, 32), ("misc", 3, 2), ("vb", 2, 16), ("wo", 16, 16)]
for _c in range(FF_CHUNKS):
    if _c == FF_CHUNKS - 1:
        STAGES += [("proj", 16, 2)]
    STAGES += [(f"ff{_c}", CH, 16), (f"fd{_c}", 16, CH)]
STAGES += [("gate", 16, 16), ("k2", 4, 16), ("v2", 2, 16), ("q2", 16, 16), ("wo2", 16, 16)]
for _c, _n in enumerate(CHUNKS2):
    STAGES += [(f"up{_c}", 2 * _n, 16), (f"dn{_c}", 16, _n)]

PB, UB, ZB = {}, {}, {}
NZ = {"cv": 0, "vb": 0, "v2": 0, "misc": 1, "proj": 0, "wo2": 0, "dn0": 0, "dn2": 0}
_p = _u = _z = 0
for _name, _n, _k in STAGES:
    PB[_name], UB[_name], ZB[_name] = _p, _u, _z
    _blocks = _n * _k
    if _name in ("vb", "v2"):
        _blocks = _n // 2 * 4 * 16
    _p += 1 if _name == "misc" else _blocks // BLK
    _u += _n
    _z += NZ.get(_name, _n)
NPIECE = _p
UB["end"] = _u


def columns(widths):
    at, out = 0, {}
    for name, width in widths:
        out[name] = (at, at + width)
        at += width
    return out, at


CO, NCONST = columns([("ident", P), ("mask", 2 * P), ("cmask", QT * CS), ("cvalid", QT * CS), ("sel", NB)])
SO, NSETUP = columns([("onehot", RB), ("band", RB), ("table", SWA_HEADS)])
PO, NPAR = columns([("g_mix", DT), ("g_ffn", DT), ("g_ple", DT), ("g_fin", DT), ("g0", DT), ("g1", DT), ("g2", DT),
                    ("g3", DT), ("conv", 3 * 2 * FF2_T), ("pos_k", CL), ("pos_v", CL), ("sink", SWA_HEADS)])


def order(n, K):
    if not 8 < K <= 16:
        return [(j, k) for j in range(n) for k in range(K)]
    return [(j, k) for g in range(0, n, 4) for a, b in ((0, 4), (4, 8), (8, K)) for j in range(g, g + 4) for k in range(a, b)]


def ends(n, K):
    at = {}
    for b, (j, k) in enumerate(order(n, K)):
        if k == K - 1:
            at.setdefault(b // BLK, []).append(j)
    return at


def chunk_at(c):
    return (f"ff{c}", f"fd{c}", 0) if isinstance(c, int) else ("ff0", "fd0", c)


class Steps:

    def __init__(self, eng, sem, base=0):
        self.eng, self.sem, self.n = eng, sem, base

    def __call__(self, ins):
        self.n = self.n + 1
        ins.then_inc(self.sem, 1)
        self.eng.wait_ge(self.sem, self.n)


def program(nc, xT, pT, wstream, consts, setup, params, out):
    import concourse.bass as bass
    from concourse import mybir

    F32, FR = mybir.dt.float32, mybir.dt.float32r
    ALU, ACT = mybir.AluOpType, mybir.ActivationFunctionType
    AX = mybir.AxisListType.X
    ds = bass.ds

    bias_rows = nc.dram_tensor("bias_rows", [SWA_HEADS, P * RB], F32)

    with ExitStack() as ctx:
        def sb(name, shape, dt=F32):
            return ctx.enter_context(nc.sbuf_tensor(name, shape, dt))

        def sem(name):
            return ctx.enter_context(nc.semaphore(name))

        raw = sb("raw", [P, SLOTS, PW])
        wboth = sb("wboth", [P, 2, SLOTS, PW], FR)
        whi, wlo = wboth[:, 0, :, :], wboth[:, 1, :, :]
        x = sb("x", [P, DT, S])
        A = sb("A", [P, DT, 2, S], FR)
        H = sb("H", [P, CH, 2, S], FR)
        pA = sb("pA", [P, 2, 2, S], FR)
        y = sb("y", [P, DT, S])
        kT = sb("kT", [P, 2, KVG, S])
        vN = sb("vN", [P, 2 * QT, 4 * P])
        z = sb("z", [P, 4, S])
        Sm = sb("Sm", [P, 3 * 8 * P])
        PT = sb("PT", [P, QT, 8, P])
        bias = sb("bias", [P, 3, 4, 2 * P])
        con = sb("con", [P, NCONST])
        par = sb("par", [P, NPAR])
        ones = sb("ones", [P, P])
        scratch = sb("scratch", [P, 1])
        acc = sb("acc", [P, S])
        rs = sb("rs", [P, S])
        rcol = sb("rcol", [P, QT])
        gg = sb("gg", [P, DT])
        gts = sb("gts", [P, QT, 3 * HEADS])
        small = sb("small", [P, 6, 16])
        psum = [ctx.enter_context(nc.psum_tensor(f"bank{i}", [P, 512], F32)) for i in range(8)]

        bflat = bias[:, :, :, :].rearrange("p m a b -> p (m a b)")
        ptf = PT[:, :, :, :].rearrange("p a b c -> p (a b c)")

        def ring(flat, a, n=4, w=S):
            return flat[:, a:a + n * w].rearrange("p (n w) -> p n w", n=n)

        zr, sq = ring(bflat, 0), ring(bflat, 4 * S, 8)
        tA, tB, tC = ring(Sm, 0), ring(Sm, 4 * S), ring(Sm, 8 * S)
        ub, c0 = ring(ptf, 0, 4, S + 4), ring(ptf, 4 * (S + 4), 2)
        sq2 = ring(ptf, 0)
        acc2, rs2, rs3 = tC[:, 0, :], tC[:, 1, :], tC[:, 2, :]
        csig, ch = tC[:, 3, 0:128], tC[:, 3, 128:256]
        pcT = bflat[:, 0:1024].rearrange("p (t r q) -> p t r q", t=QT, r=HPG)
        vczall = bflat[:, 1024:1536].rearrange("p (g d) -> p g d", g=KVG)
        kcmp = bflat[:, 1664:1792]
        cs = bflat[:, 1792:1920].rearrange("p (a b) -> p a b", a=8)
        kvc = Sm[:, 0:2048].rearrange("p (b g t) -> p b g t", b=2, g=KVG)
        blkf = ptf[:, 0:CL * KVG * NCMP].rearrange("p (l g n) -> p l g n", l=CL, g=KVG)
        blks = H[:, :, :, :].rearrange("p a b c -> p (a b c)")[:, 0:2 * CL * 2 * NB].rearrange(
            "p (b l h c) -> p b l h c", b=2, l=CL, h=2)
        cprob = Sm[:, 0:512].rearrange("p (t h n) -> p t h n", t=QT, h=HEADS)
        cpad = Sm[:, 1024:2048].rearrange("p (t r g n) -> p t r g n", t=QT, r=HPG, g=KVG)
        mx, nmx, sums, esk, tot, coef = (small[:, i, :] for i in range(6))
        csum = zr[0:2 * NB, 0:2, 0:P]
        gT = zr[0:3 * HEADS, 2, :]
        sel = con[0:2 * NB, CO["sel"][0]:CO["sel"][1]]
        ident = con[:, CO["ident"][0]:CO["ident"][1]]
        mask = con[:, CO["mask"][0]:CO["mask"][1]]
        cmask = con[:, CO["cmask"][0]:CO["cmask"][1]].rearrange("p (t n) -> p t n", t=QT)
        cvalid = con[:, CO["cvalid"][0]:CO["cvalid"][1]].rearrange("p (t n) -> p t n", t=QT)

        def gain(name, t):
            return par[:, ds(PO[name][0] + t, 1)]

        def tile(buf, t):
            return buf[:, ds(t, 1), :].rearrange("p a b -> p (a b)")

        def part(buf, t, h):
            return buf[:, ds(t, 1), h, :].rearrange("p a b -> p (a b)")

        raw_landed = [sem(f"raw_landed{i}") for i in range(SLOTS)]
        hi_ready, lo_ready = sem("hi_ready"), sem("lo_ready")
        piece_used = sem("piece_used")
        z_ready = sem("z_ready")
        z_used = sem("z_used")
        in_x = [sem(f"in_x{i}") for i in range(4)]
        in_c, in_k, in_p, in_s = sem("in_c"), sem("in_k"), sem("in_p"), sem("in_s")
        ones_set, gg_ready, pad_zero = sem("ones_set"), sem("gg_ready"), sem("pad_zero")
        table_sum, table_row, rows_out = (sem(n) for n in ("table_sum", "table_row", "rows_out"))
        x0_hi, a0_ready, x0_sq = sem("x0_hi"), sem("a0_ready"), sem("x0_sq")
        p_hi, p_ready = sem("p_hi"), sem("p_ready")
        acc_step = sem("acc_step")
        acc2_step = sem("acc2_step")
        acc_zero = sem("acc_zero")
        sum_ready, sum_step, var_ready, root_ready, rs_ready = (
            sem(n) for n in ("sum_ready", "sum_step", "var_ready", "root_ready", "rs_ready"))
        rs_turned, rcol_ready = sem("rs_turned"), sem("rcol_ready")
        blk_step, blk_hi, blk_ready = sem("blk_step"), sem("blk_hi"), sem("blk_ready")
        ch_sum, csig_ready, ch_ready, ch_hi, h1_ready = (
            sem(n) for n in ("ch_sum", "csig_ready", "ch_ready", "ch_hi", "h1_ready"))
        gate_sum, gates_turned, gates_ready, kcmp_ready, vcmp_ready = (
            sem(n) for n in ("gate_sum", "gates_turned", "gates_ready", "kcmp_ready", "vcmp_ready"))
        vcz_zero, cpad_zero, c_scores, c_step, c_shift, c_exp, cp_ready, c_turned, pcT_ready = (
            sem(n) for n in ("vcz_zero", "cpad_zero", "c_scores", "c_step", "c_shift", "c_exp", "cp_ready", "c_turned", "pcT_ready"))
        att = {k: {n: sem(f"{k}_{n}") for n in (
            "scores", "max", "step", "shift", "sinkdiff", "exp", "sinkexp", "scaled",
            "turned", "pt_act", "pt_dve", "o_done", "o_hi", "o_ready")} for k in ("nsa", "swa")}
        bias_in = [sem(f"bias_in{i}") for i in range(3)]
        wo_hi, wo_sq, a1_ready = sem("wo_hi"), sem("wo_sq"), sem("a1_ready")
        ff_relu, ff_hi, ff_step, ff_ready = sem("ff_relu"), sem("ff_hi"), sem("ff_step"), sem("ff_ready")
        fd_hi, fd_sq, a2_ready = sem("fd_hi"), sem("fd_sq"), sem("a2_ready")
        ple_sig, ple_step, ple_x, ple_hi, ple_sq, a3_ready = (
            sem(n) for n in ("ple_sig", "ple_step", "ple_x", "ple_hi", "ple_sq", "a3_ready"))
        xn_ready = sem("xn_ready")
        wo2_sq = sem("wo2_sq")
        post_t, post_x, post_hi, post_sq, a4_ready = (sem(n) for n in ("post_t", "post_x", "post_hi", "post_sq", "a4_ready"))
        up_c0, up_step, up_conv, up_sig, up_gated, up_h, up_hi, up_ready = (
            sem(n) for n in ("up_c0", "up_step", "up_conv", "up_sig", "up_gated", "up_h", "up_hi", "up_ready"))
        dn_sq = sem("dn_sq")
        fin_t, fin_x, fin_y, out_done = sem("fin_t"), sem("fin_x"), sem("fin_y"), sem("out_done")

        NORMS = ["kv", "ff0", "gate", "k2", "post", "up0", "end"]
        NACC = {"up0": DT // 2}
        ACC0 = {n: sum(NACC.get(m, DT) for m in NORMS[:i]) for i, n in enumerate(NORMS)}
        ACC2 = {"k2": DT + 1, "up0": DT + DT // 2 + 1}
        NORM_AT = {"kv": 6, "ff0": 1, "gate": 3, "k2": 3, "up0": 7}

        BLOCKS = [(0, 0, 8), (1, 0, 4), (1, 4, 8)]
        NBLOCK = 3 * KVG

        def att_block(n):
            t, e0, e1 = BLOCKS[n % 3]
            return n // 3, t, e0, e1, Sm[:, n % 3 * 8 * P:(n % 3 + 1) * 8 * P].rearrange("p (e k) -> p e k", e=e1 - e0)

        def score_bank(n, t, i):
            per = 4 // (t + 1)
            w = (t + 1) * P
            c = i % per * w
            return i // per, i % per == 0, i % per == per - 1, psum[(1 + 2 * (n % 2) + i // per) % 4][:, c:c + w]

        def turned_to(n, b):
            t, e0, e1 = BLOCKS[n % 3]
            return PT[:, 0, 4 * b:4 * b + 4, :] if t == 0 else PT[:, b, e0:e1, :]

        def o_parts(nsa, t):
            if nsa:
                return [(slice(0, P), psum[4 + t])]
            return [(slice(h * HD, h * HD + HD), psum[4 + h]) for h in range(2)]

        block = ctx.enter_context(nc.Block())

        @block.sync
        def _(sp):
            sp.dma_start(par[:, :], params).then_inc(in_c, 16)
            for i in range(4):
                sp.dma_start(x[:, 4 * i:4 * i + 4, :], xT[:, 4 * i:4 * i + 4, :]).then_inc(in_x[i], 16)
                sp.dma_start(raw[:, i, :], wstream[i]).then_inc(raw_landed[i], 16)
            sp.dma_start(con[:, :], consts).then_inc(in_k, 16)

            def load(i, s):
                sp.wait_ge(lo_ready, i - SLOTS + 1)
                sp.dma_start(raw[:, s, :], wstream[ds(i, 1)].rearrange("a p n -> p (a n)")).then_inc(raw_landed[s], 16)

            with sp.Fori(0, NPIECE // SLOTS - 1) as it:
                for j in range(SLOTS):
                    load(it * SLOTS + (SLOTS + j), j)
            for i in range(NPIECE // SLOTS * SLOTS, NPIECE):
                sp.wait_ge(lo_ready, i - SLOTS + 1)
                sp.dma_start(raw[:, i % SLOTS, :], wstream[i]).then_inc(raw_landed[i % SLOTS], 16)
            for a, b in FIN_CHUNKS:
                sp.wait_ge(fin_x, sum(t not in FIN_DVE for t in range(b)))
                sp.wait_ge(fin_y, sum(t in FIN_DVE for t in range(b)))
                sp.dma_start(out[:, a:b, :], x[:, a:b, :]).then_inc(out_done, 16)
            sp.wait_ge(out_done, 16 * len(FIN_CHUNKS))

        @block.tensor
        def _(pe):
            pe.sem_inc(piece_used, SLOTS)

            def units(p, p0, u, u0, n, K, moving, ready=None, between={}, narrow=False):
                for b, (j, k) in enumerate(order(n, K)):
                    s = (p0 + b // BLK) % SLOTS
                    if b % BLK == 0:
                        pe.wait_ge(lo_ready, p + (b // BLK + 1))
                    if k == 0:
                        pe.wait_ge(z_ready, u + (j - 3 if narrow and j >= 4 else j + 1))
                    if ready and j == 0:
                        pe.wait_ge(*ready(k))
                    bank = psum[(u0 + j) % 4 + (j // 4 % 2 * 4 if narrow else 0)]
                    w = slice(b % BLK * P, b % BLK * P + P)
                    m = moving(j, k)

                    if narrow:
                        nc.tensor.matmul(bank[:, 0:S], whi[:, s, w], m[:, 0, :], start=(k == 0), stop=False)
                        nc.tensor.matmul(bank[:, 0:S], whi[:, s, w], m[:, 1, :], start=False, stop=False)
                        last = nc.tensor.matmul(bank[:, 0:S], wlo[:, s, w], m[:, 0, :], start=False, stop=(k == K - 1))
                        if b % BLK == BLK - 1:
                            last.then_inc(piece_used, 1)
                        continue

                    def lo():
                        return nc.tensor.matmul(bank[:, 0:S], wlo[:, s, w], m[:, 0, :], start=False, stop=False)
                    if k == K - 1:
                        lo()
                    last = nc.tensor.matmul(bank[:, :], whi[:, s, w], m, start=(k == 0), stop=(k == K - 1))
                    if k < K - 1:
                        last = lo()
                    if b % BLK == BLK - 1:
                        last.then_inc(piece_used, 1)
                        if b // BLK in between:
                            between[b // BLK]()

            def norm(name, bank=4, parts=(acc[:, :],)):
                pe.wait_ge(acc_step, ACC0[name] + NACC.get(name, DT))
                if acc2 in parts:
                    pe.wait_ge(acc2_step, ACC2[name])
                for i, src in enumerate(parts):
                    last = nc.tensor.matmul(psum[bank][:, 0:S], ones[:, :], src, start=(i == 0), stop=(i == len(parts) - 1))
                last.then_inc(sum_ready, 1)

            def turn_rs(i):
                pe.wait_ge(rs_ready, i)
                for t in range(QT):
                    last = nc.tensor.transpose(psum[6][:, t * P:t * P + P], rs[:, t * P:t * P + P], ident)
                last.then_inc(rs_turned, 1)

            def natural(p, u, src, between={}, pitch=1):
                for t in range(QT):
                    pe.wait_ge(z_ready, u + t + 1)
                for k in range(DT):
                    if k in between:
                        between[k]()
                    if k % 2 == 0:
                        pe.wait_ge(lo_ready, p + k // 2 * pitch + 1)
                    s, w = (p + k // 2 * pitch) % SLOTS, slice(k % 2 * 512, k % 2 * 512 + 512)
                    for t in range(QT):
                        tok = slice(t * P, t * P + P)
                        bank = psum[(u + t) % 4]
                        nc.tensor.matmul(bank[:, :], src[:, k, 0, tok], whi[:, s, w], start=(k == 0), stop=False)
                        nc.tensor.matmul(bank[:, :], src[:, k, 0, tok], wlo[:, s, w], start=False, stop=False)
                        last = nc.tensor.matmul(bank[:, :], src[:, k, 1, tok], whi[:, s, w], start=False, stop=(k == DT - 1))
                    if k % 2 == 1:
                        last.then_inc(piece_used, 1)

            def attention(kind, begin=True, rest=True):
                sm = att[kind]
                nsa = kind == "nsa"

                def scores(n):
                    g, t, e0, e1, _ = att_block(n)
                    nk = (t + 1) * P
                    if n >= 2:
                        pe.wait_ge(sm["shift"], n - 1)
                    for e in range(e0, e1):
                        _, _, full, bank = score_bank(n, t, e - e0)
                        if nsa:
                            lhs, rhs = y[:, HPG * g + e % 4, t * P:t * P + P], kT[:, e // 4, g, 0:nk]
                        else:
                            h = slice(e // 4 * HD, e // 4 * HD + HD)
                            lhs, rhs = y[h, HPG * g + e % 4, t * P:t * P + P], kT[h, 0, g, 0:nk]
                        last = nc.tensor.matmul(bank, lhs, rhs, start=True, stop=True)
                        if full:
                            last.then_inc(sm["scores"], 1)

                def turn(n):
                    _, t, _, _, probs = att_block(n)
                    pe.wait_ge(sm["scaled"], n + 1)
                    for b in range(2):
                        if n:
                            pe.wait_ge(sm["pt_dve" if b else "pt_act"], n)
                        for i in range(4):
                            src = probs[:, 4 * b + i, :] if t == 0 else probs[:, i, b * P:b * P + P]
                            last = nc.tensor.transpose(psum[6 + b][:, i * P:i * P + P], src, ident)
                        last.then_inc(sm["turned"], 1)

                def output(n):
                    g, t, _, _, _ = att_block(n)
                    before = 2 * g + t - (1 if nsa else 0)
                    if before > 0:
                        pe.wait_ge(sm["o_ready"], before)
                    pe.wait_ge(sm["pt_act"], n + 1)
                    pe.wait_ge(sm["pt_dve"], n + 1)
                    v = slice(g * P, g * P + P)
                    if nsa:
                        steps = [(vN[:, b * QT + kt, v], PT[:, kt, 4 * b:4 * b + 4, :]) for b in range(2) for kt in range(t + 1)]
                        steps.append((vczall[:, g, :], pcT[:, t, :, :]))
                        for i, (lhs, rhs) in enumerate(steps):
                            last = nc.tensor.matmul(psum[4 + t][:, :], lhs, rhs, start=(i == 0), stop=(i == len(steps) - 1))
                    else:
                        for half in range(2):
                            for kt in range(t + 1):
                                last = nc.tensor.matmul(psum[4 + half][:, :], vN[:, kt, v], PT[:, kt, 4 * half:4 * half + 4, :],
                                                        start=(kt == 0), stop=(kt == t))
                    last.then_inc(sm["o_done"], 1)

                if begin:
                    scores(0)
                if not rest:
                    return
                scores(1)
                scores(2)
                for n in range(NBLOCK):
                    turn(n)
                    if n + 3 < NBLOCK:
                        scores(n + 3)
                    if n % 3 != 1:
                        output(n)

            pe.wait_ge(in_s, 16)
            nc.tensor.matmul(psum[7][0:SWA_HEADS, 0:RB], bflat[0:NBUCK, SO["table"][0]:SO["table"][1]],
                             bflat[0:NBUCK, SO["onehot"][0]:SO["onehot"][1]], start=True, stop=True).then_inc(table_sum, 1)
            pe.wait_ge(ones_set, 1)

            def project(st, it, **more):
                units(it * 8 + PB[st], PB[st], it * 4 + UB[st], UB[st], 4, DT, lambda j, k: A[:, k, :, :],
                      (lambda k: (a0_ready, k + 1)) if st == "kv" else None, **more)
            project("kv", 0, between={NORM_AT["kv"]: lambda: norm("kv")})
            with pe.Fori(1, 4) as it:
                project("kv", it)
            pe.wait_ge(in_k, 16)
            turn_rs(1)
            with pe.Fori(0, 4) as it:
                project("q", it)
            def compress(i):
                b, l0 = divmod(i * BLK, CL)
                piece = PB["cv"] + 2 * i
                pe.wait_ge(lo_ready, piece + 1)
                if l0 == 0:
                    pe.wait_ge(blk_ready, b + 1)
                    pe.wait_ge(z_ready, UB["cv"] + b + 1)
                for j in range(BLK):
                    last = nc.tensor.matmul(psum[(UB["cv"] + b) % 4][0:2 * NB, 0:2 * P],
                                            blks[:, b, l0 + j, :, :].rearrange("p h c -> p (h c)"),
                                            wboth[:, :, piece % SLOTS, j * P:j * P + P],
                                            start=(l0 + j == 0), stop=(l0 + j == CL - 1))
                last.then_inc(piece_used, 1)
            natural(PB["cv"] + 1, UB["cv"] + 2, A, {2 * i: lambda i=i: compress(i) for i in range(2 * CL // BLK)}, pitch=2)

            pe.wait_ge(z_ready, 4 + UB["cv"] + 2)
            for b in range(2):
                last = nc.tensor.matmul(psum[6][:, b * 64:b * 64 + NB], csum[:, b, :], sel, start=True, stop=True)
            last.then_inc(ch_sum, 1)
            p, u = PB["misc"], UB["misc"]
            s = p % SLOTS
            pe.wait_ge(lo_ready, p + 1)
            pe.wait_ge(z_ready, u + 1)
            bank = psum[u % 4][0:3 * HEADS, :]
            for k in range(DT):
                w = slice(k * 3 * HEADS, (k + 1) * 3 * HEADS)
                if k:
                    nc.tensor.matmul(bank[:, 0:S], wlo[:, s, w], A[:, k, 0, :], start=False, stop=False)
                last = nc.tensor.matmul(bank, whi[:, s, w], A[:, k, :, :], start=(k == 0), stop=(k == DT - 1))
                if not k:
                    nc.tensor.matmul(bank[:, 0:S], wlo[:, s, w], A[:, k, 0, :], start=False, stop=False)
            last.then_inc(gate_sum, 1)
            wk, wv = slice(DT * 3 * HEADS, DT * 3 * HEADS + P), slice(DT * 3 * HEADS + P, DT * 3 * HEADS + 2 * P)
            pe.wait_ge(h1_ready, 2)
            pe.wait_ge(z_ready, u + 2)
            bank = psum[(u + 1) % 4][:, 0:P]
            nc.tensor.matmul(bank, whi[:, s, wk], pA[:, 0, 0, 0:P], start=True, stop=False)
            nc.tensor.matmul(bank, wlo[:, s, wk], pA[:, 0, 0, 0:P], start=False, stop=False)
            nc.tensor.matmul(bank, whi[:, s, wk], pA[:, 0, 1, 0:P], start=False, stop=True).then_inc(gate_sum, 1)
            pe.wait_ge(z_ready, u + 3)
            bank = psum[(u + 2) % 4][:, 0:P]
            nc.tensor.matmul(bank, pA[:, 1, 0, 0:P], whi[:, s, wv], start=True, stop=False)
            nc.tensor.matmul(bank, pA[:, 1, 0, 0:P], wlo[:, s, wv], start=False, stop=False)
            nc.tensor.matmul(bank, pA[:, 1, 1, 0:P], whi[:, s, wv], start=False, stop=True).then_inc(piece_used, 1)

            def gates_and_scores():
                pe.wait_ge(z_used, 4 + ZB["misc"] + 1)
                for t in range(QT):
                    last = nc.tensor.transpose(psum[7][:, t * 3 * HEADS:(t + 1) * 3 * HEADS], gT[:, t * P:t * P + P],
                                               ident[0:3 * HEADS, 0:3 * HEADS])
                last.then_inc(gates_turned, 1)
                pe.wait_ge(kcmp_ready, 1)
                for t in range(QT):
                    for h in range(HEADS):
                        g = h // HPG
                        last = nc.tensor.matmul(psum[4 + t][:, h * CS:h * CS + CS], y[:, h, t * P:t * P + P],
                                                kcmp[:, g * NPAD:g * NPAD + CS], start=True, stop=True)
                    last.then_inc(c_scores, 1)

            def turn_c():
                for t in range(QT):
                    pe.wait_ge(cp_ready, t + 1)
                    for r in range(HPG):
                        last = nc.tensor.transpose(psum[6 + t][:, r * P:r * P + P],
                                                   cpad[:, t, r, :, :].rearrange("p g n -> p (g n)"), ident)
                    last.then_inc(c_turned, 1)
            natural(PB["vb"], UB["vb"], A, {2: gates_and_scores, 10: lambda: attention("nsa", rest=False), 14: turn_c})
            pe.wait_ge(z_ready, 4 + UB["wo"])
            pe.wait_ge(pcT_ready, QT)
            attention("nsa", begin=False)
            with pe.Fori(0, 4) as it:
                units(it * 8 + PB["wo"], PB["wo"], it * 4 + UB["wo"], UB["wo"], 4, DT, lambda j, k: H[:, k, :, :],
                      lambda k: (att["nsa"]["o_ready"], k // HPG * 2 + 2))

            def hidden(c, it, **more):
                ff, _, o = chunk_at(c)
                units(o * 64 + it * 8 + PB[ff], PB[ff], o * 32 + it * 4 + UB[ff], UB[ff], 4, DT,
                      lambda j, k: A[:, k, :, :], lambda k: (a1_ready, k + 1), **more)

            def chunk(c, first=0):
                _, fd, o = chunk_at(c)
                with pe.Fori(first, 4) as it:
                    hidden(c, it)
                with pe.Fori(0, 4) as it:
                    units(o * 64 + it * 8 + PB[fd], PB[fd], o * 32 + it * 4 + UB[fd], UB[fd], 4, CH,
                          lambda j, k: H[:, k, :, :], lambda k: (ff_ready, c * CH + (k + 1)))
            hidden(0, 0, between={NORM_AT["ff0"]: lambda: norm("ff0")})
            chunk(0, 1)
            with pe.Fori(1, FF_CHUNKS - 1) as c:
                chunk(c)
            pe.wait_ge(p_ready, 2)
            units(PB["proj"], PB["proj"], UB["proj"], UB["proj"], DT, 2, lambda j, k: pA[:, k, :, :], narrow=True)
            chunk(FF_CHUNKS - 1)

            def gate(it, **more):
                units(it * 8 + PB["gate"], PB["gate"], it * 4 + UB["gate"], UB["gate"], 4, DT, lambda j, k: A[:, k, :, :],
                      lambda k: (a2_ready, k + 1), **more)
            gate(0, between={NORM_AT["gate"]: lambda: norm("gate")})
            with pe.Fori(1, 4) as it:
                gate(it)

            def norms_k2():
                norm("k2")
                norm("k2", 5, (acc2,))
            units(PB["k2"], PB["k2"], UB["k2"], UB["k2"], 4, DT, lambda j, k: H[:, k, :, :], lambda k: (a3_ready, k + 1),
                  between={NORM_AT["k2"]: norms_k2})
            turn_rs(5)
            natural(PB["v2"], UB["v2"], H)
            with pe.Fori(0, 4) as it:
                units(it * 8 + PB["q2"], PB["q2"], it * 4 + UB["q2"], UB["q2"], 4, DT, lambda j, k: H[:, k, :, :])
            pe.wait_ge(z_ready, 4 + UB["wo2"])
            pe.wait_ge(z_used, 4 + ZB["wo2"])
            attention("swa")
            with pe.Fori(0, 4) as it:
                units(it * 8 + PB["wo2"], PB["wo2"], it * 4 + UB["wo2"], UB["wo2"], 4, DT, lambda j, k: H[:, k, :, :],
                      lambda k: (att["swa"]["o_ready"], k // HPG * 2 + 2))
            norm("post")

            t0 = 0
            for c, n in enumerate(CHUNKS2):
                up, dn = f"up{c}", f"dn{c}"

                def hidden2(it, **more):
                    units(it * 8 + PB[up], PB[up], it * 4 + UB[up], UB[up], 4, DT, lambda j, k: A[:, k, :, :],
                          lambda k: (a4_ready, k + 1), **more)
                if c == 0:
                    hidden2(0, between={NORM_AT["up0"]: lambda: norm("up0", parts=(acc[:, :], acc2))})
                with pe.Fori(1 if c == 0 else 0, n // 2) as it:
                    hidden2(it)
                if n == CH:
                    with pe.Fori(0, 4) as it:
                        units(it * 8 + PB[dn], PB[dn], it * 4 + UB[dn], UB[dn], 4, n, lambda j, k: H[:, k, :, :],
                              lambda k: (up_ready, t0 + k + 1))
                else:
                    for it in range(2):
                        units(it * n + PB[dn], PB[dn], it * 8 + UB[dn], UB[dn], 8, n, lambda j, k: H[:, k, :, :],
                              lambda k: (up_ready, t0 + k + 1))
                t0 += n
            norm("end")

        @block.vector
        def _(dve):
            V = nc.vector
            dve.sem_inc(z_ready, 4)

            def split_lo(i, s):
                dve.wait_ge(hi_ready, i + 1)
                V.tensor_tensor(wlo[:, s, :], raw[:, s, :], whi[:, s, :].bitcast(F32), ALU.subtract).then_inc(lo_ready, 1)

            def body(p, p0, u, u0, zu, z0, n, K, late=None, lag=1, skip=0, short=0, between={}, dst=None, narrow=False, add=False,
                     hold=0):
                at = ends(n, K)
                count = n * K // BLK
                for q in range(LEAD, count + AHEAD):
                    if AHEAD + skip <= q < count + AHEAD - short:
                        split_lo(p + q, (p0 + q) % SLOTS)
                    if q - LEAD - 1 in between:
                        between[q - LEAD - 1]()
                    if late:
                        for j in at.get(q - LEAD - lag - hold, []):
                            if hold == 0 or j < 4:
                                late(j)
                        for j in at.get(q - LEAD - lag, []):
                            if hold and j >= 4:
                                late(j)
                    for j in at.get(q - LEAD, []):
                        dve.wait_ge(piece_used, p + (SLOTS + q - LEAD + 1))
                        if not dst:
                            dve.wait_ge(z_used, zu + (j + 1))
                        if add:
                            bank = psum[(u0 + j) % 4]
                            steps(V.tensor_tensor(dst(j), dst(j), bank[:, 0:S], ALU.add))
                            V.tensor_tensor(dst(j), dst(j), bank[:, S:2 * S], ALU.add).then_inc(z_ready, 1)
                            continue
                        if narrow:
                            V.tensor_copy(dst(j), psum[(u0 + j) % 4 + j // 4 % 2 * 4][:, 0:S]).then_inc(z_ready, 1)
                            continue
                        V.tensor_reduce(dst(j) if dst else z[:, (z0 + j) % 4, :],
                                        psum[(u0 + j) % 4][:, :].rearrange("p (h c) -> p c h", h=2), AX, ALU.add).then_inc(z_ready, 1)

            steps = Steps(dve, sum_step)

            def rsqrt(dst, var, n):
                dve.wait_ge(root_ready, n)
                steps(V.reciprocal(dst, dst))
                steps(V.scalar_tensor_tensor(var, var, -0.5, dst, ALU.mult, ALU.mult))
                steps(V.tensor_tensor(var, var, dst, ALU.mult))
                return V.scalar_tensor_tensor(dst, var, 1.5, dst, ALU.add, ALU.mult)

            def norm(dst, n):
                dve.wait_ge(sum_ready, n)
                V.tensor_scalar(acc[:, :], psum[4][:, 0:S], 1.0 / D, EPS, ALU.mult, ALU.add).then_inc(var_ready, 1)
                dve.wait_ge(var_ready, n)
                return rsqrt(dst, acc[:, :], n)

            def columns_of_rs(n):
                dve.wait_ge(rs_turned, n)
                V.tensor_copy(rcol[:, :], psum[6][:, 0:QT * P].rearrange("p (t c) -> p t c", t=QT)[:, :, 0]).then_inc(rcol_ready, 1)
                dve.wait_ge(rcol_ready, n)

            def take_values(pieces, u, v0):
                dve.wait_ge(piece_used, SLOTS + pieces)
                for t in range(QT):
                    V.tensor_scalar(vN[:, v0 + t, :], psum[(u + t) % 4][:, :], rcol[:, t:t + 1], None,
                                    ALU.mult).then_inc(z_ready, 1)

            def values(p, u, v0, between={}, short=0):
                for q in range(AHEAD, 8 + AHEAD - short):
                    split_lo(p + q, (p + q) % SLOTS)
                    if q in between:
                        between[q]()
                    if q == 7 + LEAD:
                        take_values(p + 8, u, v0)

            def norm_lo(dst, name, hi_sem, ready):
                def late(t, i):
                    dve.wait_ge(hi_sem, i + 1)
                    V.scalar_tensor_tensor(part(dst, t, 1), tile(x, t), gain(name, t) if name else gg[:, ds(t, 1)],
                                           part(dst, t, 0).bitcast(F32), ALU.mult, ALU.subtract).then_inc(ready, 1)
                return late

            def attention(kind, begin=True, rest=True):
                sm = att[kind]
                nsa = kind == "nsa"
                st = Steps(dve, sm["step"])

                def maxima(n):
                    g, t, e0, e1, probs = att_block(n)
                    c = slice(8 * t + e0, 8 * t + e1)
                    if not nsa and t == 0:
                        for m in (2 * g, 2 * g + 1):
                            dve.wait_ge(bias_in[m % 3], m // 3 * 16 + 16)
                    for e in range(e0, e1):
                        i, first, _, bank = score_bank(n, t, e - e0)
                        add = mask if nsa else bias[:, (2 * g + e // 4) % 3, e % 4, :]
                        if first:
                            dve.wait_ge(sm["scores"], 2 * n + i + 1)
                        V.tensor_tensor_reduce(probs[:, e - e0, :], bank, add[:, (1 - t) * P:], 1.0, -3e38, ALU.add, ALU.max,
                                               mx[:, 8 * t + e:8 * t + e + 1]).then_inc(sm["max"], 1)
                    dve.wait_ge(sm["max"], 16 * g + 8 * t + e1)
                    if nsa:
                        V.tensor_scalar(nmx[:, c], mx[:, c], -1.0, None, ALU.mult).then_inc(sm["shift"], 1)
                    else:
                        sink = par[:, PO["sink"][0] + 8 * g + e0:PO["sink"][0] + 8 * g + e1]
                        st(V.tensor_tensor(mx[:, c], mx[:, c], sink, ALU.max))
                        V.tensor_scalar(nmx[:, c], mx[:, c], -1.0, None, ALU.mult).then_inc(sm["shift"], 1)
                        V.tensor_tensor(esk[:, c], sink, mx[:, c], ALU.subtract).then_inc(sm["sinkdiff"], 1)

                def scale(n):
                    g, t, e0, e1, probs = att_block(n)
                    c = slice(8 * t + e0, 8 * t + e1)
                    dve.wait_ge(sm["exp"], n + 1)
                    if nsa:
                        st(V.reciprocal(tot[:, c], sums[:, c]))
                        st(V.tensor_tensor(coef[:, c], gts[:, t, 12 * g + 4 + e0:12 * g + 4 + e1], tot[:, c], ALU.mult))
                    else:
                        dve.wait_ge(sm["sinkexp"], n + 1)
                        st(V.tensor_tensor(tot[:, c], sums[:, c], esk[:, c], ALU.add))
                        st(V.reciprocal(coef[:, c], tot[:, c]))
                    V.tensor_tensor(probs, probs, coef[:, c].unsqueeze(2).to_broadcast([P, e1 - e0, (t + 1) * P]),
                                    ALU.mult).then_inc(sm["scaled"], 1)

                def output_lo(n):
                    g, t, _, _, _ = att_block(n)
                    tok = slice(t * P, t * P + P)
                    dve.wait_ge(sm["o_hi"], 2 * g + t + 1)
                    for rows, bank in o_parts(nsa, t):
                        last = V.tensor_tensor(H[rows, HPG * g:HPG * g + HPG, 1, tok],
                                               bank[rows, :].rearrange("p (r q) -> p r q", r=HPG),
                                               H[rows, HPG * g:HPG * g + HPG, 0, tok].bitcast(F32), ALU.subtract)
                    last.then_inc(sm["o_ready"], 1)

                if begin:
                    maxima(0)
                if not rest:
                    return
                maxima(1)
                scale(0)
                maxima(2)
                for n in range(NBLOCK):
                    if n + 1 < NBLOCK:
                        scale(n + 1)
                    dve.wait_ge(sm["turned"], 2 * n + 2)
                    V.tensor_copy(turned_to(n, 1), psum[7][:, :].rearrange("p (e q) -> p e q", e=4)).then_inc(sm["pt_dve"], 1)
                    if n % 3 != 2 and n > 0:
                        output_lo(n - 1)
                    if n + 3 < NBLOCK:
                        maxima(n + 3)
                output_lo(NBLOCK - 1)

            dve.wait_ge(in_c, 16)
            V.tensor_tensor(gg[:, :], par[:, PO["g_fin"][0]:PO["g_fin"][1]], par[:, PO["g0"][0]:PO["g0"][1]],
                            ALU.mult).then_inc(gg_ready, 1)
            dve.wait_ge(table_sum, 1)
            V.tensor_tensor(bflat[0:NBUCK, 1024:1024 + RB], psum[7][0:SWA_HEADS, 0:RB],
                            bflat[0:NBUCK, SO["band"][0]:SO["band"][1]], ALU.add).then_inc(table_row, 1)
            for t in range(max(FIRST_SPLITS) + 1):
                if t < DT:
                    dve.wait_ge(x0_hi, t + 1)
                    V.scalar_tensor_tensor(A[:, t, 1, :], x[:, t, :], gain("g_mix", t), A[:, t, 0, :].bitcast(F32), ALU.mult,
                                           ALU.subtract).then_inc(a0_ready, 1)
                if t in FIRST_SPLITS:
                    i = FIRST_SPLITS.index(t)
                    split_lo(i, i % SLOTS)

            def first_norm():
                norm(rs[:, :], 1).then_inc(rs_ready, 1)
                dve.wait_ge(rs_ready, 1)
                V.tensor_scalar(rs2, rs[:, :], float(P) ** -0.5, None, ALU.mult).then_inc(rs_ready, 1)

            def project(st, it, **more):
                body(it * 8 + PB[st], PB[st], it * 4 + UB[st], UB[st], it * 4 + ZB[st], ZB[st], 4, DT, **more)
            project("kv", 0, skip=len(FIRST_SPLITS) - AHEAD, between={NORM_AT["kv"]: first_norm})
            with dve.Fori(1, 4) as it:
                project("kv", it)
            columns_of_rs(1)

            def blocks_c(b, pos):
                src = kvc[:, b, :, :].rearrange("p g (m s) -> p s g m", s=CS)
                for half in range(2):
                    emb = par[:, PO[pos][0] + CS * half:PO[pos][0] + CS * half + CS].unsqueeze(2).to_broadcast([P, CS, NCMP])
                    for g in range(KVG):
                        V.tensor_tensor(blkf[:, CS * half:CS * half + CS, g, :], src[:, :, g, half:half + NCMP], emb,
                                        ALU.add).then_inc(blk_step, 1)
                dve.wait_ge(blk_hi, b + 1)
                dve.wait_ge(blk_step, 8 * b + 8)
                V.tensor_tensor(blks[:, b, :, 1, :], blkf[:, :, :, :].rearrange("p l g n -> p l (g n)"),
                                blks[:, b, :, 0, :].bitcast(F32), ALU.subtract).then_inc(blk_ready, 1)
                dve.wait_ge(blk_ready, b + 1)
            dve.wait_ge(z_used, 4 + ZB["kv"] + 8)
            blocks_c(0, "pos_k")
            with dve.Fori(0, 2) as it:
                project("q", it)
            blocks_c(1, "pos_v")
            with dve.Fori(2, 4) as it:
                project("q", it)
            p, u = PB["cv"], UB["cv"]
            for q in range(AHEAD, 15 + AHEAD):
                split_lo(p + q, (p + q) % SLOTS)
                if q in (6 + LEAD, 14 + LEAD):
                    b = (q - LEAD) // 8
                    dve.wait_ge(piece_used, SLOTS + p + 8 * b + 7)
                    V.tensor_reduce(csum[:, b, :], psum[(u + b) % 4][0:2 * NB, 0:2 * P].rearrange("p (h f) -> p f h", h=2),
                                    AX, ALU.add).then_inc(z_ready, 1)
                if q == 15 + LEAD:
                    take_values(p + 16, u + 2, 0)

            def silu_c():
                dve.wait_ge(csig_ready, 1)
                for b in range(2):
                    c = slice(b * 64, b * 64 + NB)
                    last = V.tensor_tensor(ch[:, c], psum[6][:, c], csig[:, c], ALU.mult)
                last.then_inc(ch_ready, 1)

            def hidden_lo():
                for b in range(2):
                    dve.wait_ge(ch_hi, b + 1)
                    V.tensor_tensor(pA[:, b, 1, 0:P].rearrange("p (g n) -> p g n", g=KVG)[:, :, 0:NCMP],
                                    ch[:, b * 64:b * 64 + NB].rearrange("p (g n) -> p g n", g=KVG),
                                    pA[:, b, 0, 0:P].rearrange("p (g n) -> p g n", g=KVG)[:, :, 0:NCMP].bitcast(F32),
                                    ALU.subtract).then_inc(h1_ready, 1)
            silu_c()
            hidden_lo()
            p, u = PB["misc"], UB["misc"]
            dve.wait_ge(gate_sum, 1)
            dve.wait_ge(z_used, ZB["misc"] + 1)
            V.tensor_reduce(z[0:3 * HEADS, ZB["misc"] % 4, :], psum[u % 4][0:3 * HEADS, :].rearrange("p (h c) -> p c h", h=2),
                            AX, ALU.add).then_inc(z_ready, 1)
            dve.wait_ge(gate_sum, 2)
            V.tensor_copy(kcmp, psum[(u + 1) % 4][:, 0:P]).then_inc(kcmp_ready, 1)
            dve.wait_ge(kcmp_ready, 1)
            dve.sem_inc(z_ready, 1)
            dve.wait_ge(piece_used, SLOTS + p + 1)
            dve.wait_ge(vcz_zero, 1)
            for g in range(KVG):
                rows = slice(g * NPAD, g * NPAD + NPAD)
                V.tensor_copy(vczall[rows, g, :], psum[(u + 2) % 4][rows, 0:P]).then_inc(vcmp_ready, 1)
            dve.wait_ge(vcmp_ready, KVG)
            dve.sem_inc(z_ready, 1)
            for q in (AHEAD - 1, AHEAD):
                split_lo(p + q, (p + q) % SLOTS)
            st = Steps(dve, c_step)

            def shift_c():
                for t in range(QT):
                    c = cprob[:, t, :, :]
                    dve.wait_ge(c_scores, t + 1)
                    st(V.tensor_tensor(c, psum[4 + t][:, 0:HEADS * CS].rearrange("p (h n) -> p h n", h=HEADS),
                                       cmask[:, t, :].unsqueeze(1).to_broadcast([P, HEADS, CS]), ALU.add))
                    st(V.tensor_reduce(cs[:, t, :], c, AX, ALU.max))
                    V.tensor_tensor(c, c, cs[:, t, :].unsqueeze(2).to_broadcast([P, HEADS, CS]), ALU.subtract).then_inc(c_shift, 1)

            def probs_c():
                dve.wait_ge(gates_ready, 1)
                dve.wait_ge(cpad_zero, 1)
                for t in range(QT):
                    c = cprob[:, t, :, :]
                    dve.wait_ge(c_exp, t + 1)
                    st(V.tensor_reduce(cs[:, 2 + t, :], c, AX, ALU.add))
                    st(V.reciprocal(cs[:, 4 + t, :], cs[:, 2 + t, :]))
                    st(V.tensor_tensor(cs[:, 6 + t, :].rearrange("p (g r) -> p g r", g=KVG),
                                       cs[:, 4 + t, :].rearrange("p (g r) -> p g r", g=KVG),
                                       gts[:, t, :].rearrange("p (g b r) -> p g b r", g=KVG, b=3)[:, :, 0, :], ALU.mult))
                    st(V.tensor_tensor(c, c, cs[:, 6 + t, :].unsqueeze(2).to_broadcast([P, HEADS, CS]), ALU.mult))
                    for g in range(KVG):
                        last = V.tensor_tensor(cpad[:, t, :, g, 0:CS], c[:, HPG * g:HPG * g + HPG, :],
                                               cvalid[:, t, :].unsqueeze(1).to_broadcast([P, HPG, CS]), ALU.mult)
                    last.then_inc(cp_ready, 1)

            def begin_nsa():
                dve.wait_ge(cp_ready, QT)
                attention("nsa", rest=False)
            values(PB["vb"], UB["vb"], QT, {AHEAD: shift_c, AHEAD + 1: probs_c, AHEAD + 4: begin_nsa}, short=1)
            for t in range(QT):
                dve.wait_ge(c_turned, t + 1)
                V.tensor_copy(pcT[:, t, :, :], psum[6 + t][:, :].rearrange("p (r q) -> p r q", r=HPG)).then_inc(pcT_ready, 1)
            attention("nsa", begin=False)

            lo1 = norm_lo(A, "g_ffn", wo_hi, a1_ready)
            split_lo(PB["wo"] + 4, (PB["wo"] + 4) % SLOTS)
            with dve.Fori(0, 4) as it:
                body(it * 8 + PB["wo"], PB["wo"], it * 4 + UB["wo"], UB["wo"], it * 4 + ZB["wo"], ZB["wo"], 4, DT,
                     lambda j: lo1(it * 4 + j, it * 4 + j))

            def hidden(c, it, **more):
                ff, _, o = chunk_at(c)
                body(o * 64 + it * 8 + PB[ff], PB[ff], o * 32 + it * 4 + UB[ff], UB[ff], c * 32 + it * 4 + ZB["ff0"], ZB["ff0"],
                     4, DT, **more)

            def chunk(c, first=0, late=None):
                _, fd, o = chunk_at(c)
                with dve.Fori(first, 4) as it:
                    hidden(c, it)
                with dve.Fori(0, 4) as it:
                    body(o * 64 + it * 8 + PB[fd], PB[fd], o * 32 + it * 4 + UB[fd], UB[fd], c * 32 + it * 4 + ZB["fd0"], ZB["fd0"],
                         4, CH, (lambda j: late(it * 4 + j, it * 4 + j)) if late else None)
            hidden(0, 0, between={NORM_AT["ff0"]: lambda: norm(rs[:, :], 2).then_inc(rs_ready, 1)})
            for k in range(2):
                dve.wait_ge(p_hi, k + 1)
                V.tensor_tensor(pA[:, k, 1, :], tC[:, k, :], pA[:, k, 0, :].bitcast(F32), ALU.subtract).then_inc(p_ready, 1)
            chunk(0, 1)
            with dve.Fori(1, FF_CHUNKS - 1) as c:
                chunk(c)
            body(PB["proj"], PB["proj"], UB["proj"], UB["proj"], ZB["proj"], ZB["proj"], DT, 2,
                 dst=lambda j: y[:, j, :], narrow=True)
            chunk(FF_CHUNKS - 1, 0, norm_lo(A, "g_ple", fd_hi, a2_ready))
            lo3 = norm_lo(H, None, ple_hi, a3_ready)
            dve.sem_inc(acc2_step, 1)

            def next_lo(t, j):
                lo3(t, t)
                dve.wait_ge(ple_sq, t * 2 + 2)
                dve.wait_ge(acc2_step, t + 1)
                V.tensor_tensor(acc2, acc2, sq2[:, j, :], ALU.add).then_inc(acc2_step, 1)

            def gate(it, **more):
                body(it * 8 + PB["gate"], PB["gate"], it * 4 + UB["gate"], UB["gate"], it * 4 + ZB["gate"], ZB["gate"], 4, DT,
                     lambda j: next_lo(it * 4 + j, j), lag=2, **more)
            dve.wait_ge(acc_zero, 3)
            gate(0, between={NORM_AT["gate"]: lambda: norm(rs[:, :], 3).then_inc(rs_ready, 1)})
            with dve.Fori(1, 4) as it:
                gate(it)

            def norms_k2():
                steps(norm(rs3, 4))
                dve.wait_ge(sum_ready, 5)
                steps(V.scalar_tensor_tensor(acc2, psum[5][:, 0:S], 1.0 / D, rs3, ALU.mult, ALU.mult))
                steps(V.tensor_tensor(acc2, acc2, rs3, ALU.mult))
                V.tensor_scalar(acc2, acc2, EPS, None, ALU.add).then_inc(var_ready, 1)
                steps(rsqrt(rs[:, :], acc2, 5))
                V.tensor_tensor(rs[:, :], rs[:, :], rs3, ALU.mult).then_inc(rs_ready, 1)
                dve.wait_ge(rs_ready, 5)
                V.tensor_scalar(rs2, rs[:, :], float(HD) ** -0.5, None, ALU.mult).then_inc(rs_ready, 1)
            body(PB["k2"], PB["k2"], UB["k2"], UB["k2"], ZB["k2"], ZB["k2"], 4, DT, between={NORM_AT["k2"]: norms_k2})
            columns_of_rs(2)
            values(PB["v2"], UB["v2"], 0)

            def normed(t):
                V.scalar_tensor_tensor(tile(x, t), tile(x, t), gain("g_fin", t), rs3, ALU.mult, ALU.mult).then_inc(xn_ready, 1)

            def queries2(it, **more):
                body(it * 8 + PB["q2"], PB["q2"], it * 4 + UB["q2"], UB["q2"], it * 4 + ZB["q2"], ZB["q2"], 4, DT,
                     lambda j: normed(it * 4 + j), **more)
            with dve.Fori(0, 3) as it:
                queries2(it)
            queries2(3, short=1)
            attention("swa")
            split_lo(PB["wo2"] + 4, (PB["wo2"] + 4) % SLOTS)

            def out2(it, **more):
                body(it * 8 + PB["wo2"], PB["wo2"], it * 4 + UB["wo2"], UB["wo2"], it * 4 + ZB["wo2"], ZB["wo2"], 4, DT,
                     dst=lambda j: tile(y, it * 4 + j), **more)
            with dve.Fori(0, 3) as it:
                out2(it)
            out2(3, short=1)
            norm(rs[:, :], 6).then_inc(rs_ready, 1)
            dve.wait_ge(rs_ready, 7)
            dve.wait_ge(xn_ready, DT)
            lo4 = norm_lo(A, "g2", post_hi, a4_ready)
            for t in range(DT + 5):
                if t < DT:
                    V.scalar_tensor_tensor(tA[:, t % 4, :], y[:, t, :], gain("g1", t), rs[:, :], ALU.mult,
                                           ALU.mult).then_inc(post_t, 1)
                if 3 <= t < DT + 3:
                    lo4(t - 3, t - 3)
                if t - 3 in POST_SPLITS:
                    i = 4 + POST_SPLITS.index(t - 3)
                    split_lo(PB["up0"] + i, (PB["up0"] + i) % SLOTS)

            def conv(i, slot):
                dve.wait_ge(up_c0, i + 1)
                w = [par[:, ds(i * 3 + (PO["conv"][0] + k), 1)] for k in range(3)]
                V.scalar_tensor_tensor(tA[:, slot, :], ub[:, slot, 1:S + 1], w[1], c0[:, slot % 2, :], ALU.mult,
                                       ALU.add).then_inc(up_step, 1)
                dve.wait_ge(up_step, i + 1)
                V.scalar_tensor_tensor(tB[:, slot, :], ub[:, slot, 2:S + 2], w[2], tA[:, slot, :], ALU.mult,
                                       ALU.add).then_inc(up_conv, 1)

            t0 = 0
            for c, n in enumerate(CHUNKS2):
                up, dn = f"up{c}", f"dn{c}"

                def hidden2(it, **more):
                    body(it * 8 + PB[up], PB[up], it * 4 + UB[up], UB[up], it * 4 + ZB[up], ZB[up], more.pop("n", 4), DT,
                         lambda j: conv(it * 4 + (2 * t0 + j), j % 4), **more)
                def sum_half():
                    dve.wait_ge(post_sq, DT // 2 + 1)
                    V.tensor_copy(acc2, y[:, DT // 2, :]).then_inc(acc2_step, 1)
                    for t in range(DT // 2 + 1, DT):
                        dve.wait_ge(post_sq, t + 1)
                        dve.wait_ge(acc2_step, t + DT // 2 + 1)
                        V.tensor_tensor(acc2, acc2, y[:, t, :], ALU.add).then_inc(acc2_step, 1)
                if c == 0:
                    hidden2(0, n=8, skip=len(POST_SPLITS) + 4 - AHEAD, hold=4,
                            between={5: sum_half, NORM_AT["up0"]: lambda: norm(rs[:, :], 7).then_inc(rs_ready, 1)})
                with dve.Fori(2 if c == 0 else 0, n // 2) as it:
                    hidden2(it)
                if n == CH:
                    with dve.Fori(0, 4) as it:
                        body(it * 8 + PB[dn], PB[dn], it * 4 + UB[dn], UB[dn], it * 4 + ZB[dn], ZB[dn], 4, n,
                             dst=(lambda j: tile(y, it * 4 + j)) if c == 0 else None)
                else:
                    for it in range(2):
                        body(it * n + PB[dn], PB[dn], it * 8 + UB[dn], UB[dn], it * 8 + ZB[dn], ZB[dn], 8, n,
                             dst=lambda j: y[:, it * 8 + j, :], add=True, short=AHEAD * it)
                t0 += n
            norm(rs[:, :], 8).then_inc(rs_ready, 1)
            dve.wait_ge(rs_ready, 9)
            for t in range(DT):
                V.scalar_tensor_tensor(y[:, t, :], y[:, t, :], gain("g3", t), rs[:, :], ALU.mult, ALU.mult).then_inc(fin_t, 1)
                if t in FIN_DVE:
                    dve.wait_ge(fin_t, t + 1)
                    V.tensor_tensor(x[:, t, :], x[:, t, :], y[:, t, :], ALU.add).then_inc(fin_y, 1)

        @block.scalar
        def _(act):
            C = nc.scalar

            def warm(function):
                C.activation(scratch[:, :], ones[:, 0:1], function)

            def split_hi(i, s, lap):
                act.wait_ge(raw_landed[s], lap)
                act.wait_ge(piece_used, i + 1)
                C.copy(whi[:, s, :], raw[:, s, :]).then_inc(hi_ready, 1)

            def split(p, p0, i, per, it):
                q = p0 + i
                split_hi(p + i, q % SLOTS, (it * (per // SLOTS) + (q // SLOTS + 1)) * 16)

            def body(p, p0, it, n, K, each=None, late=None, skip=0, short=0, between={}, hold=0):
                at = ends(n, K)
                count = n * K // BLK
                for q in range(LEAD, count + AHEAD):
                    if AHEAD + skip <= q < count + AHEAD - short:
                        split(p, p0, q, count, it)
                    if q - LEAD - 1 in between:
                        between[q - LEAD - 1]()
                    for step, lag in ((late, 2), (each, 1)):
                        if step:
                            for j in at.get(q - LEAD - lag - hold, []):
                                if hold == 0 or j < 4:
                                    step(j)
                            for j in at.get(q - LEAD - lag, []):
                                if hold and j >= 4:
                                    step(j)

            def norm_hi(name, src_sem, src0, hi_sem, sq_sem):
                def each(t, i, j):
                    act.wait_ge(src_sem, i + src0 + 1)
                    C.activation(part(A, t, 0), tile(x, t), ACT.Copy, scale=gain(name, t)).then_inc(hi_sem, 1)
                    C.activation(sq[:, j, :], tile(x, t), ACT.Square).then_inc(sq_sem, 1)
                return each

            def load_bias(m):
                rows = bias_rows.ap()[4 * m:4 * m + 4, P - 1:P - 1 + P * (RB - 1)]
                act.dma_start(bias[:, m % 3, :, :],
                              rows.rearrange("e (q i) -> q e i", q=P)[:, :, 0:2 * P]).then_inc(bias_in[m % 3], 16)

            def attention(kind, begin=True, rest=True):
                sm = att[kind]
                nsa = kind == "nsa"

                def exponentials(n):
                    g, t, e0, e1, probs = att_block(n)
                    c = slice(8 * t + e0, 8 * t + e1)
                    act.wait_ge(sm["shift"], n + 1)
                    if not nsa and t == 1 and 2 * g + e0 // 4 + 3 < 2 * KVG:
                        load_bias(2 * g + e0 // 4 + 3)
                    for e in range(e0, e1):
                        i = 8 * t + e
                        last = C.activation(probs[:, e - e0, :], probs[:, e - e0, :], ACT.Exp, bias=nmx[:, i:i + 1],
                                            accum_out=sums[:, i:i + 1])
                    last.then_inc(sm["exp"], 1)
                    if not nsa:
                        act.wait_ge(sm["sinkdiff"], n + 1)
                        C.activation(esk[:, c], esk[:, c], ACT.Exp).then_inc(sm["sinkexp"], 1)

                def output_hi(n):
                    g, t, _, _, _ = att_block(n)
                    act.wait_ge(sm["o_done"], 2 * g + t + 1)
                    for rows, bank in o_parts(nsa, t):
                        last = C.copy(H[rows, HPG * g:HPG * g + HPG, 0, t * P:t * P + P],
                                      bank[rows, :].rearrange("p (r q) -> p r q", r=HPG))
                    last.then_inc(sm["o_hi"], 1)

                if begin:
                    warm(ACT.Exp)
                    exponentials(0)
                if not rest:
                    return
                exponentials(1)
                exponentials(2)
                for n in range(NBLOCK):
                    act.wait_ge(sm["turned"], 2 * n + 1)
                    C.copy(turned_to(n, 0), psum[6][:, :].rearrange("p (e q) -> p e q", e=4)).then_inc(sm["pt_act"], 1)
                    if n % 3 != 2 and n > 0:
                        output_hi(n - 1)
                    if 0 < n < NBLOCK - 2:
                        exponentials(n + 2)
                output_hi(NBLOCK - 1)

            def root(n, dst, var=acc[:, :]):
                act.wait_ge(var_ready, n)
                C.activation(dst, var, ACT.Sqrt).then_inc(root_ready, 1)

            act.dma_start(bflat[0:NBUCK, 0:NSETUP], setup).then_inc(in_s, 16)
            act.wait_ge(ones_set, 1)
            warm(ACT.Square)
            act.wait_ge(in_c, 16)
            for t in range(DT + FIRST_LAG):
                if t < DT:
                    if t % 4 == 0:
                        act.wait_ge(in_x[t // 4], 16)
                    C.activation(A[:, t, 0, :], x[:, t, :], ACT.Copy, scale=gain("g_mix", t)).then_inc(x0_hi, 1)
                if t >= FIRST_LAG:
                    C.activation(y[:, t - FIRST_LAG, :], x[:, t - FIRST_LAG, :], ACT.Square).then_inc(x0_sq, 1)
                if t in FIRST_SPLITS:
                    split(0, 0, FIRST_SPLITS.index(t), 0, 0)

            def project(st, it, **more):
                body(it * 8 + PB[st], PB[st], it, 4, DT, **more)
            project("kv", 0, skip=len(FIRST_SPLITS) - AHEAD, between={NORM_AT["kv"]: lambda: root(1, rs[:, :])})

            def write_rows(i):
                heads = slice(8 * i, 8 * i + 8)
                act.dma_start(bias_rows.ap()[heads].rearrange("h (q i) -> h q i", q=P),
                              bflat[heads, 1024:1024 + RB].unsqueeze(1).to_broadcast([8, P, RB])).then_inc(rows_out, 16)
            act.wait_ge(table_row, 1)
            write_rows(0)
            with act.Fori(1, 4) as it:
                project("kv", it)
            write_rows(1)
            for b in range(2):
                act.wait_ge(blk_step, 8 * b + 8)
                C.copy(blks[:, b, :, 0, :], blkf[:, :, :, :].rearrange("p l g n -> p l (g n)")).then_inc(blk_hi, 1)
                with act.Fori(2 * b, 2 * b + 2) as it:
                    project("q", it)
                write_rows(2 + b)
            for q in range(AHEAD, 15 + AHEAD):
                split(PB["cv"], PB["cv"], q, 0, 0)
            warm(ACT.Sigmoid)
            act.wait_ge(ch_sum, 1)
            for b in range(2):
                last = C.activation(csig[:, b * 64:b * 64 + NB], psum[6][:, b * 64:b * 64 + NB], ACT.Sigmoid)
            last.then_inc(csig_ready, 1)
            act.wait_ge(ch_ready, 1)
            act.wait_ge(pad_zero, 1)
            for b in range(2):
                C.copy(pA[:, b, 0, 0:P].rearrange("p (g n) -> p g n", g=KVG)[:, :, 0:NCMP],
                       ch[:, b * 64:b * 64 + NB].rearrange("p (g n) -> p g n", g=KVG)).then_inc(ch_hi, 1)
            split(PB["misc"], PB["misc"], AHEAD - 1, 0, 0)
            split(PB["misc"], PB["misc"], AHEAD, 0, 0)
            for q in range(AHEAD, 7 + AHEAD):
                split(PB["vb"], PB["vb"], q, 0, 0)
                if q == AHEAD:
                    act.wait_ge(gates_turned, 1)
                    C.activation(gts[:, :, :], psum[7][:, 0:QT * 3 * HEADS].rearrange("p (t c) -> p t c", t=QT),
                                 ACT.Sigmoid).then_inc(gates_ready, 1)
                    for t in range(QT):
                        act.wait_ge(c_shift, t + 1)
                        C.activation(cprob[:, t, :, :], cprob[:, t, :, :], ACT.Exp).then_inc(c_exp, 1)
                if q == AHEAD + 4:
                    attention("nsa", rest=False)
            attention("nsa", begin=False)
            act.dma_start(tC[:, 0:2, :], pT).then_inc(in_p, 16)

            h1 = norm_hi("g_ffn", z_used, 4 + ZB["wo"], wo_hi, wo_sq)
            split(PB["wo"], PB["wo"], 4, 0, 0)
            with act.Fori(0, 4) as it:
                body(it * 8 + PB["wo"], PB["wo"], it, 4, DT, lambda j: h1(it * 4 + j, it * 4 + j, j))

            def hidden(c, it, **more):
                ff, _, o = chunk_at(c)

                def relu_squared(j):
                    i = c * 16 + it * 4 + j
                    act.wait_ge(z_used, c * 32 + it * 4 + (4 + ZB["ff0"] + j + 1))
                    C.activation(tA[:, j, :], zr[:, j, :], ACT.Relu).then_inc(ff_relu, 1)
                    act.wait_ge(ff_relu, i + 1)
                    C.activation(part(H, it * 4 + j, 0), tA[:, j, :], ACT.Square).then_inc(ff_hi, 1)
                body(o * 64 + it * 8 + PB[ff], PB[ff], o * 8 + it, 4, DT, relu_squared, **more)

            def chunk(c, first=0, prep=None):
                _, fd, o = chunk_at(c)
                with act.Fori(first, 4) as it:
                    hidden(c, it)
                with act.Fori(0, 4) as it:
                    body(o * 64 + it * 8 + PB[fd], PB[fd], o * 8 + it, 4, CH,
                         (lambda j: prep(it * 4 + j, it * 4 + j, j)) if prep else None)
            hidden(0, 0, between={NORM_AT["ff0"]: lambda: root(2, rs[:, :])})
            act.wait_ge(in_p, 16)
            for k in range(2):
                C.copy(pA[:, k, 0, :], tC[:, k, :]).then_inc(p_hi, 1)
            chunk(0, 1)
            with act.Fori(1, FF_CHUNKS - 1) as c:
                chunk(c)
            body(PB["proj"], PB["proj"], 0, DT, 2)
            last = f"fd{FF_CHUNKS - 1}"
            chunk(FF_CHUNKS - 1, 0, norm_hi("g_ple", z_used, 4 + ZB[last], fd_hi, fd_sq))

            def gate(it, **more):
                def sigmoid(j):
                    act.wait_ge(z_used, it * 4 + (4 + ZB["gate"] + j + 1))
                    C.activation(tA[:, j, :], zr[:, j, :], ACT.Sigmoid).then_inc(ple_sig, 1)

                def next_input(j):
                    t = it * 4 + j
                    act.wait_ge(ple_x, t + 1)
                    C.activation(part(H, t, 0), tile(x, t), ACT.Copy, scale=gg[:, ds(t, 1)]).then_inc(ple_hi, 1)
                    C.activation(sq[:, j, :], tile(x, t), ACT.Square).then_inc(ple_sq, 1)
                    C.activation(sq2[:, j, :], tile(x, t), ACT.Square, scale=gain("g_fin", t)).then_inc(ple_sq, 1)
                body(it * 8 + PB["gate"], PB["gate"], it, 4, DT, sigmoid, next_input, **more)
            act.wait_ge(gg_ready, 1)
            gate(0, between={NORM_AT["gate"]: lambda: root(3, rs[:, :])})
            with act.Fori(1, 4) as it:
                gate(it)

            def roots_k2():
                root(4, rs3)
                root(5, rs[:, :], acc2)
            body(PB["k2"], PB["k2"], 0, 4, DT, between={NORM_AT["k2"]: roots_k2})
            for i in range(8):
                split(PB["v2"], PB["v2"], i + AHEAD, 0, 0)
            act.wait_ge(rows_out, 64)
            act.wait_ge(rs_ready, 6)
            for m in range(3):
                load_bias(m)
            with act.Fori(0, 3) as it:
                body(it * 8 + PB["q2"], PB["q2"], it, 4, DT)
            body(3 * 8 + PB["q2"], PB["q2"], 3, 4, DT, short=1)
            act.wait_ge(z_used, 4 + ZB["wo2"])
            attention("swa")
            split(PB["wo2"], PB["wo2"], 4, 0, 0)

            def square(i, j):
                act.wait_ge(z_ready, i + (4 + UB["wo2"] + 1))
                act.wait_ge(acc_step, i + (ACC0["post"] - 3))
                C.activation(sq[:, j, :], tile(y, i), ACT.Square).then_inc(wo2_sq, 1)

            def out2(it, **more):
                body(it * 8 + PB["wo2"], PB["wo2"], it, 4, DT, lambda j: square(it * 4 + j, j), **more)
            with act.Fori(0, 3) as it:
                out2(it)
            out2(3, short=1)
            root(6, rs[:, :])
            for t in range(DT + 8):
                if t < DT:
                    act.wait_ge(post_x, t + 1)
                    C.activation(A[:, t, 0, :], x[:, t, :], ACT.Copy, scale=gain("g2", t)).then_inc(post_hi, 1)
                if t in POST_SPLITS:
                    split(PB["up0"], PB["up0"], 4 + POST_SPLITS.index(t), 0, 0)
                if t >= 8:
                    C.activation(y[:, t - 8, :], x[:, t - 8, :], ACT.Square).then_inc(post_sq, 1)

            t0 = 0
            for c, n in enumerate(CHUNKS2):
                up, dn = f"up{c}", f"dn{c}"

                def hidden2(it, **more):
                    def tap(j):
                        act.wait_ge(z_used, it * 4 + (4 + ZB[up] + j + 1))
                        C.activation(c0[:, j % 2, :], ub[:, j % 4, 0:S], ACT.Copy,
                                     scale=par[:, ds(it * 12 + (PO["conv"][0] + 3 * (2 * t0 + j)), 1)]).then_inc(up_c0, 1)

                    def tail(j):
                        if j % 2 == 0:
                            act.wait_ge(up_conv, it * 4 + (2 * t0 + j + 1))
                            C.activation(tC[:, j % 4, :], tB[:, j % 4, :], ACT.Sigmoid).then_inc(up_sig, 1)
                        else:
                            act.wait_ge(up_h, it * 2 + (t0 + j // 2 + 1))
                            C.copy(part(H, it * 2 + j // 2, 0), zr[:, j % 4, :]).then_inc(up_hi, 1)
                    body(it * 8 + PB[up], PB[up], it, more.pop("n", 4), DT, tap, tail, **more)
                if c == 0:
                    hidden2(0, n=8, skip=len(POST_SPLITS) + 4 - AHEAD, hold=4,
                            between={NORM_AT["up0"]: lambda: root(7, rs[:, :])})
                with act.Fori(2 if c == 0 else 0, n // 2) as it:
                    hidden2(it)
                if n == CH:
                    with act.Fori(0, 4) as it:
                        body(it * 8 + PB[dn], PB[dn], it, 4, n)
                else:
                    def square3(i):
                        act.wait_ge(z_ready, 4 + UB[dn] + i + 1)
                        act.wait_ge(acc_step, ACC0["end"] + i - 7)
                        C.activation(sq[:, i % 8, :], y[:, i, :], ACT.Square).then_inc(dn_sq, 1)
                    for it in range(2):
                        body(it * n + PB[dn], PB[dn], it, 8, n, lambda j: square3(it * 8 + j), short=AHEAD * it)
                t0 += n
            root(8, rs[:, :])

        @block.gpsimd
        def _(pool):
            G = nc.gpsimd
            pool.sem_inc(z_used, 4)
            G.memset(ones[:, :], 1.0).then_inc(ones_set, 1)

            def add_acc(dst, src, n):
                pool.wait_ge(acc_step, n)
                G.tensor_tensor(dst, dst, src, ALU.add).then_inc(acc_step, 1)

            def take(u, z0, j, fn):
                pool.wait_ge(z_ready, u + (4 + j + 1))
                fn(z[:, (z0 + j) % 4, :]).then_inc(z_used, 1)

            def mul(dst, by):
                return lambda zz: G.tensor_tensor(dst, zz, by, ALU.mult)

            pool.sem_inc(acc_step, 1)
            pool.wait_ge(x0_sq, 2)
            G.tensor_tensor(acc[:, :], y[:, 0, :], y[:, 1, :], ALU.add).then_inc(acc_step, 1)
            for t in range(2, DT):
                pool.wait_ge(x0_sq, t + 1)
                add_acc(acc[:, :], y[:, t, :], t)
            pool.wait_ge(rs_ready, 2)
            for b in range(2):
                with pool.Fori(0, 2) as it:
                    for j in range(4):
                        dst = kvc if b == 0 else kT
                        take(it * 4 + (UB["kv"] + 8 * b), ZB["kv"], j,
                             mul(dst[:, ds(it, 1), j, :].rearrange("p a t -> p (a t)"), rs[:, :]))
            with pool.Fori(0, 4) as it:
                for j in range(4):
                    take(it * 4 + UB["q"], ZB["q"], j, mul(tile(y, it * 4 + j), rs2))
            pool.wait_ge(rows_out, 64)
            G.memset(pA[:, :, :, :].rearrange("p a b c -> p (a b c)").bitcast(F32), 0.0).then_inc(pad_zero, 1)
            G.memset(vczall[:, :, :], 0.0).then_inc(vcz_zero, 1)
            pool.wait_ge(blk_ready, 2)
            G.memset(cpad[:, :, :, :, :].rearrange("p t r g n -> p (t r g n)"), 0.0).then_inc(cpad_zero, 1)
            take(UB["misc"], ZB["misc"], 0, lambda zz: G.tensor_tensor(gT, zz[0:3 * HEADS], rs[0:3 * HEADS, :], ALU.mult))

            def residual(st, c, it, j):
                take(c * 32 + it * 4 + UB[st], ZB[st], j,
                     lambda zz: G.tensor_tensor(tile(x, it * 4 + j), tile(x, it * 4 + j), zz, ALU.add))

            G.memset(acc[:, :], 0.0).then_inc(acc_zero, 1)
            pool.wait_ge(acc_zero, 1)
            with pool.Fori(0, 4) as it:
                for j in range(4):
                    residual("wo", 0, it, j)
                    pool.wait_ge(wo_sq, it * 4 + (j + 1))
                    add_acc(acc[:, :], sq[:, j, :], it * 4 + (ACC0["ff0"] + j))
            pool.wait_ge(rs_ready, 3)

            def chunk(c, prep):
                ff, fd, o = chunk_at(c)
                with pool.Fori(0, 4) as it:
                    for j in range(4):
                        i = c * 16 + it * 4 + j
                        take(o * 32 + it * 4 + UB[ff], ZB["ff0"], j, mul(zr[:, j, :], rs[:, :]))
                        pool.wait_ge(ff_relu, i + 1)
                        G.tensor_tensor(tB[:, j, :], tA[:, j, :], tA[:, j, :], ALU.mult).then_inc(ff_step, 1)
                        pool.wait_ge(ff_step, i + 1)
                        pool.wait_ge(ff_hi, i + 1)
                        G.tensor_tensor(part(H, it * 4 + j, 1), tB[:, j, :], part(H, it * 4 + j, 0).bitcast(F32),
                                        ALU.subtract).then_inc(ff_ready, 1)
                with pool.Fori(0, 4) as it:
                    for j in range(4):
                        residual(fd, o, it, j)
                        if prep:
                            pool.wait_ge(fd_sq, it * 4 + (j + 1))
                            add_acc(acc[:, :], sq[:, j, :], it * 4 + (ACC0["gate"] + j))
            with pool.Fori(0, FF_CHUNKS - 1) as c:
                chunk(c, False)
            G.memset(acc[:, :], 0.0).then_inc(acc_zero, 1)
            pool.wait_ge(acc_zero, 2)
            chunk(FF_CHUNKS - 1, True)
            G.memset(acc2, 0.0).then_inc(acc_zero, 1)
            pool.wait_ge(rs_ready, 4)
            G.memset(acc[:, :], 0.0).then_inc(acc_zero, 1)
            pool.wait_ge(acc_zero, 4)
            with pool.Fori(0, 4) as it:
                for j in range(4):
                    t = it * 4 + j
                    take(it * 4 + UB["gate"], ZB["gate"], j, mul(zr[:, j, :], rs[:, :]))
                    pool.wait_ge(ple_sig, t + 1)
                    G.tensor_tensor(tB[:, j, :], tA[:, j, :], tile(y, t), ALU.mult).then_inc(ple_step, 1)
                    pool.wait_ge(ple_step, t + 1)
                    G.tensor_tensor(tile(x, t), tile(x, t), tB[:, j, :], ALU.add).then_inc(ple_x, 1)
                    for i in ([j - 1] if 0 < j < 3 else [j - 1, j] if j == 3 else []):
                        pool.wait_ge(ple_sq, it * 8 + (2 * i + 1))
                        add_acc(acc[:, :], sq[:, i, :], it * 4 + (ACC0["k2"] + i))
            pool.wait_ge(rs_ready, 6)
            for j in range(4):
                take(UB["k2"], ZB["k2"], j, mul(kT[:, 0, j, :], rs[:, :]))
            with pool.Fori(0, 4) as it:
                for j in range(4):
                    take(it * 4 + UB["q2"], ZB["q2"], j, mul(tile(y, it * 4 + j), rs2))
            G.memset(acc[:, :], 0.0).then_inc(acc_zero, 1)
            pool.wait_ge(acc_zero, 5)
            with pool.Fori(0, 4) as it:
                for j in range(4):
                    pool.wait_ge(wo2_sq, it * 4 + (j + 1))
                    add_acc(acc[:, :], sq[:, j, :], it * 4 + (ACC0["post"] + j))
            with pool.Fori(0, 4) as it:
                for j in range(4):
                    t = it * 4 + j
                    pool.wait_ge(post_t, t + 1)
                    G.tensor_tensor(tile(x, t), tile(x, t), tA[:, j, :], ALU.add).then_inc(post_x, 1)
            G.memset(acc[:, :], 0.0).then_inc(acc_zero, 1)
            pool.wait_ge(acc_zero, 6)
            with pool.Fori(0, 2) as it:
                for j in range(4):
                    pool.wait_ge(post_sq, it * 4 + (j + 1))
                    add_acc(acc[:, :], tile(y, it * 4 + j), it * 4 + (ACC0["up0"] + j))
            G.memset(ub[:, :, 0:2], 0.0).then_inc(acc_zero, 1)
            pool.wait_ge(rs_ready, 8)
            G.memset(acc[:, :], 0.0).then_inc(acc_zero, 1)
            pool.wait_ge(acc_zero, 8)
            t0 = 0
            for c, n in enumerate(CHUNKS2):
                up, dn = f"up{c}", f"dn{c}"
                with pool.Fori(0, n // 2) as it:
                    def preact(j):
                        take(it * 4 + UB[up], ZB[up], j, mul(ub[:, j, 2:S + 2], rs[:, :]))

                    def gated(j):
                        pool.wait_ge(up_sig, it * 2 + (t0 + j // 2 + 1))
                        G.tensor_tensor(tC[:, j, :], tC[:, j, :], tB[:, j, :], ALU.mult).then_inc(up_gated, 1)

                    def product(j):
                        i = it * 2 + (t0 + j // 2)
                        pool.wait_ge(up_conv, i * 2 + 2)
                        pool.wait_ge(up_gated, i + 1)
                        G.tensor_tensor(zr[:, j, :], tC[:, j - 1, :], tB[:, j, :], ALU.mult).then_inc(up_h, 1)

                    def product_lo(j):
                        i = it * 2 + (t0 + j // 2)
                        pool.wait_ge(up_h, i + 1)
                        pool.wait_ge(up_hi, i + 1)
                        G.tensor_tensor(part(H, it * 2 + j // 2, 1), zr[:, j, :], part(H, it * 2 + j // 2, 0).bitcast(F32),
                                        ALU.subtract).then_inc(up_ready, 1)
                    preact(0)
                    preact(1)
                    gated(0)
                    preact(2)
                    product(1)
                    preact(3)
                    product_lo(1)
                    gated(2)
                    product(3)
                    product_lo(3)
                if n == CH and c > 0:
                    with pool.Fori(0, 4) as it:
                        for j in range(4):
                            t = it * 4 + j
                            take(it * 4 + UB[dn], ZB[dn], j, lambda zz: G.tensor_tensor(tile(y, t), tile(y, t), zz, ALU.add))
                elif n < CH:
                    for j in range(DT):
                        pool.wait_ge(dn_sq, j + 1)
                        add_acc(acc[:, :], sq[:, j % 8, :], ACC0["end"] + j)
                t0 += n
            for t in range(DT):
                if t not in FIN_DVE:
                    pool.wait_ge(fin_t, t + 1)
                    G.tensor_tensor(x[:, t, :], x[:, t, :], y[:, t, :], ALU.add).then_inc(fin_x, 1)


def tiled(w):
    k, n = w.shape
    tiles = w.reshape(k // P, P, n // P, P).transpose(2, 0, 1, 3)
    return ordered(tiles)


def ordered(tiles):
    unit, kt = zip(*order(*tiles.shape[:2]))
    return tiles[list(unit), list(kt)]


def kernel(**inp):
    import concourse.bacc as bacc
    from concourse import mybir
    from concourse.bass_utils import run_bass_kernel_spmd

    f = np.float32
    a = {k: np.asarray(v) for k, v in inp.items()}

    w_in = a["nsa_w_in"][0]
    kvw = KVG * P
    cut = [D + i * kvw for i in range(7)]
    kc, vc, ks, vs, kw, vw = (w_in[:, cut[i]:cut[i + 1]] for i in range(6))

    def rows(w):
        k, n = w.shape
        return w.reshape(k // P, P, n // P, P).transpose(0, 2, 1, 3).reshape(-1, P, P)

    compress = [tiled(a["nsa_cmp_w1_k"][0]), tiled(a["nsa_cmp_w1_v"][0])]
    in_turn = np.stack([t.reshape(-1, BLK, P, P) for t in (np.concatenate(compress), rows(vs))], axis=1).reshape(-1, P, P)
    gates = w_in[:, cut[6]:].reshape(DT, P, KVG, HPG, 3).transpose(1, 0, 2, 4, 3).reshape(P, DT * 48)
    misc = np.concatenate([gates, a["nsa_cmp_w2_k"][0], a["nsa_cmp_w2_v"][0]], axis=1)
    stream = [tiled(kc), tiled(vc), tiled(ks), tiled(kw), tiled(w_in[:, :D]),  in_turn,
              misc.reshape(P, BLK, P).transpose(1, 0, 2), rows(vw), tiled(a["nsa_w_out"][0])]
    for c in range(FF_CHUNKS):
        h = slice(c * CH * P, (c + 1) * CH * P)
        if c == FF_CHUNKS - 1:
            stream.append(tiled(a["ple_w_proj"][0]))
        stream += [tiled(a["ffn_w1"][0][:, h]), tiled(a["ffn_w2"][0][h])]
    stream.append(tiled(a["ple_w_gate"][0]))
    swa = a["swa_w_in_2"][0]
    kv2 = SWA_KV * HD
    order = np.arange(SWA_HEADS * HD).reshape(PAIRS, 2, HPG, HD).transpose(0, 2, 1, 3).reshape(-1)
    stream += [tiled(swa[:, D:D + kv2]), rows(swa[:, D + kv2:]), tiled(swa[:, :D][:, order]), tiled(a["swa_w_out_2"][0][order])]
    up, down = a["ffn_w_up_2"][0], a["ffn_w_down_2"][0]
    both = up.reshape(DT, P, 2, FF2_T, P).transpose(3, 2, 0, 1, 4)
    t0 = 0
    for n in CHUNKS2:
        stream += [ordered(both[t0:t0 + n].reshape(2 * n, DT, P, P)), tiled(down[t0 * P:(t0 + n) * P])]
        t0 += n
    wstream = np.concatenate(stream).reshape(NPIECE, BLK, P, P).transpose(0, 2, 1, 3)
    wstream = np.ascontiguousarray(wstream).reshape(NPIECE, P, PW)

    q = np.arange(P)
    causal = np.where(q[None, :] <= q[:, None], 0, NEG)
    tok = np.arange(S).reshape(QT, P, 1)
    n = np.arange(CS)
    valid = (n * CS + CL - 1 <= tok) & (n < NCMP)
    consts = np.concatenate([np.eye(P), np.zeros((P, P)), causal, np.where(valid, 0, NEG).transpose(1, 0, 2).reshape(P, -1),
                             valid.transpose(1, 0, 2).reshape(P, -1), q[:, None] % NB == np.arange(NB)], axis=1).astype(f)
    dist = 2 * P - 1 - np.arange(RB)
    near = np.clip(dist, 1, None)
    exact = NBUCK // 2
    far = np.minimum(exact + (np.log(near / exact) / np.log(MAXD / exact) * (NBUCK - exact)).astype(int), NBUCK - 1)
    bucket = np.where(dist < exact, np.maximum(dist, 0), far)
    onehot = (bucket[None, :] == np.arange(NBUCK)[:, None]).astype(f)
    band = np.broadcast_to(np.where((dist >= 0) & (dist < WIN), 0, NEG), (SWA_HEADS, RB)).astype(f)
    setup = np.concatenate([onehot, band, a["rel_bias_table_2"]], axis=1)

    def col(g):
        return g.reshape(-1, P).T

    conv = a["ffn_conv_2"][0].reshape(3, 2, FF2_T, P).transpose(3, 2, 1, 0).reshape(P, -1)
    g2 = a["norm_g_2"][0]
    params = np.concatenate([col(a["norm_mix"][0]), col(a["norm_ffn"][0]), col(a["norm_ple"][0]), col(a["norm_final"]),
                             col(g2[0]), col(g2[1]), col(g2[2]), col(g2[3]), conv, a["nsa_cmp_pos_k"][0].T,
                             a["nsa_cmp_pos_v"][0].T, np.broadcast_to(a["swa_sinks_2"][0], (P, SWA_HEADS))], axis=1)
    arrays = {
        "xT": a["x"][0].T.reshape(DT, P, S).transpose(1, 0, 2),
        "pT": a["p"][0, 0].T.reshape(2, P, S).transpose(1, 0, 2),
        "wstream": wstream, "consts": consts, "setup": setup, "params": params,
    }
    arrays = {k: np.ascontiguousarray(v) for k, v in arrays.items()}

    nc = bacc.Bacc("TRN2", target_bir_lowering=False, num_devices=1)
    F32 = mybir.dt.float32
    aps = [nc.dram_tensor(k, v.shape, F32, kind="ExternalInput").ap() for k, v in arrays.items()]
    out = nc.dram_tensor("out", (P, DT, S), F32, kind="ExternalOutput").ap()
    program(nc, *aps, out)
    r = run_bass_kernel_spmd(nc, [arrays], core_ids=[0])
    return np.ascontiguousarray(r.results[0]["out"].transpose(2, 1, 0)).reshape(1, S, D)
```
